# Optimizing a Trainium2 kernel written in Bass

```python
import jax, jax.numpy as jnp
from jax import lax
import numpy as np

D_MODEL = 1024
BATCH = 1
SEQ = 256
DEPTH = 2

GRID_W = 64
CTX_LEN = 256
D_MIX = D_MODEL
D_CONV = D_MIX // 2
D_ATTN = D_MIX - D_CONV
HEAD_DIM = 64
N_HEADS = D_ATTN // HEAD_DIM
N_KV = 2
GQA = N_HEADS // N_KV
CONV_WIDTH = 3
WINDOW = 128
BLOCK = 128
ROPE_THETA = 10000.0
D_FF = 2816
N_EXPERTS = 8
TOP_K = 2
D_FF_EXPERT = 1408
N_DENSE = (DEPTH + 1) // 2
N_MOE = DEPTH // 2
EPS = 1e-6
KV_OFF = 3 * D_CONV + D_ATTN
D_IN = KV_OFF + 2 * N_KV * HEAD_DIM
SPLITS = (D_CONV, 2 * D_CONV, 3 * D_CONV, KV_OFF, KV_OFF + N_KV * HEAD_DIM)

kernel_name = "hybrid_conv_swa_moe_dit_block"

def rmsnorm(x, g):
    xf = x.astype(jnp.float32)
    y = xf * lax.rsqrt(jnp.mean(xf * xf, axis=-1, keepdims=True) + EPS)
    return (y * g.astype(jnp.float32)).astype(x.dtype)

def modulate(x, shift, scale):
    return x * (1 + scale) + shift

def axial_rope_tables(rows):
    row, col = jnp.meshgrid(jnp.arange(rows, dtype=jnp.float32),
                            jnp.arange(GRID_W, dtype=jnp.float32), indexing='ij')
    n_freq = HEAD_DIM // 4
    inv_freq = ROPE_THETA ** (-jnp.arange(n_freq, dtype=jnp.float32) / n_freq)
    ang_r = row.reshape(-1, 1) * inv_freq
    ang_c = col.reshape(-1, 1) * inv_freq
    ang = jnp.concatenate([ang_r, ang_r, ang_c, ang_c], axis=-1)
    return jnp.cos(ang)[None, :, None, :], jnp.sin(ang)[None, :, None, :]

def apply_axial_rope(t, cos, sin):
    tf = t.astype(jnp.float32)
    tr = tf.reshape(t.shape[:-1] + (2, 2, HEAD_DIM // 4))
    rot = jnp.stack([-tr[..., 1, :], tr[..., 0, :]], axis=-2).reshape(t.shape)
    return (tf * cos + rot * sin).astype(t.dtype)

def split_heads_kv(zkv, k_g):
    B, L = zkv.shape[:2]
    k, v = jnp.split(zkv, 2, axis=-1)
    k = rmsnorm(k.reshape(B, L, N_KV, HEAD_DIM), k_g)
    return k, v.reshape(B, L, N_KV, HEAD_DIM)

def mixer_inputs(xn, w_in, q_g, k_g):
    B, L = xn.shape[:2]
    bg, cg, hu, q, k, v = jnp.split(xn @ w_in, SPLITS, axis=-1)
    q = rmsnorm(q.reshape(B, L, N_HEADS, HEAD_DIM), q_g)
    k = rmsnorm(k.reshape(B, L, N_KV, HEAD_DIM), k_g)
    return bg, cg, hu, q, k, v.reshape(B, L, N_KV, HEAD_DIM)

def short_gated_conv(bg, cg, hu, conv_w):
    u = cg * hu
    y = lax.conv_general_dilated(u, conv_w[:, None, :].astype(u.dtype), window_strides=(1,),
                                 padding='SAME', dimension_numbers=('NWC', 'WIO', 'NWC'),
                                 feature_group_count=u.shape[-1])
    return bg * y

def window_attention(q, k, v, kc, vc, sink):
    B, S = q.shape[:2]
    nb = S // BLOCK
    scale = HEAD_DIM ** -0.5
    f32 = jnp.float32
    qb = q.astype(f32).reshape(B, nb, BLOCK, N_KV, GQA, HEAD_DIM)
    pad = ((0, 0), (BLOCK, BLOCK), (0, 0), (0, 0))
    kp = jnp.pad(k.astype(f32), pad)
    vp = jnp.pad(v.astype(f32), pad)

    def bands(t):
        return jnp.concatenate(
            [t[:, o:o + S].reshape(B, nb, BLOCK, N_KV, HEAD_DIM) for o in (0, BLOCK, 2 * BLOCK)], axis=2)

    kb, vb = bands(kp), bands(vp)
    kcf, vcf = kc.astype(f32), vc.astype(f32)
    s_win = jnp.einsum('bnqgrd,bnkgd->bngrqk', qb, kb) * scale
    qi = jnp.arange(BLOCK)[:, None]
    kj = jnp.arange(3 * BLOCK)[None, :]
    key_pos = jnp.arange(nb)[:, None, None] * BLOCK + kj[None] - BLOCK
    valid = (jnp.abs(kj - BLOCK - qi) <= WINDOW)[None] & (key_pos >= 0) & (key_pos < S)
    s_win = jnp.where(valid[None, :, None, None], s_win, -jnp.inf)
    s_ctx = jnp.einsum('bnqgrd,blgd->bngrql', qb, kcf) * scale
    sk = sink.astype(f32).reshape(1, 1, N_KV, GQA, 1, 1)
    m = jnp.maximum(jnp.maximum(s_win.max(-1, keepdims=True), s_ctx.max(-1, keepdims=True)), sk)
    p_win = jnp.exp(s_win - m)
    p_ctx = jnp.exp(s_ctx - m)
    denom = jnp.exp(sk - m) + p_win.sum(-1, keepdims=True) + p_ctx.sum(-1, keepdims=True)
    o = (jnp.einsum('bngrqk,bnkgd->bnqgrd', p_win, vb)
         + jnp.einsum('bngrql,blgd->bnqgrd', p_ctx, vcf))
    o = o / jnp.moveaxis(denom, 4, 2)
    return o.reshape(B, S, D_ATTN).astype(q.dtype)

def context_attention(qc, kc, vc, sink):
    B, L = qc.shape[:2]
    f32 = jnp.float32
    q = qc.astype(f32).reshape(B, L, N_KV, GQA, HEAD_DIM)
    s = jnp.einsum('blgrd,bmgd->bgrlm', q, kc.astype(f32)) * (HEAD_DIM ** -0.5)
    sk = jnp.broadcast_to(sink.astype(f32).reshape(1, N_KV, GQA, 1, 1), s.shape[:-1] + (1,))
    p = jax.nn.softmax(jnp.concatenate([sk, s], axis=-1), axis=-1)[..., 1:]
    o = jnp.einsum('bgrlm,bmgd->blgrd', p, vc.astype(f32))
    return o.reshape(B, L, D_ATTN).astype(qc.dtype)

def merge_groups(y_conv, y_attn, g_conv, g_attn, w_out):
    return jnp.concatenate([rmsnorm(y_conv, g_conv), rmsnorm(y_attn, g_attn)], axis=-1) @ w_out

def swiglu(x, w1, w3, w2):
    return (jax.nn.silu(x @ w1) * (x @ w3)) @ w2

def moe_swiglu(x, router, w1, w3, w2):
    logits = (x @ router).astype(jnp.float32)
    top_v, top_i = lax.top_k(logits, TOP_K)
    gates = jax.nn.softmax(top_v, axis=-1)
    combine = jnp.sum(jax.nn.one_hot(top_i, N_EXPERTS, dtype=jnp.float32) * gates[..., None], axis=-2)
    combine = combine.astype(x.dtype)
    out = jnp.zeros_like(x)
    for e in range(N_EXPERTS):
        out = out + combine[..., e:e + 1] * swiglu(x, w1[e], w3[e], w2[e])
    return out

def channel_mixer(layer, xn, ffn_w1, ffn_w3, ffn_w2, moe_router, moe_w1, moe_w3, moe_w2):
    i = layer // 2
    if layer % 2 == 0:
        return swiglu(xn, ffn_w1[i], ffn_w3[i], ffn_w2[i])
    return moe_swiglu(xn, moe_router[i], moe_w1[i], moe_w3[i], moe_w2[i])

def setup_inputs(seed: int = 0) -> dict:
    key = jax.random.key(seed)
    ks = jax.random.split(key, 24)
    n = jax.random.normal
    f32 = jnp.float32
    D = D_MODEL
    return {
        "x": n(ks[0], (BATCH, SEQ, D), f32),
        "c": n(ks[1], (BATCH, D), f32),
        "ctx": n(ks[2], (BATCH, CTX_LEN, D), f32),
        "c_ctx": n(ks[3], (D,), f32),
        "w_ada": n(ks[4], (DEPTH, D, 6 * D), f32) * (0.5 * D ** -0.5),
        "b_ada": n(ks[5], (DEPTH, 6 * D), f32) * 0.01,
        "norm1_g": 1.0 + 0.02 * n(ks[6], (DEPTH, D), f32),
        "norm2_g": 1.0 + 0.02 * n(ks[7], (DEPTH, D), f32),
        "w_in": n(ks[8], (DEPTH, D, D_IN), f32) * D ** -0.5,
        "conv_w": n(ks[9], (DEPTH, CONV_WIDTH, D_CONV), f32) * CONV_WIDTH ** -0.5,
        "q_norm_g": 1.0 + 0.02 * n(ks[10], (DEPTH, HEAD_DIM), f32),
        "k_norm_g": 1.0 + 0.02 * n(ks[11], (DEPTH, HEAD_DIM), f32),
        "attn_sink": 0.5 * n(ks[12], (DEPTH, N_HEADS), f32),
        "out_norm_conv_g": 1.0 + 0.02 * n(ks[13], (DEPTH, D_CONV), f32),
        "out_norm_attn_g": 1.0 + 0.02 * n(ks[14], (DEPTH, D_ATTN), f32),
        "w_out": n(ks[15], (DEPTH, D_MIX, D), f32) * D_MIX ** -0.5,
        "ffn_w1": n(ks[16], (N_DENSE, D, D_FF), f32) * D ** -0.5,
        "ffn_w3": n(ks[17], (N_DENSE, D, D_FF), f32) * D ** -0.5,
        "ffn_w2": n(ks[18], (N_DENSE, D_FF, D), f32) * D_FF ** -0.5,
        "moe_router": n(ks[19], (N_MOE, D, N_EXPERTS), f32) * D ** -0.5,
        "moe_w1": n(ks[20], (N_MOE, N_EXPERTS, D, D_FF_EXPERT), f32) * D ** -0.5,
        "moe_w3": n(ks[21], (N_MOE, N_EXPERTS, D, D_FF_EXPERT), f32) * D ** -0.5,
        "moe_w2": n(ks[22], (N_MOE, N_EXPERTS, D_FF_EXPERT, D), f32) * D_FF_EXPERT ** -0.5,
    }

def reference(x, c, ctx, c_ctx, w_ada, b_ada, norm1_g, norm2_g, w_in, conv_w, q_norm_g, k_norm_g,
              attn_sink, out_norm_conv_g, out_norm_attn_g, w_out, ffn_w1, ffn_w3, ffn_w2,
              moe_router, moe_w1, moe_w3, moe_w2):
    B, S, D = x.shape
    ROWS = S // GRID_W
    cos, sin = axial_rope_tables(ROWS)
    sc = jax.nn.silu(c)[:, None, :]
    scc = jax.nn.silu(c_ctx)[None, None, :]
    h, hc = x, ctx
    for layer in range(DEPTH):
        last = layer == DEPTH - 1
        sh1, sc1, g1, sh2, sc2, g2 = jnp.split(sc @ w_ada[layer] + b_ada[layer], 6, axis=-1)
        n_mod_c = 2 if last else 6
        mod_c = jnp.split(scc @ w_ada[layer][:, :n_mod_c * D] + b_ada[layer][:n_mod_c * D], n_mod_c, axis=-1)

        xn = modulate(rmsnorm(h, norm1_g[layer]), sh1, sc1)
        xnc = modulate(rmsnorm(hc, norm1_g[layer]), mod_c[0], mod_c[1])
        bg, cg, hu, q, k, v = mixer_inputs(xn, w_in[layer], q_norm_g[layer], k_norm_g[layer])
        q = apply_axial_rope(q, cos, sin)
        k = apply_axial_rope(k, cos, sin)
        if last:
            kc, vc = split_heads_kv(xnc @ w_in[layer][:, KV_OFF:], k_norm_g[layer])
        else:
            bgc, cgc, huc, qc, kc, vc = mixer_inputs(xnc, w_in[layer], q_norm_g[layer], k_norm_g[layer])
        y_conv = short_gated_conv(bg, cg, hu, conv_w[layer])
        y_attn = window_attention(q, k, v, kc, vc, attn_sink[layer])
        y = merge_groups(y_conv, y_attn, out_norm_conv_g[layer], out_norm_attn_g[layer], w_out[layer])
        h = h + g1 * y
        if not last:
            yc_conv = short_gated_conv(bgc, cgc, huc, conv_w[layer])
            yc_attn = context_attention(qc, kc, vc, attn_sink[layer])
            yc = merge_groups(yc_conv, yc_attn, out_norm_conv_g[layer], out_norm_attn_g[layer], w_out[layer])
            hc = hc + mod_c[2] * yc

        xn2 = modulate(rmsnorm(h, norm2_g[layer]), sh2, sc2)
        h = h + g2 * channel_mixer(layer, xn2, ffn_w1, ffn_w3, ffn_w2, moe_router, moe_w1, moe_w3, moe_w2)
        if not last:
            xnc2 = modulate(rmsnorm(hc, norm2_g[layer]), mod_c[3], mod_c[4])
            hc = hc + mod_c[5] * channel_mixer(layer, xnc2, ffn_w1, ffn_w3, ffn_w2,
                                               moe_router, moe_w1, moe_w3, moe_w2)
    return h


_drawn_inputs = setup_inputs


def setup_inputs(seed=0):
    import zlib

    import numpy as np

    out = dict(_drawn_inputs(seed))
    spreads = {}
    factors = {'norm1_g': 3.929,
     'norm2_g': 3.555,
     'q_norm_g': 8.0,
     'k_norm_g': 8.0,
     'attn_sink': 8.0,
     'out_norm_conv_g': 5.644,
     'out_norm_attn_g': 4.781}
    for name, (base, spread) in spreads.items():
        noise = np.random.default_rng([zlib.crc32(name.encode()), seed]).standard_normal(out[name].shape)
        drawn = base * np.exp(spread * noise) if base else spread * noise
        out[name] = __import__('jax').numpy.asarray(drawn.astype(out[name].dtype))
    for name, factor in factors.items():
        out[name] = (out[name] * factor).astype(out[name].dtype)
    return out
```

```python
import math
from contextlib import ExitStack

import concourse.bass as bass
from concourse import mybir

F32 = mybir.dt.float32
F32R = mybir.dt.float32r
BF16 = mybir.dt.bfloat16
U32 = mybir.dt.uint32
I32 = mybir.dt.int32
ALU = mybir.AluOpType
ACT = mybir.ActivationFunctionType
AX = mybir.AxisListType

P = 128
D = 1024
KT = D // P
SEQ, CTX = 256, 256
TOK = SEQ + CTX
NBLK = TOK // P
DEPTH = 2
D_CONV = D // 2
CT = D_CONV // P
HEADS, N_KV, HD = 8, 2, 64
D_IN = 3 * D_CONV + 512 + 2 * N_KV * HD
ZT = D_IN // P
D_FF = 2816
EXPERTS, F_EXP = 8, 1408
EPS = 1e-6
SCALE = HD ** -0.5
CW = 256
SLOT = KT * CW
IN_CH, OUT_CH = D_IN // CW, D // CW
FF_CH = D_FF // CW
PART = (FF_CH + 1) // 2
FT = F_EXP // P
MC = F_EXP // 8
MSLOT = 2 * MC * KT
MCH = 8 + D // CW
assert MSLOT == FT * CW
GROUPS = 6
SH1, SC1, G1, SH2, SC2, G2 = range(GROUPS)

V_N1, V_N2 = 0, DEPTH * KT
V_GC = V_N2 + DEPTH * KT
V_GA = V_GC + DEPTH * CT
V_CW = V_GA + DEPTH * CT
V_C = V_CW + DEPTH * 3 * CT
V_CC = V_C + KT
V_QG = V_CC + KT
V_KG = V_QG + DEPTH
V_ROWS = V_KG + DEPTH

C_COS, C_SIN = 0, SEQ
C_ROT = 2 * SEQ
C_DUP = C_ROT + P
C_BONES = C_DUP + 4 * P
C_ID = C_BONES + P
C_ONES = C_ID + P
C_TRI = C_ONES + P
C_MASK = C_TRI + P
C_IOTA = C_MASK + 2 * P
C_ALL = C_IOTA + P


def constant_table(np):
    n_freq = HD // 4
    inv = (np.float32(10000.0) ** (-np.arange(n_freq, dtype=np.float32) / np.float32(n_freq))).astype(np.float32)
    tok = np.arange(SEQ)
    row, col = (tok // 64).astype(np.float32), (tok % 64).astype(np.float32)
    ar, ac = row[:, None] * inv, col[:, None] * inv
    ang = np.concatenate([ar, ar, ac, ac], axis=-1).astype(np.float32).T
    t = np.zeros((P, C_ALL), np.float32)
    t[:, C_COS:C_COS + SEQ] = np.tile(np.cos(ang), (2, 1))
    t[:, C_SIN:C_SIN + SEQ] = np.tile(np.sin(ang), (2, 1))
    for p in range(P):
        if p % 32 < 16:
            t[p + 16, C_ROT + p] = -1.0
        else:
            t[p - 16, C_ROT + p] = 1.0
        for g in range(2):
            t[HD * g + p % HD, C_DUP + (2 * g + p // HD) * P + p] = 1.0
        t[HD * (p // HD):HD * (p // HD + 1), C_BONES + p] = 1.0
        t[p, C_ID + p] = 1.0
        t[p, C_TRI + p + 1:C_TRI + P] = 1.0
    t[:, C_ONES:C_ONES + P] = 1.0
    q, k = np.arange(P)[:, None], np.arange(P)[None, :]
    t[:, C_MASK:C_MASK + P] = np.where(k <= q, 0.0, -1e30)
    t[:, C_MASK + P:C_MASK + 2 * P] = np.where(k >= q, 0.0, -1e30)
    t[:, C_IOTA:C_IOTA + P] = np.arange(P, dtype=np.float32)
    return t


def stages():
    out, n = [], 0
    for layer in range(DEPTH):
        plan = [("in", IN_CH), ("out", OUT_CH)]
        if layer == 0:
            plan += [("up0", 2 * PART), ("down0", PART), ("up1", 2 * (FF_CH - PART)), ("down1", FF_CH - PART)]
        for name, count in plan:
            out.append((layer, name, n, count))
            n += count
    return out, n


def hybrid_backbone(nc, x, c, ctx, c_ctx, w_ada, b_ada, norm1_g, norm2_g, w_in, conv_w, q_norm_g, k_norm_g,
                    attn_sink, out_norm_conv_g, out_norm_attn_g, w_out, ffn_w1, ffn_w3, ffn_w2,
                    moe_router, moe_w1, moe_w3, moe_w2, table, out):
    STAGES, CHUNKS = stages()
    first_chunk = {(layer, name): n for layer, name, n, _ in STAGES}

    with ExitStack() as stack:
        sems = {}

        def sem(name):
            if name not in sems:
                sems[name] = stack.enter_context(nc.semaphore(name))
            return sems[name]

        base = -(-nc.sbuf_base // 64) * 64

        def at(name, offset, shape, dt=F32):
            size = -(-math.prod(shape[1:]) * (2 if dt == BF16 else 4) // 64) * 64
            assert base + offset + size <= nc.sbuf_usable_end, (name, offset + size)
            return nc.alloc_sbuf_tensor_at(name, shape, dt, offset=base + offset), offset + size

        const, o = at("const", 0, [P, C_ALL])
        ident_b, o = at("ident_b", o, [P, P], BF16)
        mask_b, o = at("mask_b", o, [P, 2, P], BF16)
        vec, o = at("vec", o, [P, V_ROWS])
        b_ada_t, o = at("b_ada_t", o, [P, DEPTH * GROUPS * KT])
        cs, o = at("cs", o, [P, 2, KT])
        mod, o = at("mod", o, [P, DEPTH, 2, GROUPS * KT])
        gain, o = at("gain", o, [P, DEPTH, 2, 2, KT])
        nsink, o = at("nsink", o, [P, DEPTH * HEADS])
        router, o = at("router", o, [P, KT, EXPERTS])
        route, o = at("route", o, [P, 12, 2, EXPERTS])
        top_i, o = at("top_i", o, [P, 2, EXPERTS], U32)
        most, o = at("most", o, [P, 1], I32)
        h, o = at("h", o, [P, KT, TOK])
        ZONE = o
        xh, o = at("xh", o, [P, KT, TOK], F32R)
        xl, o = at("xl", o, [P, KT, TOK], F32R)
        Z = o
        z, o = at("z", Z, [P, ZT, TOK])
        VAR = o
        var, o = at("var", o, [P, 2, TOK])
        std, o = at("std", o, [P, 2, TOK])
        rstd, o = at("rstd", o, [P, 2, TOK])
        xin, _ = at("xin", Z, [P, NBLK, D])
        hid_h, o2 = at("hid_h", Z, [P, 2 * PART, TOK], F32R)
        hid_l, o2 = at("hid_l", o2, [P, 2 * PART, TOK], F32R)
        RAW = max(o, o2)
        raw, o = at("raw", RAW, [P, 2, SLOT])
        rows_a, o2 = at("rows_a", o, [P, P])
        rows_b, o2 = at("rows_b", o2, [P, P])
        sink_row, o2 = at("sink_row", o2, [P, DEPTH * HEADS])
        wh, o = at("wh", o, [P, 2, SLOT], F32R)
        wl, o = at("wl", o, [P, 2, SLOT], F32R)
        ada, o = at("ada", o, [P, 2, D])
        TMP = o
        tmp, o = at("tmp", o, [P, 2, TOK])
        tn, o = at("tn", o, [P, 2, SEQ])
        A = o
        acc, _ = at("acc", A, [P, 8, D])
        kd, o = at("kd", A, [P, 2, 2, TOK])
        vtok, o = at("vtok", o, [P, NBLK, P])
        pm, o = at("pm", o, [P, 2, TOK])
        pt, o = at("pt", o, [P, 2, TOK])
        otok, o = at("otok", o, [P, NBLK, D_CONV])
        NU = NBLK * HEADS
        mx, o = at("mx", o, [P, NU])
        negm, o = at("negm", o, [P, NU])
        rsum, o = at("rsum", o, [P, NU])
        esink, o = at("esink", o, [P, NU])
        rden, o = at("rden", o, [P, NU])
        osq, o = at("osq", o, [P, 3, NBLK])
        mwh, o = at("mwh", A, [P, 3, MSLOT], F32R)
        g2b, o = at("g2b", o, [P, D])
        mwl, o = at("mwl", ZONE, [P, 3, MSLOT], F32R)
        assert o <= Z + 2048
        mraw, o = at("mraw", Z + 2048, [P, 3, MSLOT])
        assert o <= VAR
        ye_h, o = at("ye_h", VAR, [P, D], F32R)
        ye_l, o = at("ye_l", o, [P, D], F32R)
        pick, o = at("pick", o, [P, 2, P])
        pick_r, o = at("pick_r", o, [P, 2, P], F32R)
        place, o = at("place", o, [P, SEQ], F32R)
        assert o <= RAW
        x2t_h, o = at("x2t_h", RAW, [P, 2, D], F32R)
        x2t_l, o = at("x2t_l", o, [P, 2, D], F32R)
        xg_h, o = at("xg_h", o, [P, KT, P], F32R)
        xg_l, o = at("xg_l", o, [P, KT, P], F32R)
        x2, _ = at("x2", o, [P, KT, SEQ])
        ht_h, _ = at("ht_h", o, [P, FT * P], F32R)
        htok, o = at("htok", o + KT * SEQ * 4, [P, 2, D])
        ytok, o = at("ytok", o, [P, 2, D])
        ht_l, o = at("ht_l", o, [P, FT * P], F32R)
        sg, o = at("sg", o, [P, 2, MC])
        assert o <= TMP
        hg, o = at("hg", TMP, [P, F_EXP])
        assert o <= A

        ps = stack.enter_context(nc.psum_tensor("ps", [P, 8, 512], F32))

        cos, sin = const[:, C_COS:C_COS + SEQ], const[:, C_SIN:C_SIN + SEQ]
        ident, ones = const[:, C_ID:C_ID + P], const[:, C_ONES:C_ONES + P]
        rot, bones = const[:, C_ROT:C_ROT + P], const[:, C_BONES:C_BONES + P]

        def width(layer):
            return TOK if layer == 0 else SEQ

        def modc(layer, stream, group, k):
            return mod[:, layer, stream, group * KT + k:group * KT + k + 1]

        def vcol(v):
            return vec[:, v:v + 1]

        def span(stream):
            return slice(stream * SEQ, (stream + 1) * SEQ)

        def arrived(eng, n0, i=0):
            eng.wait_ge(sem(f"raw_in{n0 % 2}"), 16 * (n0 // 2 + 1) + 16 * i)

        def split_hi(act, n0, i=0):
            s = n0 % 2
            arrived(act, n0, i)
            if n0 >= 2:
                act.wait_ge(sem("gemm_done"), n0 - 1 + 2 * i)
            act.activation(wh[:, s, :], raw[:, s, :], ACT.Copy).then_inc(sem("hi_done"), 1)

        def split_lo(dve, n0, i=0):
            s = n0 % 2
            arrived(dve, n0, i)
            dve.wait_ge(sem("hi_done"), n0 + 1 + 2 * i)
            dve.tensor_tensor(wl[:, s, :], raw[:, s, :], wh[:, s, :], ALU.subtract).then_inc(sem("lo_done"), 1)

        def load(sp, src, n0, i=0, cols=None):
            s = n0 % 2
            if n0 >= 2:
                sp.wait_ge(sem("lo_done"), n0 - 1 + 2 * i)
            sp.dma_start(raw[:, s, :].rearrange("p (k n) -> p k n", k=cols or KT), src).then_inc(
                sem(f"raw_in{s}"), 16)

        def w_in_src(layer, col):
            return w_in[layer].rearrange("(k p) n -> p k n", p=P)[:, :, bass.ts(col, CW)]

        def w_out_src(layer, col):
            return w_out[layer].rearrange("(k p) n -> p k n", p=P)[:, :, bass.ts(col, CW)]

        def up_src(w, col):
            return w[0].rearrange("(k p) n -> p k n", p=P)[:, :, bass.ts(col, CW)]

        def down_src(chunk):
            return ffn_w2[0].rearrange("(c p) n -> p c n", p=P)[:, bass.ts(chunk, 2), :]

        def in_col(j):
            return (2 * 3 + j) % IN_CH

        def product(pe, lo_hi, rhs, out_ap, first, last):
            (lh, ll), (rh, rl) = lo_hi, rhs
            pe.matmul(out_ap, lh, rh, start=first, stop=False)
            pe.matmul(out_ap, lh, rl, start=False, stop=False)
            return pe.matmul(out_ap, ll, rh, start=False, stop=last)

        def gemm_chunk(pe, n0, i, w):
            s = n0 % 2
            pe.wait_ge(sem("lo_done"), n0 + 1 + 2 * i)
            for mt in range(2):
                for k in range(KT):
                    a = k * CW + mt * P
                    last = product(pe, (wh[:, s, a:a + P], wl[:, s, a:a + P]), (xh[:, k, 0:w], xl[:, k, 0:w]),
                                   ps[:, 2 * s + mt, 0:w], k == 0, k == KT - 1)
            last.then_inc(sem("gemm_done"), 1)

        ADA = [
            dict(layer=0, groups=[SH1, SC1], both=2),
            dict(layer=0, groups=[G1, SH2, SC2, G2], both=4),
            dict(layer=1, groups=[SH1, SC1, G1, SH2, SC2, G2], both=2),
        ]
        ada_base = [0]
        for ph in ADA:
            ada_base.append(ada_base[-1] + KT * len(ph["groups"]))

        def acc_at(phase, stream, gi):
            return gi if stream == 0 else len(ADA[phase]["groups"]) + gi

        def ada_load(sp, phase, k0, i=0):
            ph = ADA[phase]
            n = len(ph["groups"])
            for gi, g in enumerate(ph["groups"]):
                t = ada_base[phase] + k0 * n + gi
                if t >= 2:
                    sp.wait_ge(sem("ada_used"), t - 1 + n * i)
                src = w_ada[ph["layer"]][:, g * D:(g + 1) * D]
                src = src[bass.ts(k0 + i, P), :]
                sp.dma_start(ada[:, t % 2, :], src).then_inc(sem(f"ada_in{t % 2}"), 16)

        def ada_step(dve, phase, k0, i=0):
            ph = ADA[phase]
            n = len(ph["groups"])
            for gi, g in enumerate(ph["groups"]):
                t = ada_base[phase] + k0 * n + gi
                dve.wait_ge(sem(f"ada_in{t % 2}"), 16 * (t // 2 + 1) + 16 * (n // 2) * i)
                if k0 > 0:
                    dve.wait_ge(sem("ada_used"), t - n + 1 + n * i)
                for s in range(2 if gi < ph["both"] else 1):
                    a = acc[:, acc_at(phase, s, gi), :]
                    scalar = cs[:, s, bass.ds(k0 + i, 1)]
                    if k0 == 0:
                        last = dve.tensor_scalar(a, ada[:, t % 2, :], scalar, None, ALU.mult)
                    else:
                        last = dve.scalar_tensor_tensor(a, ada[:, t % 2, :], scalar, a, ALU.mult, ALU.add)
                last.then_inc(sem("ada_used"), 1)

        def mod_sum(pe, phase, bank):
            ph = ADA[phase]
            pe.wait_ge(sem("ada_used"), ada_base[phase + 1])
            for s in range(2):
                for gi, g in enumerate(ph["groups"]):
                    if s == 1 and gi >= ph["both"]:
                        continue
                    for m in range(KT):
                        col = s * GROUPS * KT + g * KT + m
                        last = pe.matmul(ps[:, bank, col:col + 1], acc[:, acc_at(phase, s, gi), m * P:(m + 1) * P],
                                         ones[:, 0:1], start=True, stop=True)
            last.then_inc(sem("mod_sum"), 1)

        def mod_out(dve, phase, bank):
            ph = ADA[phase]
            layer = ph["layer"]
            dve.wait_ge(sem("mod_sum"), phase + 1)
            g0, g1 = ph["groups"][0], ph["groups"][-1] + 1
            for s in range(2):
                e = g1 if s == 0 else ph["groups"][0] + ph["both"]
                last = dve.tensor_tensor(mod[:, layer, s, g0 * KT:e * KT],
                                         ps[:, bank, (s * GROUPS + g0) * KT:(s * GROUPS + e) * KT],
                                         b_ada_t[:, (layer * GROUPS + g0) * KT:(layer * GROUPS + e) * KT], ALU.add)
            last.then_inc(sem("mod_out"), 1)
            dve.wait_ge(sem("mod_out"), phase + 1)
            for norm, scale, v in ((0, SC1, V_N1), (1, SC2, V_N2)):
                if scale not in ph["groups"]:
                    continue
                for s in range(1 if norm == 1 and ph["both"] < 4 else 2):
                    last = dve.scalar_tensor_tensor(
                        gain[:, layer, norm, s, :], mod[:, layer, s, scale * KT:(scale + 1) * KT], 1.0,
                        vec[:, v + layer * KT:v + (layer + 1) * KT], ALU.add, ALU.mult)
            last.then_inc(sem("gain_out"), 1)

        NORM_BANK = 7
        norm_w = {(0, 0): TOK, (0, 1): TOK, (1, 0): TOK, (1, 1): SEQ}
        h_sem = {(0, 0): ("h_loaded", KT), (0, 1): ("h_mixed0", OUT_CH), (1, 0): ("h_ffn", 2 * KT),
                 (1, 1): ("h_mixed1", OUT_CH)}
        mods_at = {(0, 0): 1, (0, 1): 2, (1, 0): 3, (1, 1): 3}

        def norm_act(act, key):
            q, w = 2 * key[0] + key[1], norm_w[key]
            act.wait_ge(sem(h_sem[key][0]), h_sem[key][1])
            for k in range(KT):
                if k >= 2:
                    act.wait_ge(sem("sq_used"), KT * q + k - 1)
                act.activation(tmp[:, k % 2, 0:w], h[:, k, 0:w], ACT.Square).then_inc(sem("sq"), 1)
            act.wait_ge(sem("var"), q + 1)
            act.activation(std[:, 0, 0:w], var[:, 0, 0:w], ACT.Sqrt).then_inc(sem("std"), 1)
            for u in range(KT * w // SEQ):
                k, s = u % KT, u // KT
                act.wait_ge(sem("tn"), 2 * KT * q + u + 1)
                act.activation(x2[:, k, :] if key == (1, 1) else xh[:, k, span(s)], tn[:, u % 2, :], ACT.Identity,
                               bias=modc(key[0], s, 3 * key[1] + SH1, k)).then_inc(sem("xh"), 1)

        def norm_pe(pe, key):
            q, w = 2 * key[0] + key[1], norm_w[key]
            for k in range(KT):
                pe.wait_ge(sem("sq"), KT * q + k + 1)
                pe.matmul(ps[:, NORM_BANK, 0:w], ones, tmp[:, k % 2, 0:w], start=k == 0,
                          stop=k == KT - 1).then_inc(sem("sq_used"), 1)

        def norm_dve(dve, key):
            q, w = 2 * key[0] + key[1], norm_w[key]
            layer, norm = key
            dve.wait_ge(sem("sq_used"), KT * (q + 1))
            dve.tensor_scalar(var[:, 0, 0:w], ps[:, NORM_BANK, 0:w], 1.0 / D, EPS, ALU.mult, ALU.add).then_inc(
                sem("var"), 1)
            dve.wait_ge(sem("std"), q + 1)
            dve.reciprocal(rstd[:, 0, 0:w], std[:, 0, 0:w]).then_inc(sem("rstd"), 1)
            dve.wait_ge(sem("rstd"), q + 1)
            dve.wait_ge(sem("gain_out"), mods_at[key])
            units = KT * w // SEQ
            for u in range(units + 1):
                if u < units:
                    k, s = u % KT, u // KT
                    if u >= 2:
                        dve.wait_ge(sem("xh" if key == (1, 1) else "xl"), 2 * KT * q + u - 1)
                    dve.scalar_tensor_tensor(tn[:, u % 2, :], h[:, k, span(s)], gain[:, layer, norm, s, k:k + 1],
                                             rstd[:, 0, span(s)], ALU.mult, ALU.mult).then_inc(sem("tn"), 1)
                if u >= 1 and key != (1, 1):
                    k, s = (u - 1) % KT, (u - 1) // KT
                    dve.wait_ge(sem("xh"), 2 * KT * q + u)
                    dve.scalar_tensor_tensor(xl[:, k, span(s)], tn[:, (u - 1) % 2, :],
                                             modc(layer, s, 3 * norm + SH1, k), xh[:, k, span(s)],
                                             ALU.add, ALU.subtract).then_inc(sem("xl"), 1)

        QK = CT + 1

        def qk_w(layer, j):
            return TOK if j == QK - 1 else width(layer)

        def qk_act(act, layer):
            for j in range(QK):
                w = qk_w(layer, j)
                if j >= 2:
                    act.wait_ge(sem("qk_ss"), QK * layer + j - 1)
                act.activation(tmp[:, j % 2, 0:w], z[:, 12 + j, 0:w], ACT.Square).then_inc(sem("qk_sq"), 1)
                if j >= 1:
                    qk_root(act, layer, j - 1)
            qk_root(act, layer, QK - 1)

        def qk_root(act, layer, j):
            w = qk_w(layer, j)
            act.wait_ge(sem("qk_var"), QK * layer + j + 1)
            act.activation(std[:, j % 2, 0:w], var[:, j % 2, 0:w], ACT.Sqrt).then_inc(sem("qk_std"), 1)

        def qk_pe(pe, layer):
            for j in range(QK + 1):
                if j < QK:
                    w = qk_w(layer, j)
                    pe.wait_ge(sem("qk_sq"), QK * layer + j + 1)
                    if j >= 2:
                        pe.wait_ge(sem("qk_var"), QK * layer + j - 1)
                    pe.matmul(ps[:, 6 + j % 2, 0:w], bones, tmp[:, j % 2, 0:w], start=True, stop=True).then_inc(
                        sem("qk_ss"), 1)
                if j >= 1:
                    i = j - 1
                    pe.wait_ge(sem("qk_hat"), QK * layer + i + 1)
                    if i >= 2:
                        pe.wait_ge(sem("qk_rs"), QK * layer + i - 1)
                    pe.matmul(ps[:, 4 + i % 2, 0:SEQ], rot, z[:, 12 + i, 0:SEQ], start=True, stop=True).then_inc(
                        sem("qk_rot"), 1)
            pe.wait_ge(sem("qk_done"), QK * layer + QK)
            for g in range(2):
                for half in range(2):
                    i = 2 * g + half
                    pe.matmul(ps[:, i, :], const[:, C_DUP + i * P:C_DUP + (i + 1) * P], z[:, 16, :],
                              start=True, stop=True).then_inc(sem(f"kd_ps{layer}"), 1)
            for b in range(NBLK):
                last = pe.transpose(ps[:, 6, b * P:(b + 1) * P], z[:, 17, b * P:(b + 1) * P], ident)
            last.then_inc(sem(f"vt_ps{layer}"), 1)

        def qk_dve(dve, layer):
            for j in range(QK):
                w = qk_w(layer, j)
                dve.wait_ge(sem("qk_ss"), QK * layer + j + 1)
                dve.tensor_scalar(var[:, j % 2, 0:w], ps[:, 6 + j % 2, 0:w], 1.0 / HD, EPS, ALU.mult,
                                  ALU.add).then_inc(sem("qk_var"), 1)
                if j >= 1:
                    qk_scale(dve, layer, j - 1)
                if j >= 2:
                    qk_turn(dve, layer, j - 2)
            qk_scale(dve, layer, QK - 1)
            qk_turn(dve, layer, QK - 2)
            qk_turn(dve, layer, QK - 1)

        def qk_scale(dve, layer, j):
            w = qk_w(layer, j)
            g = vcol((V_KG if j == QK - 1 else V_QG) + layer)
            dve.wait_ge(sem("qk_std"), QK * layer + j + 1)
            dve.reciprocal(rstd[:, j % 2, 0:w], std[:, j % 2, 0:w]).then_inc(sem("qk_rcp"), 1)
            dve.wait_ge(sem("qk_rcp"), QK * layer + j + 1)
            dve.scalar_tensor_tensor(z[:, 12 + j, 0:w], z[:, 12 + j, 0:w], g, rstd[:, j % 2, 0:w], ALU.mult,
                                     ALU.mult).then_inc(sem("qk_hat"), 1)

        def qk_turn(dve, layer, j):
            lat = z[:, 12 + j, 0:SEQ]
            dve.wait_ge(sem("qk_rot"), QK * layer + j + 1)
            dve.tensor_tensor(tn[:, j % 2, :], ps[:, 4 + j % 2, 0:SEQ], sin, ALU.mult).then_inc(
                sem("qk_rs"), 1)
            dve.tensor_tensor(lat, lat, cos, ALU.mult).then_inc(sem("qk_rc"), 1)
            dve.wait_ge(sem("qk_rc"), QK * layer + j + 1)
            dve.tensor_tensor(lat, lat, tn[:, j % 2, :], ALU.add).then_inc(sem("qk_done"), 1)

        def units(layer):
            return [(hd, b) for b in range(NBLK if layer == 0 else 2) for hd in range(HEADS)]

        def unit_keys(b):
            return (0, NBLK) if b < 2 else (2, NBLK)

        def att_pe(pe, layer):
            us = units(layer)
            pe.wait_ge(sem(f"kd{layer}"), 4)
            for u in range(len(us) + 2):
                if u < len(us):
                    hd, b = us[u]
                    k0, k1 = unit_keys(b)
                    if u >= 2:
                        pe.wait_ge(sem(f"p{layer}"), u - 1)
                    s = ps[:, u % 2, 0:(k1 - k0) * P]
                    last = pe.matmul(s, z[:, 12 + hd // 2, b * P:(b + 1) * P],
                                     kd[:, hd // (HEADS // N_KV), hd % 2, k0 * P:k1 * P], start=True, stop=True)
                    if b < 2:
                        m = P * (1 - b)
                        last = pe.matmul(ps[:, u % 2, m:m + P], ident_b[:, :], mask_b[:, b, :], start=False,
                                         stop=True, skip_group_check=True)
                    last.then_inc(sem(f"s{layer}"), 1)
                if 1 <= u <= len(us):
                    v = u - 1
                    k0, k1 = unit_keys(us[v][1])
                    pe.wait_ge(sem(f"p{layer}"), v + 1)
                    if v >= 2:
                        pe.wait_ge(sem(f"pt{layer}"), v - 1)
                    for i in range(k1 - k0):
                        last = pe.transpose(ps[:, 2 + v % 2, i * P:(i + 1) * P], pm[:, v % 2, i * P:(i + 1) * P],
                                            ident)
                    last.then_inc(sem(f"pt_ps{layer}"), 1)
                if u >= 2:
                    v = u - 2
                    hd, b = us[v]
                    g = hd // (HEADS // N_KV)
                    k0, k1 = unit_keys(b)
                    pe.wait_ge(sem(f"pt{layer}"), v + 1)
                    if v == 0:
                        pe.wait_ge(sem(f"vtok{layer}"), 1)
                    if v >= 2:
                        pe.wait_ge(sem(f"o{layer}"), v - 1)
                    for i in range(k1 - k0):
                        last = pe.matmul(ps[:, 4 + v % 2, 0:HD], pt[:, v % 2, i * P:(i + 1) * P],
                                         vtok[:, k0 + i, g * HD:(g + 1) * HD], start=i == 0, stop=i == k1 - k0 - 1)
                    last.then_inc(sem(f"o_ps{layer}"), 1)

        def att_act(act, layer):
            for i in range(4):
                act.wait_ge(sem(f"kd_ps{layer}"), i + 1)
                act.activation(kd[:, i // 2, i % 2, :], ps[:, i, :], ACT.Copy).then_inc(sem(f"kd{layer}"), 1)
            us = units(layer)
            for u in range(len(us) + 2):
                if u < len(us):
                    hd, b = us[u]
                    k0, k1 = unit_keys(b)
                    n = (k1 - k0) * P
                    act.wait_ge(sem(f"negm{layer}"), u + 1)
                    if u >= 2:
                        act.wait_ge(sem(f"pt_ps{layer}"), u - 1)
                    act.activation(pm[:, u % 2, 0:n], ps[:, u % 2, 0:n], ACT.Exp, bias=negm[:, u:u + 1], scale=SCALE,
                                   accum_out=rsum[:, u:u + 1]).then_inc(sem(f"p{layer}"), 1)
                    i = layer * HEADS + hd
                    act.activation(esink[:, u:u + 1], nsink[:, i:i + 1], ACT.Exp, bias=negm[:, u:u + 1],
                                   scale=-1.0).then_inc(sem(f"es{layer}"), 1)
                if u >= 2:
                    v = u - 2
                    hd, b = us[v]
                    act.wait_ge(sem(f"o_ps{layer}"), v + 1)
                    act.wait_ge(sem(f"rden{layer}"), v + 1)
                    act.activation(otok[:, b, hd * HD:(hd + 1) * HD], ps[:, 4 + v % 2, 0:HD], ACT.Copy,
                                   scale=rden[:, v:v + 1]).then_inc(sem(f"o{layer}"), 1)

        def att_dve(dve, layer):
            dve.wait_ge(sem(f"vt_ps{layer}"), 1)
            dve.tensor_copy(vtok[:, :, :].rearrange("p b c -> p (b c)"), ps[:, 6, :]).then_inc(sem(f"vtok{layer}"), 1)
            us = units(layer)
            for u in range(len(us) + 1):
                if u < len(us):
                    hd, b = us[u]
                    k0, k1 = unit_keys(b)
                    dve.wait_ge(sem(f"s{layer}"), u + 1)
                    dve.tensor_reduce(mx[:, u:u + 1], ps[:, u % 2, 0:(k1 - k0) * P], AX.X, ALU.max).then_inc(
                        sem(f"mx{layer}"), 1)
                    dve.wait_ge(sem(f"mx{layer}"), u + 1)
                    i = layer * HEADS + hd
                    dve.tensor_scalar(negm[:, u:u + 1], mx[:, u:u + 1], -SCALE, nsink[:, i:i + 1], ALU.mult,
                                      ALU.min).then_inc(sem(f"negm{layer}"), 1)
                if u >= 1:
                    v = u - 1
                    k0, k1 = unit_keys(us[v][1])
                    n = (k1 - k0) * P
                    dve.wait_ge(sem(f"es{layer}"), v + 1)
                    dve.tensor_tensor(rden[:, v:v + 1], rsum[:, v:v + 1], esink[:, v:v + 1], ALU.add).then_inc(
                        sem(f"den{layer}"), 1)
                    dve.wait_ge(sem(f"pt_ps{layer}"), v + 1)
                    if v >= 2:
                        dve.wait_ge(sem(f"o_ps{layer}"), v - 1)
                    dve.tensor_copy(pt[:, v % 2, 0:n], ps[:, 2 + v % 2, 0:n]).then_inc(sem(f"pt{layer}"), 1)
                    dve.wait_ge(sem(f"den{layer}"), v + 1)
                    dve.reciprocal(rden[:, v:v + 1], rden[:, v:v + 1]).then_inc(sem(f"rden{layer}"), 1)
                if u % 4 == 3 and u < 16:
                    conv_tile(dve, layer, u // 4)

        def conv_tile(dve, layer, t):
            w = width(layer)
            n = w // SEQ
            bg, u, y = z[:, t, 0:w], z[:, CT + t, 0:w], z[:, 2 * CT + t, 0:w]
            u3, y3 = u.rearrange("p (s t) -> p s t", s=n), y.rearrange("p (s t) -> p s t", s=n)
            tap = [vcol(V_CW + (layer * 3 + i) * CT + t) for i in range(3)]
            done = sem(f"cv{layer}")
            dve.tensor_tensor(u, u, y, ALU.mult).then_inc(done, 1)
            dve.wait_ge(done, 5 * t + 1)
            dve.tensor_scalar(y, u, tap[1], None, ALU.mult).then_inc(done, 1)
            dve.wait_ge(done, 5 * t + 2)
            dve.scalar_tensor_tensor(y3[:, :, 1:], u3[:, :, :-1], tap[0], y3[:, :, 1:], ALU.mult,
                                     ALU.add).then_inc(done, 1)
            dve.wait_ge(done, 5 * t + 3)
            dve.scalar_tensor_tensor(y3[:, :, :-1], u3[:, :, 1:], tap[2], y3[:, :, :-1], ALU.mult,
                                     ALU.add).then_inc(done, 1)
            dve.wait_ge(done, 5 * t + 4)
            dve.tensor_tensor(y, y, bg, ALU.mult).then_inc(done, 1)

        def merge_act(act, layer):
            w, nb = width(layer), width(layer) // P
            for b in range(nb):
                act.wait_ge(sem(f"o{layer}"), len(units(layer)))
                if b >= 2:
                    act.wait_ge(sem(f"osq{layer}"), b - 1)
                act.activation(pm[:, b % 2, :], otok[:, b, :], ACT.Square, accum_out=osq[:, 0, b:b + 1]).then_inc(
                    sem(f"osq{layer}"), 1)
            for t in range(CT):
                act.wait_ge(sem(f"cv{layer}"), 5 * (t + 1))
                if t >= 2:
                    act.wait_ge(sem(f"cv_ss{layer}"), t - 1)
                act.activation(tmp[:, t % 2, 0:w], z[:, 2 * CT + t, 0:w], ACT.Square).then_inc(sem(f"cv_sq{layer}"), 1)
            act.wait_ge(sem(f"ovar{layer}"), 1)
            act.activation(osq[:, 2, 0:nb], osq[:, 1, 0:nb], ACT.Sqrt).then_inc(sem(f"ostd{layer}"), 1)
            act.wait_ge(sem(f"cv_var{layer}"), 1)
            act.activation(std[:, 0, 0:w], var[:, 0, 0:w], ACT.Sqrt).then_inc(sem(f"cv_std{layer}"), 1)
            for b in range(nb):
                act.wait_ge(sem(f"ot_ps{layer}"), b + 1)
                for i in range(CT):
                    act.activation(xh[:, CT + i, b * P:(b + 1) * P], ps[:, b, i * P:(i + 1) * P], ACT.Copy,
                                   scale=vcol(V_GA + layer * CT + i)).then_inc(sem(f"yah{layer}"), 1)
            for t in range(CT):
                act.wait_ge(sem(f"cv_n{layer}"), t + 1)
                act.activation(xh[:, t, 0:w], z[:, 2 * CT + t, 0:w], ACT.Copy).then_inc(sem(f"ych{layer}"), 1)

        def merge_pe(pe, layer):
            w, nb = width(layer), width(layer) // P
            for t in range(CT):
                pe.wait_ge(sem(f"cv_sq{layer}"), t + 1)
                pe.matmul(ps[:, NORM_BANK, 0:w], ones, tmp[:, t % 2, 0:w], start=t == 0,
                          stop=t == CT - 1).then_inc(sem(f"cv_ss{layer}"), 1)
            for b in range(nb):
                pe.wait_ge(sem(f"on{layer}"), b + 1)
                for i in range(CT):
                    last = pe.transpose(ps[:, b, i * P:(i + 1) * P], otok[:, b, i * P:(i + 1) * P], ident)
                last.then_inc(sem(f"ot_ps{layer}"), 1)

        def merge_dve(dve, layer):
            w, nb = width(layer), width(layer) // P
            dve.wait_ge(sem(f"osq{layer}"), nb)
            dve.tensor_scalar(osq[:, 1, 0:nb], osq[:, 0, 0:nb], 1.0 / D_CONV, EPS, ALU.mult, ALU.add).then_inc(
                sem(f"ovar{layer}"), 1)
            dve.wait_ge(sem(f"cv_ss{layer}"), CT)
            dve.tensor_scalar(var[:, 0, 0:w], ps[:, NORM_BANK, 0:w], 1.0 / D_CONV, EPS, ALU.mult,
                              ALU.add).then_inc(sem(f"cv_var{layer}"), 1)
            dve.wait_ge(sem(f"ostd{layer}"), 1)
            dve.reciprocal(osq[:, 0, 0:nb], osq[:, 2, 0:nb]).then_inc(sem(f"orcp{layer}"), 1)
            dve.wait_ge(sem(f"orcp{layer}"), 1)
            for b in range(nb):
                dve.tensor_scalar(otok[:, b, :], otok[:, b, :], osq[:, 0, b:b + 1], None, ALU.mult).then_inc(
                    sem(f"on{layer}"), 1)
            dve.wait_ge(sem(f"cv_std{layer}"), 1)
            dve.reciprocal(rstd[:, 0, 0:w], std[:, 0, 0:w]).then_inc(sem(f"cv_rcp{layer}"), 1)
            dve.wait_ge(sem(f"cv_rcp{layer}"), 1)
            for t in range(CT):
                dve.scalar_tensor_tensor(z[:, 2 * CT + t, 0:w], z[:, 2 * CT + t, 0:w], vcol(V_GC + layer * CT + t),
                                         rstd[:, 0, 0:w], ALU.mult, ALU.mult).then_inc(sem(f"cv_n{layer}"), 1)
            for b in range(nb):
                dve.wait_ge(sem(f"yah{layer}"), CT * (b + 1))
                for i in range(CT):
                    dve.scalar_tensor_tensor(xl[:, CT + i, b * P:(b + 1) * P], ps[:, b, i * P:(i + 1) * P],
                                             vcol(V_GA + layer * CT + i), xh[:, CT + i, b * P:(b + 1) * P],
                                             ALU.mult, ALU.subtract).then_inc(sem(f"yl{layer}"), 1)
            for t in range(CT):
                dve.wait_ge(sem(f"ych{layer}"), t + 1)
                dve.tensor_tensor(xl[:, t, 0:w], z[:, 2 * CT + t, 0:w], xh[:, t, 0:w], ALU.subtract).then_inc(
                    sem(f"yl{layer}"), 1)

        def yl_count(layer):
            return width(layer) // P * CT + CT

        R_LG, R_TOP, R_SEL1, R_SEL, R_COMB, R_RANK, R_POS, R_IDX, R_GATE = range(9)

        def rt(i, b):
            return route[:, i, b, :]

        def route_pe(pe):
            pe.wait_ge(sem("xh"), 7 * KT)
            for b in range(2):
                for k in range(KT):
                    last = pe.matmul(ps[:, 6, b * EXPERTS:(b + 1) * EXPERTS], x2[:, k, b * P:(b + 1) * P],
                                     router[:, k, :], start=k == 0, stop=k == KT - 1)
            last.then_inc(sem("logits"), 1)
            for b in range(2):
                for k in range(KT):
                    a = (k % 4) * P
                    last = pe.transpose(ps[:, 2 * b + k // 4, a:a + P], x2[:, k, b * P:(b + 1) * P], ident)
                last.then_inc(sem("x2t_ps"), 1)
            pe.wait_ge(sem("g2_diag"), 1)
            for k in range(KT):
                last = pe.matmul(ps[:, 4 + k // 4, (k % 4) * P:(k % 4 + 1) * P], ones, hg[:, k * P:(k + 1) * P],
                                 start=True, stop=True)
            last.then_inc(sem("g2_ps"), 1)
            pe.wait_ge(sem("selected"), 1)
            tri = const[:, C_TRI:C_TRI + P]
            r0 = 2 * EXPERTS
            pe.matmul(ps[:, 7, r0:r0 + EXPERTS], tri, rt(R_SEL, 0), start=True, stop=True)
            pe.matmul(ps[:, 7, r0 + EXPERTS:r0 + 2 * EXPERTS], tri, rt(R_SEL, 1), start=True, stop=False)
            pe.matmul(ps[:, 7, r0 + EXPERTS:r0 + 2 * EXPERTS], ones, rt(R_SEL, 0), start=False, stop=True)
            pe.matmul(ps[:, 7, 0:EXPERTS], ones, rt(R_SEL, 0), start=True, stop=False)
            pe.matmul(ps[:, 7, 0:EXPERTS], ones, rt(R_SEL, 1), start=False, stop=True).then_inc(sem("rank_ps"), 1)
            pe.wait_ge(sem("g2b"), 1)
            pe.wait_ge(sem("x2t_l"), 2)
            for b in range(2):
                for k in range(KT):
                    a = (k % 4) * P
                    last = pe.transpose(ps[:, 2 * b + k // 4, a:a + P], h[:, k, b * P:(b + 1) * P], ident)
                last.then_inc(sem("h_ps"), 1)

        def route_act(act):
            for b in range(2):
                act.wait_ge(sem("x2t_ps"), b + 1)
                act.activation(x2t_h[:, b, :], ps[:, 2 * b:2 * b + 2, :].rearrange("p a b -> p (a b)"),
                               ACT.Copy).then_inc(sem("x2t_h"), 1)
            act.wait_ge(sem("top"), 1)
            for b in range(2):
                last = act.activation(rt(R_GATE, b)[:, 0:1], rt(R_GATE, b)[:, 2:3], ACT.Exp)
            last.then_inc(sem("gate_exp"), 1)
            act.wait_ge(sem("g2_ps"), 1)
            act.activation(g2b[:, :], ps[:, 4:6, :].rearrange("p a b -> p (a b)"), ACT.Copy).then_inc(sem("g2b"), 1)
            for b in range(2):
                act.wait_ge(sem("h_ps"), b + 1)
                act.activation(htok[:, b, :], ps[:, 2 * b:2 * b + 2, :].rearrange("p a b -> p (a b)"),
                               ACT.Copy).then_inc(sem("htok"), 1)

        def route_dve(dve):
            step = [0]

            def link(ins):
                step[0] += 1
                ins.then_inc(sem("route"), 1)
                dve.wait_ge(sem("route"), step[0])

            dve.wait_ge(sem("xh"), 7 * KT)
            for k in range(KT):
                last = dve.tensor_scalar(hg[:, k * P:(k + 1) * P], ident, modc(1, 0, G2, k), None, ALU.mult)
            last.then_inc(sem("g2_diag"), 1)
            dve.wait_ge(sem("logits"), 1)
            link(dve.tensor_copy(route[:, R_LG, :, :].rearrange("p b e -> p (b e)"), ps[:, 6, 0:2 * EXPERTS]))
            for b in range(2):
                last = dve.max(rt(R_TOP, b), rt(R_LG, b))
            link(last)
            for b in range(2):
                last = dve.tensor_tensor(rt(R_GATE, b)[:, 2:3], rt(R_TOP, b)[:, 1:2], rt(R_TOP, b)[:, 0:1],
                                         ALU.subtract)
            last.then_inc(sem("top"), 1)
            for b in range(2):
                last = dve.max_index(top_i[:, b, :], rt(R_TOP, b), rt(R_LG, b))
            link(last)
            link(dve.tensor_copy(route[:, R_IDX, :, :].rearrange("p b e -> p (b e)"),
                                 top_i[:, :, :].rearrange("p b e -> p (b e)")))
            iota_e = const[:, C_IOTA:C_IOTA + EXPERTS]
            for b in range(2):
                dve.tensor_scalar(rt(R_SEL1, b), iota_e, rt(R_IDX, b)[:, 0:1], None, ALU.is_equal)
                last = dve.tensor_scalar(rt(R_SEL, b), iota_e, rt(R_IDX, b)[:, 1:2], None, ALU.is_equal)
            link(last)
            dve.wait_ge(sem("gate_exp"), 1)
            for b in range(2):
                last = dve.tensor_scalar(rt(R_GATE, b)[:, 1:2], rt(R_GATE, b)[:, 0:1], 1.0, None, ALU.add)
            link(last)
            for b in range(2):
                last = dve.reciprocal(rt(R_GATE, b)[:, 3:4], rt(R_GATE, b)[:, 1:2])
            link(last)
            for b in range(2):
                last = dve.tensor_tensor(rt(R_GATE, b)[:, 4:5], rt(R_GATE, b)[:, 3:4], rt(R_GATE, b)[:, 0:1], ALU.mult)
            link(last)
            for b in range(2):
                last = dve.tensor_scalar(rt(R_COMB, b), rt(R_SEL, b), rt(R_GATE, b)[:, 4:5], None, ALU.mult)
            link(last)
            for b in range(2):
                last = dve.scalar_tensor_tensor(rt(R_COMB, b), rt(R_SEL1, b), rt(R_GATE, b)[:, 3:4], rt(R_COMB, b),
                                                ALU.mult, ALU.add)
            link(last)
            dve.tensor_tensor(route[:, R_SEL, :, :], route[:, R_SEL, :, :], route[:, R_SEL1, :, :],
                              ALU.add).then_inc(sem("selected"), 1)
            dve.wait_ge(sem("selected"), 1)
            link(dve.tensor_scalar(route[:, R_POS, :, :], route[:, R_SEL, :, :], -4.0 * TOK, 4.0 * TOK, ALU.mult,
                                   ALU.add))
            dve.wait_ge(sem("rank_ps"), 1)
            link(dve.tensor_tensor(route[:, R_POS, :, :].rearrange("p b e -> p (b e)"),
                                   route[:, R_POS, :, :].rearrange("p b e -> p (b e)"),
                                   ps[:, 7, 2 * EXPERTS:4 * EXPERTS], ALU.add))
            dve.tensor_reduce(most[:, :], ps[:, 7, 0:EXPERTS], AX.X, ALU.max).then_inc(sem("most"), 1)
            for b in range(2):
                dve.wait_ge(sem("x2t_h"), b + 1)
                dve.tensor_tensor(x2t_l[:, b, :], ps[:, 2 * b:2 * b + 2, :].rearrange("p a b -> p (a b)"),
                                  x2t_h[:, b, :], ALU.subtract).then_inc(sem("x2t_l"), 1)

        def experts(eng, q, body):
            body(0, True, False)
            with eng.Fori(0, EXPERTS - 2) as i:
                body(1 + i, False, False)
            body(EXPERTS - 1, False, True)

        def m_load(sp, q, e, j, first):
            g = e + EXPERTS * q
            s = j % 3
            n = MCH * g + j
            if not first or j >= 3:
                sp.wait_ge(sem("mlo"), n - 2)
            if j < 8:
                dst = mraw[:, s, :].rearrange("p (k w n) -> p k w n", k=KT, w=2)
                for w, src in enumerate((moe_w1, moe_w3)):
                    sp.dma_start(dst[:, :, w, :], src.rearrange("a e (k p) n -> p (a e k) n", p=P)[
                        :, bass.ts(e, KT), j * MC:(j + 1) * MC]).then_inc(sem(f"mraw{s}"), 16)
            else:
                dst = mraw[:, s, :].rearrange("p (k n) -> p k n", k=FT)
                src = moe_w2.rearrange("a e (k p) n -> p (a e k) n", p=P)
                for k0, k1 in ((0, 6), (6, FT)):
                    sp.dma_start(dst[:, k0:k1, :], src[:, bass.ds(e * FT + k0, k1 - k0),
                                                       (j - 8) * CW:(j - 7) * CW]).then_inc(sem(f"mraw{s}"), 16)

        def m_arrived(eng, q, e, j):
            g = e + EXPERTS * q
            eng.wait_ge(sem(f"mraw{j % 3}"), 32 * (g * 4 + j // 3 + 1))

        def m_hi(act, q, e, j, first):
            g = e + EXPERTS * q
            s = j % 3
            m_arrived(act, q, e, j)
            if not first or j >= 3:
                act.wait_ge(sem("mgemm"), MCH * g + j - 2)
            act.activation(mwh[:, s, :], mraw[:, s, :], ACT.Copy).then_inc(sem("mhi"), 1)

        def m_lo(dve, q, e, j, first):
            g = e + EXPERTS * q
            s = j % 3
            m_arrived(dve, q, e, j)
            dve.wait_ge(sem("mhi"), MCH * g + j + 1)
            dve.tensor_tensor(mwl[:, s, :], mraw[:, s, :], mwh[:, s, :], ALU.subtract).then_inc(sem("mlo"), 1)

        def gather(pe, q, e):
            g = e + EXPERTS * q
            pe.wait_ge(sem("pick"), g + 1)
            for m in range(KT):
                o = ps[:, 4 + m // 4, (m % 4) * P:(m % 4 + 1) * P]
                for b in range(2):
                    for i, part in enumerate((x2t_h, x2t_l)):
                        last = pe.matmul(o, part[:, b, m * P:(m + 1) * P], pick_r[:, b, :], start=b == 0 and i == 0,
                                         stop=b == 1 and i == 1)
            last.then_inc(sem("xg_ps"), 1)

        def put_back(pe, q, e):
            g = e + EXPERTS * q
            pe.wait_ge(sem("ye_l"), g + 1)
            pe.wait_ge(sem("place"), g + 1)
            for b in range(2):
                for half in range(2):
                    o = ps[:, 2 + 2 * b + half, :]
                    pe.matmul(o, place[:, b * P:(b + 1) * P], ye_h[:, half * 512:(half + 1) * 512], start=True,
                              stop=False)
                    pe.matmul(o, place[:, b * P:(b + 1) * P], ye_l[:, half * 512:(half + 1) * 512], start=False,
                              stop=True).then_inc(sem("put"), 1)

        def m_pe(pe, q, e, first, last_e):
            g = e + EXPERTS * q
            for j in range(8):
                s = j % 3
                pe.wait_ge(sem("mlo"), MCH * g + j + 1)
                if j == 0:
                    pe.wait_ge(sem("xg_l"), g + 1)
                if j >= 2:
                    pe.wait_ge(sem("hg"), 8 * g + j - 1)
                for k in range(KT):
                    a = k * 2 * MC
                    last = product(pe, (xg_h[:, k, :], xg_l[:, k, :]),
                                   (mwh[:, s, a:a + 2 * MC], mwl[:, s, a:a + 2 * MC]), ps[:, j % 2, 0:2 * MC],
                                   k == 0, k == KT - 1)
                last.then_inc(sem("mgemm"), 1)
                if j == 1 and not first:
                    put_back(pe, q, e - 1)
                if j == 3:
                    if first:
                        pe.wait_ge(sem("pick"), 1)
                    else:
                        pe.wait_ge(sem("yacc"), 4 * g + 4)
                    for b in range(2):
                        last = pe.transpose(ps[:, 2, b * P:(b + 1) * P], pick[:, b, :], ident)
                    last.then_inc(sem("place_ps"), 1)
            if not last_e:
                gather(pe, q, e + 1)
            pe.wait_ge(sem("hg"), 8 * g + 8)
            pe.wait_ge(sem("place"), g + 1)
            for k in range(FT):
                bank = (2, 3, 0)[k // 4]
                last = pe.transpose(ps[:, bank, (k % 4) * P:(k % 4 + 1) * P], hg[:, k * P:(k + 1) * P], ident)
            last.then_inc(sem("ht_ps"), 1)
            pe.wait_ge(sem("ht_l"), g + 1)
            for c4 in range(4):
                s = (8 + c4) % 3
                pe.wait_ge(sem("mlo"), MCH * g + 9 + c4)
                for k in range(FT):
                    last = product(pe, (ht_h[:, k * P:(k + 1) * P], ht_l[:, k * P:(k + 1) * P]),
                                   (mwh[:, s, k * CW:(k + 1) * CW], mwl[:, s, k * CW:(k + 1) * CW]),
                                   ps[:, 6 + c4 // 2, (c4 % 2) * CW:(c4 % 2 + 1) * CW], k == 0, k == FT - 1)
                last.then_inc(sem("mgemm"), 1)
            if last_e:
                put_back(pe, q, e)

        def m_act(act, q, e, first, last_e):
            g = e + EXPERTS * q
            for j in range(8):
                m_hi(act, q, e, j + 1, first)
                act.wait_ge(sem("mgemm"), MCH * g + j + 1)
                if not first or j >= 2:
                    act.wait_ge(sem("hg"), 8 * g + j - 1)
                act.activation(sg[:, j % 2, :], ps[:, j % 2, 0:MC], ACT.Silu).then_inc(sem("sg"), 1)
            act.wait_ge(sem("ht_ps"), g + 1)
            act.activation(ht_h[:, 0:8 * P], ps[:, 2:4, :].rearrange("p a b -> p (a b)"), ACT.Copy)
            act.activation(ht_h[:, 8 * P:FT * P], ps[:, 0, 0:(FT - 8) * P], ACT.Copy).then_inc(sem("ht_h"), 1)
            if not last_e:
                xg_act(act, q, e + 1)
            for j in range(9, MCH + 1):
                if j < MCH:
                    m_hi(act, q, e, j, first)
                elif not last_e:
                    m_hi(act, q, e + 1, 0, False)
            act.wait_ge(sem("mgemm"), MCH * g + MCH)
            act.activation(ye_h[:, :], ps[:, 6:8, :].rearrange("p a b -> p (a b)"), ACT.Copy).then_inc(
                sem("ye_h"), 1)

        def xg_act(act, q, e):
            g = e + EXPERTS * q
            act.wait_ge(sem("xg_ps"), g + 1)
            act.activation(xg_h[:, :, :].rearrange("p k s -> p (k s)"),
                           ps[:, 4:6, :].rearrange("p a b -> p (a b)"), ACT.Copy).then_inc(sem("xg_h"), 1)

        def xg_dve(dve, q, e):
            g = e + EXPERTS * q
            dve.wait_ge(sem("xg_h"), g + 1)
            dve.tensor_tensor(xg_l[:, :, :].rearrange("p k s -> p (k s)"),
                              ps[:, 4:6, :].rearrange("p a b -> p (a b)"),
                              xg_h[:, :, :].rearrange("p k s -> p (k s)"), ALU.subtract).then_inc(sem("xg_l"), 1)

        def pick_dve(dve, q, e):
            g = e + EXPERTS * q
            iota = const[:, C_IOTA:C_IOTA + P]
            for b in range(2):
                pos = route[:, R_POS, b, bass.ds(e, 1)]
                dve.tensor_scalar(pick[:, b, :], iota, pos, None, ALU.is_equal)
                last = dve.tensor_scalar(pick_r[:, b, :], iota, pos, None, ALU.is_equal)
            last.then_inc(sem("pick"), 1)

        def sum_dve(dve, q, e):
            g = e + EXPERTS * q
            for b in range(2):
                for half in range(2):
                    i = 2 * b + half
                    dve.wait_ge(sem("put"), 4 * g + i + 1)
                    dve.wait_ge(sem("yacc"), 4 * g + 1 + i)
                    y = ytok[:, b, half * 512:(half + 1) * 512]
                    dve.scalar_tensor_tensor(y, ps[:, 2 + i, :], route[:, R_COMB, b, bass.ds(e, 1)], y, ALU.mult,
                                             ALU.add).then_inc(sem("yacc"), 1)

        def m_dve(dve, q, e, first, last_e):
            g = e + EXPERTS * q
            for j in range(8):
                m_lo(dve, q, e, j + 1, first)
                dve.wait_ge(sem("sg"), 8 * g + j + 1)
                dve.tensor_tensor(hg[:, j * MC:(j + 1) * MC], sg[:, j % 2, :], ps[:, j % 2, MC:2 * MC],
                                  ALU.mult).then_inc(sem("hg"), 1)
                if j == 1 and not first:
                    sum_dve(dve, q, e - 1)
                if j == 3:
                    dve.wait_ge(sem("place_ps"), g + 1)
                    dve.tensor_copy(place[:, :], ps[:, 2, 0:SEQ]).then_inc(sem("place"), 1)
                if j == 5 and not last_e:
                    pick_dve(dve, q, e + 1)
            dve.wait_ge(sem("ht_h"), g + 1)
            dve.tensor_tensor(ht_l[:, 0:8 * P], ps[:, 2:4, :].rearrange("p a b -> p (a b)"), ht_h[:, 0:8 * P],
                              ALU.subtract)
            dve.tensor_tensor(ht_l[:, 8 * P:FT * P], ps[:, 0, 0:(FT - 8) * P], ht_h[:, 8 * P:FT * P],
                              ALU.subtract).then_inc(sem("ht_l"), 1)
            if not last_e:
                xg_dve(dve, q, e + 1)
            for j in range(9, MCH + 1):
                if j < MCH:
                    m_lo(dve, q, e, j, first)
                elif not last_e:
                    m_lo(dve, q, e + 1, 0, False)
            dve.wait_ge(sem("ye_h"), g + 1)
            dve.tensor_tensor(ye_l[:, :], ps[:, 6:8, :].rearrange("p a b -> p (a b)"), ye_h[:, :],
                              ALU.subtract).then_inc(sem("ye_l"), 1)
            if last_e:
                sum_dve(dve, q, e)

        def pass_sp(sp, q):
            if q == 0:
                sp.wait_ge(sem("yl1"), yl_count(1))
            experts(sp, q, lambda e, first, last: [m_load(sp, q, e, j, first) for j in range(MCH)] and None)

        def pass_pe(pe, q):
            gather(pe, q, 0)
            experts(pe, q, lambda e, first, last: m_pe(pe, q, e, first, last))

        def pass_act(act, q):
            m_hi(act, q, 0, 0, True)
            xg_act(act, q, 0)
            experts(act, q, lambda e, first, last: m_act(act, q, e, first, last))

        def pass_dve(dve, q):
            pick_dve(dve, q, 0)
            m_lo(dve, q, 0, 0, True)
            xg_dve(dve, q, 0)
            experts(dve, q, lambda e, first, last: m_dve(dve, q, e, first, last))

        def overflow(eng):
            eng.wait_ge(sem("most"), 1)
            return eng.value_load(most[0:1, 0:1], min_val=0, max_val=SEQ) > P

        block = stack.enter_context(nc.Block())
        PARTS = [(0, PART), (PART, FF_CH)]

        @block.sync
        def _(sp):
            for dst, src in (
                (const[:, :], table),
                (rows_b[V_C:V_C + KT, :], c.rearrange("b (k p) -> (b k) p", p=P)),
                (rows_b[V_CC:V_CC + KT, :], c_ctx.rearrange("(k p) -> k p", p=P)),
                (rows_b[V_N1:V_N1 + DEPTH * KT, :], norm1_g.rearrange("l (k p) -> (l k) p", p=P)),
                (rows_b[V_N2:V_N2 + DEPTH * KT, :], norm2_g.rearrange("l (k p) -> (l k) p", p=P)),
                (rows_b[V_GC:V_GC + DEPTH * CT, :], out_norm_conv_g.rearrange("l (k p) -> (l k) p", p=P)),
                (rows_b[V_GA:V_GA + DEPTH * CT, :], out_norm_attn_g.rearrange("l (k p) -> (l k) p", p=P)),
                (rows_b[V_CW:V_CW + DEPTH * 3 * CT, :], conv_w.rearrange("l t (k p) -> (l t k) p", p=P)),
                (rows_b[V_QG:V_QG + DEPTH, 0:HD], q_norm_g),
                (rows_b[V_QG:V_QG + DEPTH, HD:P], q_norm_g),
                (rows_b[V_KG:V_KG + DEPTH, 0:HD], k_norm_g),
                (rows_b[V_KG:V_KG + DEPTH, HD:P], k_norm_g),
                (rows_a[0:DEPTH * GROUPS * KT, :], b_ada.rearrange("l (k p) -> (l k) p", p=P)),
                (sink_row[0:1, :], attn_sink.rearrange("(a l) h -> a (l h)", a=1)),
                (router[:, :, :], moe_router[0].rearrange("(k p) e -> p k e", p=P)),
            ):
                sp.dma_start(dst, src).then_inc(sem("params_in"), 16)
            for b in range(2):
                sp.dma_start(xin[:, b, :], x[0].rearrange("(b p) d -> b p d", p=P)[b]).then_inc(sem("x_in"), 16)
                sp.dma_start(xin[:, 2 + b, :], ctx[0].rearrange("(b p) d -> b p d", p=P)[b]).then_inc(
                    sem("x_in"), 16)
            for k in range(KT):
                ada_load(sp, 0, k)
            n = first_chunk[0, "in"]
            load(sp, w_in_src(0, in_col(0)), n)
            load(sp, w_in_src(0, in_col(1)), n + 1)
            ada_load(sp, 1, 0)
            load(sp, w_in_src(0, in_col(2)), n + 2)
            ada_load(sp, 1, 1)
            load(sp, w_in_src(0, in_col(3)), n + 3)
            for j in range(3, IN_CH):
                if j + 1 < IN_CH:
                    load(sp, w_in_src(0, in_col(j + 1)), n + j + 1)
                else:
                    load(sp, w_out_src(0, 0), first_chunk[0, "out"])
                ada_load(sp, 1, j - 1)
            for j in range(1, OUT_CH):
                load(sp, w_out_src(0, j), first_chunk[0, "out"] + j)
            for part, (c0, c1) in enumerate(PARTS):
                n = first_chunk[0, f"up{part}"]
                load(sp, up_src(ffn_w1, c0), n)
                with sp.Fori(0, c1 - c0 - 1) as i:
                    load(sp, up_src(ffn_w3, c0 + i), n + 1, i)
                    load(sp, up_src(ffn_w1, c0 + 1 + i), n + 2, i)
                    if part == 0:
                        ada_load(sp, 2, 0, i)
                load(sp, up_src(ffn_w3, c1 - 1), n + 2 * (c1 - c0) - 1)
                n = first_chunk[0, f"down{part}"]
                load(sp, down_src(c0), n, cols=2)
                if part == 0:
                    ada_load(sp, 2, c1 - c0 - 1)
                for j in range(1, c1 - c0):
                    load(sp, down_src(c0 + j), n + j, cols=2)
                    if part == 0 and j <= 2:
                        ada_load(sp, 2, c1 - c0 - 1 + j)
            n = first_chunk[1, "in"]
            for j in range(IN_CH):
                load(sp, w_in_src(1, in_col(j)), n + j)
            for j in range(OUT_CH):
                load(sp, w_out_src(1, j), first_chunk[1, "out"] + j)

            pass_sp(sp, 0)
            with sp.If(overflow(sp)):
                sp.wait_ge(sem("yacc"), 4 * EXPERTS + 4)
                pass_sp(sp, 1)
            for b in range(2):
                sp.wait_ge(sem("result"), b + 1)
                sp.dma_start(out[0].rearrange("(b p) d -> b p d", p=P)[b], ytok[:, b, :]).then_inc(sem("stored"), 16)
            sp.wait_ge(sem("stored"), 32)

        @block.tensor
        def _(pe):
            pe.wait_ge(sem("params_in"), 15 * 16)
            pe.transpose(ps[:, 0, 0:V_ROWS], rows_b[0:V_ROWS, :], const[0:V_ROWS, C_ID:C_ID + V_ROWS])
            n = DEPTH * GROUPS * KT
            pe.transpose(ps[:, 0, P:P + n], rows_a[0:n, :], const[0:n, C_ID:C_ID + n])
            pe.matmul(ps[:, 0, 2 * P:2 * P + DEPTH * HEADS], const[0:1, C_ONES:C_ONES + P], sink_row[0:1, :],
                      start=True, stop=True).then_inc(sem("params_ps"), 1)
            pe.wait_ge(sem("x_in"), 64)
            pe.wait_ge(sem("params_out"), 3)
            for k in range(KT):
                for b in range(NBLK):
                    last = pe.transpose(ps[:, k, b * P:(b + 1) * P], xin[:, b, k * P:(k + 1) * P], ident)
                last.then_inc(sem("x_ps"), 1)
            pe.wait_ge(sem("h_loaded"), KT)
            norm_pe(pe, (0, 0))
            mod_sum(pe, 0, 6)
            for layer in range(DEPTH):
                w = width(layer)
                n = first_chunk[layer, "in"]
                pe.wait_ge(sem("xl"), 2 * KT * (2 * layer + 1))
                for j in range(3):
                    if j >= 2:
                        pe.wait_ge(sem(f"z{layer}"), j - 1)
                    gemm_chunk(pe, n + j, 0, TOK if j == 2 else w)
                with pe.Fori(0, (IN_CH - 3) // 2) as i:
                    for q in range(2):
                        pe.wait_ge(sem(f"z{layer}"), 2 * i + q + 2)
                        gemm_chunk(pe, n + 3 + q, i, w)
                if layer == 0:
                    mod_sum(pe, 1, 6)
                    pe.wait_ge(sem("mod_out"), 2)
                pe.wait_ge(sem(f"z{layer}"), IN_CH)
                qk_pe(pe, layer)
                att_pe(pe, layer)
                merge_pe(pe, layer)
                pe.wait_ge(sem(f"yl{layer}"), yl_count(layer))
                n = first_chunk[layer, "out"]
                for j in range(OUT_CH):
                    if j >= 2:
                        pe.wait_ge(sem(f"h_mixed{layer}"), j - 1)
                    gemm_chunk(pe, n + j, 0, w)
                norm_pe(pe, (layer, 1))
                if layer == 0:
                    pe.wait_ge(sem("xl"), 4 * KT)
                    for part, (c0, c1) in enumerate(PARTS):
                        n = first_chunk[0, f"up{part}"]

                        def pair(i, first):
                            n1 = n if first else n + 2
                            if c0 or not first:
                                pe.wait_ge(sem("silu"), c0 + (0 if first else 1) + i)
                            if c0 and first:
                                pe.wait_ge(sem("h_ffn"), 4)
                            gemm_chunk(pe, n1, i, TOK)
                            if c0 or not first:
                                pe.wait_ge(sem("glu"), c0 + (0 if first else 1) + i)
                            gemm_chunk(pe, n1 + 1, i, TOK)

                        pair(0, True)
                        with pe.Fori(0, c1 - c0 - 1) as i:
                            pair(i, False)
                        n = first_chunk[0, f"down{part}"]
                        pe.wait_ge(sem("glu"), c1)
                        if part:
                            pe.wait_ge(sem("h_ffn"), KT)
                        for j in range(c1 - c0):
                            s = (n + j) % 2
                            pe.wait_ge(sem("lo_done"), n + j + 1)
                            pe.wait_ge(sem("hid"), c0 + j + 1)
                            for r in range(2):
                                for m in range(KT):
                                    a = r * D + m * P
                                    last = product(pe, (wh[:, s, a:a + P], wl[:, s, a:a + P]),
                                                   (hid_h[:, 2 * j + r, :], hid_l[:, 2 * j + r, :]), ps[:, m, :],
                                                   j == 0 and r == 0, j == c1 - c0 - 1 and r == 1)
                            last.then_inc(sem("gemm_done"), 1)
                    pe.wait_ge(sem("h_ffn"), 2 * KT)
                    mod_sum(pe, 2, 6)
                    norm_pe(pe, (1, 0))
            route_pe(pe)
            pass_pe(pe, 0)
            with pe.If(overflow(pe)):
                pe.wait_ge(sem("yacc"), 4 * EXPERTS + 4)
                pass_pe(pe, 1)

        @block.scalar
        def _(act):
            act.wait_ge(sem("params_ps"), 1)
            act.activation(cs[:, :, :].rearrange("p s k -> p (s k)"), ps[:, 0, V_C:V_C + 2 * KT], ACT.Silu).then_inc(
                sem("cs"), 1)
            for k in range(0, KT, 2):
                act.wait_ge(sem("x_ps"), k + 1)
                act.activation(h[:, k, :], ps[:, k, :], ACT.Copy).then_inc(sem("h_loaded"), 1)
            norm_act(act, (0, 0))
            split_hi(act, 0)
            for layer in range(DEPTH):
                w = width(layer)
                n = first_chunk[layer, "in"]

                def z_out(act, n0, i, col, w):
                    act.wait_ge(sem("gemm_done"), n0 + 1 + 2 * i)
                    b = 2 * (n0 % 2)
                    act.activation(z[:, bass.ts(col, 2), 0:w], ps[:, b:b + 2, 0:w], ACT.Copy).then_inc(
                        sem(f"z{layer}"), 1)

                for j in range(3):
                    split_hi(act, n + j + 1)
                    z_out(act, n + j, 0, in_col(j), TOK if j == 2 else w)
                with act.Fori(0, (IN_CH - 3) // 2) as i:
                    for q in range(2):
                        split_hi(act, n + 4 + q, i)
                        z_out(act, n + 3 + q, i, 2 * i + q, w)
                qk_act(act, layer)
                att_act(act, layer)
                merge_act(act, layer)
                n = first_chunk[layer, "out"]
                for j in range(OUT_CH - 1 if layer else OUT_CH):
                    split_hi(act, n + j + 1)
                norm_act(act, (layer, 1))
                if layer == 0:
                    for part, (c0, c1) in enumerate(PARTS):
                        n = first_chunk[0, f"up{part}"]

                        def pair(i, n0, p):
                            split_hi(act, n0 + 1, i)
                            act.wait_ge(sem("gemm_done"), n0 + 1 + 2 * i)
                            if p:
                                act.wait_ge(sem("hid"), p + i)
                            b1 = 2 * (n0 % 2)
                            act.activation(tmp[:, :, :], ps[:, b1:b1 + 2, :], ACT.Silu).then_inc(sem("silu"), 1)
                            split_hi(act, n0 + 2, i)
                            act.wait_ge(sem("glu"), p + 1 + i)
                            act.activation(hid_h[:, bass.ts(p - c0 + i, 2), :], tmp[:, :, :], ACT.Copy).then_inc(
                                sem("hid_h"), 1)

                        pair(0, n, c0)
                        with act.Fori(0, c1 - c0 - 1) as i:
                            pair(i, n + 2, c0 + 1)
                        n = first_chunk[0, f"down{part}"]
                        for j in range(c1 - c0):
                            split_hi(act, n + j + 1)
                    norm_act(act, (1, 0))
            route_act(act)
            pass_act(act, 0)
            with act.If(overflow(act)):
                act.wait_ge(sem("yacc"), 4 * EXPERTS + 4)
                pass_act(act, 1)

        @block.vector
        def _(dve):
            dve.wait_ge(sem("params_ps"), 1)
            dve.wait_ge(sem("cs"), 1)
            dve.tensor_copy(vec[:, :], ps[:, 0, 0:V_ROWS]).then_inc(sem("params_out"), 1)
            dve.tensor_copy(b_ada_t[:, :], ps[:, 0, P:P + DEPTH * GROUPS * KT]).then_inc(sem("params_out"), 1)
            dve.tensor_scalar(nsink[:, :], ps[:, 0, 2 * P:2 * P + DEPTH * HEADS], -1.0, None, ALU.mult).then_inc(
                sem("params_out"), 1)
            dve.tensor_copy(ident_b[:, :], ident).then_inc(sem("masks"), 1)
            dve.tensor_copy(mask_b[:, :, :].rearrange("p a b -> p (a b)"), const[:, C_MASK:C_MASK + 2 * P]).then_inc(
                sem("masks"), 1)
            for k in range(1, KT, 2):
                dve.wait_ge(sem("x_ps"), k + 1)
                dve.tensor_copy(h[:, k, :], ps[:, k, :]).then_inc(sem("h_loaded"), 1)
            for k in range(KT):
                ada_step(dve, 0, k)
            mod_out(dve, 0, 6)
            norm_dve(dve, (0, 0))
            split_lo(dve, 0)
            for layer in range(DEPTH):
                w = width(layer)
                n = first_chunk[layer, "in"]
                for j in range(3):
                    split_lo(dve, n + j + 1)
                    if layer == 0 and j < 2:
                        ada_step(dve, 1, j)
                if layer == 0:
                    for j in range(3, IN_CH):
                        split_lo(dve, n + j + 1)
                        ada_step(dve, 1, j - 1)
                    mod_out(dve, 1, 6)
                else:
                    for j in range(3, IN_CH):
                        split_lo(dve, n + j + 1)
                dve.wait_ge(sem(f"z{layer}"), IN_CH)
                qk_dve(dve, layer)
                att_dve(dve, layer)
                merge_dve(dve, layer)
                n = first_chunk[layer, "out"]
                for j in range(OUT_CH):
                    if j < OUT_CH - 1 or layer == 0:
                        split_lo(dve, n + j + 1)
                    dve.wait_ge(sem("gemm_done"), n + j + 1)
                    for mt in range(2):
                        m = 2 * j + mt
                        for s in range(w // SEQ):
                            last = dve.scalar_tensor_tensor(
                                h[:, m, span(s)], ps[:, 2 * ((n + j) % 2) + mt, span(s)], modc(layer, s, G1, m),
                                h[:, m, span(s)], ALU.mult, ALU.add)
                    last.then_inc(sem(f"h_mixed{layer}"), 1)
                norm_dve(dve, (layer, 1))
                if layer == 0:
                    for part, (c0, c1) in enumerate(PARTS):
                        n = first_chunk[0, f"up{part}"]

                        def pair(i, n0, p):
                            split_lo(dve, n0 + 1, i)
                            split_lo(dve, n0 + 2, i)
                            if part == 0:
                                ada_step(dve, 2, p, i)
                            dve.wait_ge(sem("silu"), p + 1 + i)
                            dve.wait_ge(sem("gemm_done"), n0 + 2 + 2 * i)
                            b3 = 2 * ((n0 + 1) % 2)
                            dve.tensor_tensor(tmp[:, :, :], tmp[:, :, :], ps[:, b3:b3 + 2, :], ALU.mult).then_inc(
                                sem("glu"), 1)
                            dve.wait_ge(sem("hid_h"), p + 1 + i)
                            dve.tensor_tensor(hid_l[:, bass.ts(p - c0 + i, 2), :], tmp[:, :, :],
                                              hid_h[:, bass.ts(p - c0 + i, 2), :], ALU.subtract).then_inc(
                                sem("hid"), 1)

                        pair(0, n, c0)
                        with dve.Fori(0, c1 - c0 - 1) as i:
                            pair(i, n + 2, c0 + 1)
                        n = first_chunk[0, f"down{part}"]
                        for j in range(c1 - c0):
                            split_lo(dve, n + j + 1)
                            if part == 0 and j < 2:
                                ada_step(dve, 2, c1 - c0 + j)
                        dve.wait_ge(sem("gemm_done"), n + c1 - c0)
                        for m in range(KT):
                            for s in range(2):
                                last = dve.scalar_tensor_tensor(h[:, m, span(s)], ps[:, m, span(s)],
                                                                modc(0, s, G2, m), h[:, m, span(s)], ALU.mult,
                                                                ALU.add)
                            last.then_inc(sem("h_ffn"), 1)
                    mod_out(dve, 2, 6)
                    norm_dve(dve, (1, 0))
            route_dve(dve)
            dve.wait_ge(sem("yacc"), 4)
            pass_dve(dve, 0)
            with dve.If(overflow(dve)):
                dve.wait_ge(sem("yacc"), 4 * EXPERTS + 4)
                dve.tensor_scalar(route[:, R_POS, :, :], route[:, R_POS, :, :], -float(P), None,
                                  ALU.add).then_inc(sem("shifted"), 1)
                dve.wait_ge(sem("shifted"), 1)
                pass_dve(dve, 1)
                dve.wait_ge(sem("yacc"), 8 * EXPERTS + 4)
            dve.wait_ge(sem("htok"), 2)
            dve.wait_ge(sem("yacc"), 4 * EXPERTS + 4)
            for b in range(2):
                dve.tensor_tensor(ytok[:, b, :], ytok[:, b, :], g2b[:, :], ALU.mult).then_inc(sem("gated"), 1)
            for b in range(2):
                dve.wait_ge(sem("gated"), b + 1)
                dve.tensor_tensor(ytok[:, b, :], ytok[:, b, :], htok[:, b, :], ALU.add).then_inc(sem("result"), 1)

        @block.gpsimd
        def _(pool):
            pool.wait_ge(sem("h_mixed1"), OUT_CH)
            for i in range(4):
                pool.memset(ytok[:, i // 2, (i % 2) * 512:(i % 2 + 1) * 512], 0.0).then_inc(sem("yacc"), 1)


_INS = ["x", "c", "ctx", "c_ctx", "w_ada", "b_ada", "norm1_g", "norm2_g", "w_in", "conv_w", "q_norm_g", "k_norm_g",
        "attn_sink", "out_norm_conv_g", "out_norm_attn_g", "w_out", "ffn_w1", "ffn_w3", "ffn_w2",
        "moe_router", "moe_w1", "moe_w3", "moe_w2"]
_OUTS = [((1, SEQ, D), "float32")]


def kernel(**inputs):
    import numpy as _np
    import concourse.bacc as _bacc
    from concourse import mybir as _mybir
    from concourse.bass_utils import run_bass_kernel_spmd as _run

    nc = _bacc.Bacc("TRN2", target_bir_lowering=False, num_devices=1)
    arrays, args = {}, []
    for name in _INS:
        a = _np.ascontiguousarray(inputs[name])
        arrays[f"in_{name}_dram"] = a
        args.append(nc.dram_tensor(f"in_{name}_dram", a.shape, _mybir.dt.from_np(a.dtype), kind="ExternalInput").ap())
    table = constant_table(_np)
    arrays["table_dram"] = table
    args.append(nc.dram_tensor("table_dram", table.shape, _mybir.dt.from_np(table.dtype), kind="ExternalInput").ap())
    for i, (shape, dtype) in enumerate(_OUTS):
        dt = _mybir.dt.from_np(_np.dtype(dtype))
        args.append(nc.dram_tensor(f"out_{i}_dram", shape, dt, kind="ExternalOutput").ap())
    hybrid_backbone(nc, *args)
    r = _run(nc, [arrays], core_ids=[0])
    got = tuple(r.results[0][f"out_{i}_dram"] for i in range(len(_OUTS)))
    return got[0]
```

```python
import math
from contextlib import ExitStack

import concourse.bass as bass
from concourse import mybir

F32 = mybir.dt.float32
F32R = mybir.dt.float32r
BF16 = mybir.dt.bfloat16
U32 = mybir.dt.uint32
I32 = mybir.dt.int32
ALU = mybir.AluOpType
ACT = mybir.ActivationFunctionType
AX = mybir.AxisListType

P = 128
D = 1024
KT = D // P
SEQ, CTX = 256, 256
TOK = SEQ + CTX
NBLK = TOK // P
DEPTH = 2
D_CONV = D // 2
CT = D_CONV // P
HEADS, N_KV, HD = 8, 2, 64
D_IN = 3 * D_CONV + 512 + 2 * N_KV * HD
ZT = D_IN // P
D_FF = 2816
EXPERTS, F_EXP = 8, 1408
EPS = 1e-6
SCALE = HD ** -0.5
CW = 256
SLOT = KT * CW
IN_CH, OUT_CH = D_IN // CW, D // CW
FF_CH = D_FF // CW
PART = (FF_CH + 1) // 2
FT = F_EXP // P
MC = F_EXP // 8
MSLOT = 2 * MC * KT
MCH = 8 + D // CW
MRING = 6
assert MSLOT == FT * CW
GROUPS = 6
SH1, SC1, G1, SH2, SC2, G2 = range(GROUPS)

V_N1, V_N2 = 0, DEPTH * KT
V_GC = V_N2 + DEPTH * KT
V_GA = V_GC + DEPTH * CT
V_CW = V_GA + DEPTH * CT
V_C = V_CW + DEPTH * 3 * CT
V_CC = V_C + KT
V_QG = V_CC + KT
V_KG = V_QG + DEPTH
V_ROWS = V_KG + DEPTH

C_COS, C_SIN = 0, SEQ
C_ROT = 2 * SEQ
C_DUP = C_ROT + P
C_BONES = C_DUP + 4 * P
C_ID = C_BONES + P
C_ONES = C_ID + P
C_TRI = C_ONES + P
C_MASK = C_TRI + P
C_IOTA = C_MASK + 2 * P
C_SLIDE = C_IOTA + P
C_ALL = C_SLIDE + 31


def constant_table(np):
    n_freq = HD // 4
    inv = (np.float32(10000.0) ** (-np.arange(n_freq, dtype=np.float32) / np.float32(n_freq))).astype(np.float32)
    tok = np.arange(SEQ)
    row, col = (tok // 64).astype(np.float32), (tok % 64).astype(np.float32)
    ar, ac = row[:, None] * inv, col[:, None] * inv
    ang = np.concatenate([ar, ar, ac, ac], axis=-1).astype(np.float32).T
    t = np.zeros((P, C_ALL), np.float32)
    t[:, C_COS:C_COS + SEQ] = np.tile(np.cos(ang), (2, 1))
    t[:, C_SIN:C_SIN + SEQ] = np.tile(np.sin(ang), (2, 1))
    for p in range(P):
        if p % 32 < 16:
            t[p + 16, C_ROT + p] = -1.0
        else:
            t[p - 16, C_ROT + p] = 1.0
        for g in range(2):
            t[HD * g + p % HD, C_DUP + (2 * g + p // HD) * P + p] = 1.0
        t[HD * (p // HD):HD * (p // HD + 1), C_BONES + p] = 1.0
        t[p, C_ID + p] = 1.0
        t[p, C_TRI + p + 1:C_TRI + P] = 1.0
    t[:, C_ONES:C_ONES + P] = 1.0
    q, k = np.arange(P)[:, None], np.arange(P)[None, :]
    t[:, C_MASK:C_MASK + P] = np.where(k <= q, 0.0, -1e30)
    t[:, C_MASK + P:C_MASK + 2 * P] = np.where(k >= q, 0.0, -1e30)
    t[:, C_IOTA:C_IOTA + P] = np.arange(P, dtype=np.float32)
    t[:, C_SLIDE + 15] = 1.0
    return t


def stages():
    out, n = [], 0
    for layer in range(DEPTH):
        plan = [("in", IN_CH), ("out", OUT_CH)]
        if layer == 0:
            plan += [("up0", 2 * PART), ("down0", PART), ("up1", 2 * (FF_CH - PART)), ("down1", FF_CH - PART)]
        for name, count in plan:
            out.append((layer, name, n, count))
            n += count
    return out, n


def hybrid_backbone(nc, x, c, ctx, c_ctx, w_ada, b_ada, norm1_g, norm2_g, w_in, conv_w, q_norm_g, k_norm_g,
                    attn_sink, out_norm_conv_g, out_norm_attn_g, w_out, ffn_w1, ffn_w3, ffn_w2,
                    moe_router, moe_w1, moe_w3, moe_w2, table, out):
    STAGES, CHUNKS = stages()
    first_chunk = {(layer, name): n for layer, name, n, _ in STAGES}

    with ExitStack() as stack:
        sems = {}

        def sem(name):
            if name not in sems:
                sems[name] = stack.enter_context(nc.semaphore(name))
            return sems[name]

        base = -(-nc.sbuf_base // 64) * 64

        def at(name, offset, shape, dt=F32):
            size = -(-math.prod(shape[1:]) * (2 if dt == BF16 else 4) // 64) * 64
            assert base + offset + size <= nc.sbuf_usable_end, (name, offset + size)
            return nc.alloc_sbuf_tensor_at(name, shape, dt, offset=base + offset), offset + size

        const, o = at("const", 0, [P, C_ALL])
        ident_b, o = at("ident_b", o, [P, P], BF16)
        mask_b, o = at("mask_b", o, [P, 2, P], BF16)
        vec, o = at("vec", o, [P, V_ROWS])
        b_ada_t, o = at("b_ada_t", o, [P, DEPTH * GROUPS * KT])
        cs, o = at("cs", o, [P, KT, 2])
        mod, o = at("mod", o, [P, DEPTH, 2, GROUPS * KT])
        gain, o = at("gain", o, [P, DEPTH, 2, 2, KT])
        nsink, o = at("nsink", o, [P, DEPTH * HEADS])
        router, o = at("router", o, [P, KT, EXPERTS])
        route, o = at("route", o, [P, 12, 2, EXPERTS])
        top_i, o = at("top_i", o, [P, 2, EXPERTS], U32)
        most, o = at("most", o, [P, 1], I32)
        h, o = at("h", o, [P, KT, TOK])
        ZONE = o
        xh, o = at("xh", o, [P, KT, TOK], F32R)
        xl, o = at("xl", o, [P, KT, TOK], F32R)
        Z = o
        z, o = at("z", Z, [P, ZT, TOK])
        VAR = o
        var, o = at("var", o, [P, 2, TOK])
        std, o = at("std", o, [P, 2, TOK])
        rstd, o = at("rstd", o, [P, 2, TOK])
        xin, o2 = at("xin", Z, [P, NBLK, D])
        rows0, o2 = at("rows0", o2, [2, 2 * D])
        hid_h, o2 = at("hid_h", Z, [P, 2 * PART, TOK], F32R)
        hid_l, o2 = at("hid_l", o2, [P, 2 * PART, TOK], F32R)
        RAW = max(o, o2)
        raw, o = at("raw", RAW, [P, 2, SLOT])
        rows_a, o2 = at("rows_a", o, [P, P])
        rows_b, o2 = at("rows_b", o2, [P, P])
        sink_row, o2 = at("sink_row", o2, [P, DEPTH * HEADS])
        wh, o = at("wh", o, [P, 2, SLOT], F32R)
        wl, o = at("wl", o, [P, 2, SLOT], F32R)
        ada, o = at("ada", o, [P, 2, D])
        TMP = o
        tmp, o = at("tmp", o, [P, 2, TOK])
        tn, o = at("tn", o, [P, 2, SEQ])
        tmp4 = tmp[:, :, :].rearrange("p a (b t) -> p (a b) t", b=2)
        A = o
        acc, _ = at("acc", A, [P, 8, D])
        ada0 = [at("ada0_a", ZONE, [P, 4, 2 * D])[0], at("ada0_b", A, [P, 4, 2 * D])[0]]
        kd, o = at("kd", A, [P, 2, 2, TOK])
        vtok, o = at("vtok", o, [P, NBLK, P])
        acc_mix, rows_at = at("acc_mix", o, [P, 6, D])
        mod_row, _ = at("mod_row", rows_at, [16, TOK])
        pm, o = at("pm", o, [P, 2, TOK])
        pt, o = at("pt", o, [P, 2, TOK])
        otok, o = at("otok", o, [P, NBLK, D_CONV])
        NU = NBLK * HEADS
        mx, o = at("mx", o, [P, NU])
        negm, o = at("negm", o, [P, NU])
        rsum, o = at("rsum", o, [P, NU])
        esink, o = at("esink", o, [P, NU])
        rden, o = at("rden", o, [P, NU])
        osq, o = at("osq", o, [P, 3, NBLK])
        mwh, o = at("mwh", A, [P, 3, MSLOT], F32R)
        g2b, o = at("g2b", o, [P, D])
        mraw, o = at("mraw", ZONE, [P, MRING, MSLOT])
        mwl, _ = at("mwl", ZONE, [P, MRING, MSLOT], F32R)
        assert o <= VAR and Z <= ZONE + MRING // 2 * MSLOT * 4
        ye_h, o = at("ye_h", VAR, [P, D], F32R)
        ye_l, o = at("ye_l", o, [P, D], F32R)
        pick, o = at("pick", o, [P, 2, P])
        pick_r, o = at("pick_r", o, [P, 2, P], F32R)
        place, o = at("place", o, [P, SEQ], F32R)
        assert o <= RAW
        x2t_h, o = at("x2t_h", RAW, [P, 2, D], F32R)
        x2t_l, o = at("x2t_l", o, [P, 2, D], F32R)
        xg_h, o = at("xg_h", o, [P, KT, P], F32R)
        xg_l, o = at("xg_l", o, [P, KT, P], F32R)
        x2, _ = at("x2", o, [P, KT, SEQ])
        ht_h, _ = at("ht_h", o, [P, FT * P], F32R)
        htok, o = at("htok", o + KT * SEQ * 4, [P, 2, D])
        ytok, o = at("ytok", o, [P, 2, D])
        ht_l, o = at("ht_l", o, [P, FT * P], F32R)
        sg, o = at("sg", o, [P, 2, MC])
        assert o <= TMP
        hg, o = at("hg", TMP, [P, F_EXP])
        assert o <= A

        ps = stack.enter_context(nc.psum_tensor("ps", [P, 8, 512], F32))

        cos, sin = const[:, C_COS:C_COS + SEQ], const[:, C_SIN:C_SIN + SEQ]
        ident, ones = const[:, C_ID:C_ID + P], const[:, C_ONES:C_ONES + P]
        rot, bones = const[:, C_ROT:C_ROT + P], const[:, C_BONES:C_BONES + P]

        def width(layer):
            return TOK if layer == 0 else SEQ

        def modc(layer, stream, group, k):
            return mod[:, layer, stream, group * KT + k:group * KT + k + 1]

        def vcol(v):
            return vec[:, v:v + 1]

        def span(stream):
            return slice(stream * SEQ, (stream + 1) * SEQ)

        def arrived(eng, n0, i=0):
            eng.wait_ge(sem(f"raw_in{n0 % 2}"), 16 * (n0 // 2 + 1) + 16 * i)

        def split_hi(act, n0, i=0):
            s = n0 % 2
            arrived(act, n0, i)
            if n0 >= 2:
                act.wait_ge(sem("gemm_done"), n0 - 1 + 2 * i)
            act.activation(wh[:, s, :], raw[:, s, :], ACT.Copy).then_inc(sem("hi_done"), 1)

        def split_lo(dve, n0, i=0):
            s = n0 % 2
            arrived(dve, n0, i)
            dve.wait_ge(sem("hi_done"), n0 + 1 + 2 * i)
            dve.tensor_tensor(wl[:, s, :], raw[:, s, :], wh[:, s, :], ALU.subtract).then_inc(sem("lo_done"), 1)

        def load(sp, src, n0, i=0, cols=None):
            s = n0 % 2
            if n0 >= 2:
                sp.wait_ge(sem("lo_done"), n0 - 1 + 2 * i)
            sp.dma_start(raw[:, s, :].rearrange("p (k n) -> p k n", k=cols or KT), src).then_inc(
                sem(f"raw_in{s}"), 16)

        def w_in_src(layer, col):
            return w_in[layer].rearrange("(k p) n -> p k n", p=P)[:, :, bass.ts(col, CW)]

        def w_out_src(layer, col):
            return w_out[layer].rearrange("(k p) n -> p k n", p=P)[:, :, bass.ts(col, CW)]

        def up_src(w, col):
            return w[0].rearrange("(k p) n -> p k n", p=P)[:, :, bass.ts(col, CW)]

        def down_src(chunk):
            return ffn_w2[0].rearrange("(c p) n -> p c n", p=P)[:, bass.ts(chunk, 2), :]

        def in_col(j):
            return (2 * 3 + j) % IN_CH

        def product(pe, lo_hi, rhs, out_ap, first, last):
            (lh, ll), (rh, rl) = lo_hi, rhs
            pe.matmul(out_ap, lh, rh, start=first, stop=False)
            pe.matmul(out_ap, lh, rl, start=False, stop=False)
            return pe.matmul(out_ap, ll, rh, start=False, stop=last)

        def gemm_chunk(pe, n0, i, w):
            s = n0 % 2
            pe.wait_ge(sem("lo_done"), n0 + 1 + 2 * i)
            for mt in range(2):
                for k in range(KT):
                    a = k * CW + mt * P
                    last = product(pe, (wh[:, s, a:a + P], wl[:, s, a:a + P]), (xh[:, k, 0:w], xl[:, k, 0:w]),
                                   ps[:, 2 * s + mt, 0:w], k == 0, k == KT - 1)
            last.then_inc(sem("gemm_done"), 1)

        def gemm_first(pe, n0, w, ready):
            s = n0 % 2
            pe.wait_ge(sem("lo_done"), n0 + 1)
            for k in range(KT):
                pe.wait_ge(*ready(k))
                for mt in range(2):
                    a = k * CW + mt * P
                    last = product(pe, (wh[:, s, a:a + P], wl[:, s, a:a + P]), (xh[:, k, 0:w], xl[:, k, 0:w]),
                                   ps[:, 2 * s + mt, 0:w], k == 0, k == KT - 1)
            last.then_inc(sem("gemm_done"), 1)

        def normed(layer, norm):
            return lambda k: (sem("xl"), 2 * KT * (2 * layer + norm) + 2 * k + 2)

        ADA = [
            dict(layer=0, groups=[SH1, SC1], both=2),
            dict(layer=0, groups=[G1, SH2, SC2], both=3),
            dict(layer=0, groups=[G2], both=1),
            dict(layer=1, groups=[SH1, SC1, G1, SH2, SC2, G2], both=2),
        ]
        ada_base = [0, 0]
        for ph in ADA[1:]:
            ada_base.append(ada_base[-1] + KT * len(ph["groups"]))

        def sums(phase):
            ph = ADA[phase]
            return [(s, gi) for s in range(2) for gi in range(len(ph["groups"])) if s == 0 or gi < ph["both"]]

        def acc_at(phase, stream, gi):
            return (acc if phase == 3 else acc_mix)[:, sums(phase).index((stream, gi)), :]

        def ada_load(sp, phase, k0, i=0):
            ph = ADA[phase]
            n = len(ph["groups"])
            for gi, g in enumerate(ph["groups"]):
                t = ada_base[phase] + k0 * n + gi
                if t >= 2:
                    sp.wait_ge(sem("ada_used"), t - 1 + n * i)
                src = w_ada[ph["layer"]][:, g * D:(g + 1) * D]
                src = src[bass.ts(k0 + i, P), :]
                sp.dma_start(ada[:, t % 2, :], src).then_inc(sem(f"ada_in{t % 2}"), 16)

        def ada_step(dve, phase, k0, i=0):
            ph = ADA[phase]
            n = len(ph["groups"])
            for gi, g in enumerate(ph["groups"]):
                t = ada_base[phase] + k0 * n + gi
                dve.wait_ge(sem(f"ada_in{t % 2}"), 16 * (t // 2 + 1) + 16 * (n // 2) * i)
                if k0 > 0:
                    dve.wait_ge(sem("ada_used"), t - n + 1 + n * i)
                for s in range(2 if gi < ph["both"] else 1):
                    a = acc_at(phase, s, gi)
                    scalar = cs[:, bass.ds(k0 + i, 1), s]
                    if k0 == 0:
                        last = dve.tensor_scalar(a, ada[:, t % 2, :], scalar, None, ALU.mult)
                    else:
                        last = dve.scalar_tensor_tensor(a, ada[:, t % 2, :], scalar, a, ALU.mult, ALU.add)
                last.then_inc(sem("ada_used"), 1)

        SUM_BANK, COL_BANK = 5, 6

        def ada0_pe(pe, k):
            if k % 2 == 0:
                pe.wait_ge(sem(f"ada0_in{k // 2}"), 32)
            for b in range(4):
                last = pe.matmul(ps[0:2, b, :], cs[:, k, :], ada0[k // 4][:, k % 4, b * 512:(b + 1) * 512],
                                 start=k == 0, stop=k == KT - 1)
            if k == KT - 1:
                last.then_inc(sem("mod_sum"), 1)

        def ada0_cols(pe):
            pe.wait_ge(sem("mod_row"), 1)
            for i in range(2 * KT):
                last = pe.transpose(ps[:, COL_BANK, 2 * i:2 * i + 2], rows0[0:2, i * P:(i + 1) * P], ident[0:2, 0:2])
            last.then_inc(sem("mod_col"), 1)

        def mod_rows(pe, phase):
            pe.wait_ge(sem("ada_used"), ada_base[phase + 1])
            n = 2 * len(sums(phase))
            for v, (s, gi) in enumerate(sums(phase)):
                for half in range(2):
                    a = C_SLIDE + 15 - (2 * v + half)
                    last = pe.matmul(ps[0:n, SUM_BANK, :], const[:, a:a + n],
                                     acc_at(phase, s, gi)[:, half * 512:(half + 1) * 512],
                                     start=v == 0 and half == 0, stop=2 * v + half == n - 1)
            last.then_inc(sem("mod_sum"), 1)

        def mod_row_act(act, phase):
            act.wait_ge(sem("mod_sum"), phase + 1)
            if phase == 0:
                act.activation(rows0[:, :], ps[0:2, 0:4, :].rearrange("p a b -> p (a b)"), ACT.Copy).then_inc(
                    sem("mod_row"), 1)
                return
            n = 2 * len(sums(phase))
            act.activation(mod_row[0:n, :], ps[0:n, SUM_BANK, :], ACT.Copy).then_inc(sem("mod_row"), 1)

        def mod_cols(pe, phase):
            pe.wait_ge(sem("mod_row"), phase + 1)
            n = 2 * len(sums(phase))
            for q in range(4):
                last = pe.transpose(ps[:, COL_BANK, 16 * q:16 * q + n], mod_row[0:n, q * P:(q + 1) * P],
                                    ident[0:n, 0:n])
            last.then_inc(sem("mod_col"), 1)

        def mod_out(dve, phase):
            ph = ADA[phase]
            layer = ph["layer"]
            dve.wait_ge(sem("mod_col"), phase + 1)
            g0, g1 = ph["groups"][0], ph["groups"][-1] + 1
            for s in range(2):
                e = g1 if s == 0 else ph["groups"][0] + ph["both"]
                dst = mod[:, layer, s, g0 * KT:e * KT]
                bias = b_ada_t[:, (layer * GROUPS + g0) * KT:(layer * GROUPS + e) * KT]
                if phase == 0:
                    src = ps[:, COL_BANK, 0:4 * KT].rearrange("p (i s) -> p s i", s=2)[:, s, :]
                else:
                    v = 2 * (g1 - g0) * s
                    src = ps[:, COL_BANK, 0:64].rearrange("p (q v) -> p v q", q=4)[:, v:v + 2 * (e - g0), :]
                    dst = dst.rearrange("p (v q) -> p v q", q=4)
                    bias = bias.rearrange("p (v q) -> p v q", q=4)
                last = dve.tensor_tensor(dst, src, bias, ALU.add)
            last.then_inc(sem("mod_out"), 1)
            dve.wait_ge(sem("mod_out"), phase + 1)
            for norm, scale, v in ((0, SC1, V_N1), (1, SC2, V_N2)):
                if scale not in ph["groups"]:
                    continue
                for s in range(1 if norm == 1 and layer == 1 else 2):
                    last = dve.scalar_tensor_tensor(
                        gain[:, layer, norm, s, :], mod[:, layer, s, scale * KT:(scale + 1) * KT], 1.0,
                        vec[:, v + layer * KT:v + (layer + 1) * KT], ALU.add, ALU.mult)
            if SC1 in ph["groups"] or SC2 in ph["groups"]:
                last.then_inc(sem("gain_out"), 1)

        NORM_BANK = 7
        norm_w = {(0, 0): TOK, (0, 1): TOK, (1, 0): TOK, (1, 1): SEQ}

        def h_ready(key, k):
            if key == (0, 0):
                return sem("h_loaded"), KT
            if key == (1, 0):
                return sem("h_ffn"), KT + k + 1
            return sem(f"h_mixed{key[0]}"), k // 2 + 1

        mods_at = {(0, 0): 1, (0, 1): 2, (1, 0): 3, (1, 1): 3}

        def norm_bank(key):
            return 0 if key == (1, 0) else NORM_BANK

        def norm_sq(act, key, k0=0, k1=KT):
            q, w = 2 * key[0] + key[1], norm_w[key]
            for k in range(k0, k1):
                act.wait_ge(*h_ready(key, k))
                if k >= 2:
                    act.wait_ge(sem("sq_used"), KT * q + k - 1)
                act.activation(tmp[:, k % 2, 0:w], h[:, k, 0:w], ACT.Square).then_inc(sem("sq"), 1)

        def norm_unit(key, u):
            return (u // 2, u % 2) if norm_w[key] == TOK else (u, 0)

        def norm_act(act, key):
            q, w = 2 * key[0] + key[1], norm_w[key]
            act.wait_ge(sem("var"), q + 1)
            act.activation(std[:, 0, 0:w], var[:, 0, 0:w], ACT.Sqrt).then_inc(sem("std"), 1)
            for u in range(KT * w // SEQ):
                k, s = norm_unit(key, u)
                act.wait_ge(sem("tn"), 2 * KT * q + u + 1)
                act.activation(x2[:, k, :] if key == (1, 1) else xh[:, k, span(s)], tmp4[:, u % 4, :], ACT.Identity,
                               bias=modc(key[0], s, 3 * key[1] + SH1, k)).then_inc(sem("xh"), 1)

        def norm_pe(pe, key, k0=0, k1=KT):
            q, w = 2 * key[0] + key[1], norm_w[key]
            for k in range(k0, k1):
                pe.wait_ge(sem("sq"), KT * q + k + 1)
                pe.matmul(ps[:, norm_bank(key), 0:w], ones, tmp[:, k % 2, 0:w], start=k == 0,
                          stop=k == KT - 1).then_inc(sem("sq_used"), 1)

        def norm_dve(dve, key):
            q, w = 2 * key[0] + key[1], norm_w[key]
            layer, norm = key
            dve.wait_ge(sem("sq_used"), KT * (q + 1))
            dve.tensor_scalar(var[:, 0, 0:w], ps[:, norm_bank(key), 0:w], 1.0 / D, EPS, ALU.mult, ALU.add).then_inc(
                sem("var"), 1)
            dve.wait_ge(sem("std"), q + 1)
            dve.reciprocal(rstd[:, 0, 0:w], std[:, 0, 0:w]).then_inc(sem("rstd"), 1)
            dve.wait_ge(sem("rstd"), q + 1)
            dve.wait_ge(sem("gain_out"), mods_at[key])
            units = KT * w // SEQ
            for u in range(units + 2):
                if u < units:
                    k, s = norm_unit(key, u)
                    if u >= 4:
                        dve.wait_ge(sem("xh" if key == (1, 1) else "xl"), 2 * KT * q + u - 3)
                    dve.scalar_tensor_tensor(tmp4[:, u % 4, :], h[:, k, span(s)], gain[:, layer, norm, s, k:k + 1],
                                             rstd[:, 0, span(s)], ALU.mult, ALU.mult).then_inc(sem("tn"), 1)
                if u >= 2 and key != (1, 1):
                    k, s = norm_unit(key, u - 2)
                    dve.wait_ge(sem("xh"), 2 * KT * q + u - 1)
                    dve.scalar_tensor_tensor(xl[:, k, span(s)], tmp4[:, (u - 2) % 4, :],
                                             modc(layer, s, 3 * norm + SH1, k), xh[:, k, span(s)],
                                             ALU.add, ALU.subtract).then_inc(sem("xl"), 1)

        QK = CT + 1

        def qk_w(layer, j):
            return TOK if j == QK - 1 else width(layer)

        QK_SS = {2: (0, 1), 3: (2, 3), 4: (4,)}
        QK_ROT = {3: (0, 1), 4: (2, 3), 5: (4,)}
        QK_SQ = {1: (0, 1), 2: (2, 3), 3: (4,)}
        KD_AT, VT_AT = 6, 7

        def qk_act(act, layer, c):
            for j in QK_SS.get(c, ()):
                w = qk_w(layer, j)
                act.wait_ge(sem("qk_var"), QK * layer + j + 1)
                act.activation(std[:, j % 2, 0:w], var[:, j % 2, 0:w], ACT.Sqrt).then_inc(sem("qk_std"), 1)
            for j in QK_SQ.get(c, ()):
                w = qk_w(layer, j)
                act.wait_ge(sem(f"z{layer}"), j // 2 + 1)
                if j >= 2:
                    act.wait_ge(sem("qk_ss"), QK * layer + j - 1)
                act.activation(tmp[:, j % 2, 0:w], z[:, 12 + j, 0:w], ACT.Square).then_inc(sem("qk_sq"), 1)
            if c == KD_AT:
                for i in range(4):
                    act.wait_ge(sem(f"kd_ps{layer}"), i + 1)
                    act.activation(kd[:, i // 2, i % 2, :], ps[:, 4 + i, :], ACT.Copy).then_inc(sem(f"kd{layer}"), 1)

        def qk_pe(pe, layer, c):
            for i in QK_ROT.get(c, ()):
                pe.wait_ge(sem("qk_hat"), QK * layer + i + 1)
                if i >= 2:
                    pe.wait_ge(sem("qk_rs"), QK * layer + i - 1)
                pe.matmul(ps[:, 4 + i % 2, 0:SEQ], rot, z[:, 12 + i, 0:SEQ], start=True, stop=True).then_inc(
                    sem("qk_rot"), 1)
            for j in QK_SS.get(c, ()):
                w = qk_w(layer, j)
                pe.wait_ge(sem("qk_sq"), QK * layer + j + 1)
                if j >= 2:
                    pe.wait_ge(sem("qk_var"), QK * layer + j - 1)
                pe.matmul(ps[:, 6 + j % 2, 0:w], bones, tmp[:, j % 2, 0:w], start=True, stop=True).then_inc(
                    sem("qk_ss"), 1)
            if c == KD_AT:
                pe.wait_ge(sem("qk_done"), QK * layer + QK)
                for i in range(4):
                    pe.matmul(ps[:, 4 + i, :], const[:, C_DUP + i * P:C_DUP + (i + 1) * P], z[:, 16, :],
                              start=True, stop=True).then_inc(sem(f"kd_ps{layer}"), 1)
            if c == VT_AT:
                pe.wait_ge(sem(f"kd{layer}"), 3)
                for b in range(NBLK):
                    last = pe.transpose(ps[:, 6, b * P:(b + 1) * P], z[:, 17, b * P:(b + 1) * P], ident)
                last.then_inc(sem(f"vt_ps{layer}"), 1)

        def qk_dve(dve, layer, c):
            for j in QK_ROT.get(c, ()):
                qk_turn(dve, layer, j)
            for j in QK_SS.get(c, ()):
                w = qk_w(layer, j)
                dve.wait_ge(sem("qk_ss"), QK * layer + j + 1)
                dve.tensor_scalar(var[:, j % 2, 0:w], ps[:, 6 + j % 2, 0:w], 1.0 / HD, EPS, ALU.mult,
                                  ALU.add).then_inc(sem("qk_var"), 1)
            for j in QK_SS.get(c, ()):
                qk_scale(dve, layer, j)
            if c == VT_AT:
                dve.wait_ge(sem(f"vt_ps{layer}"), 1)
                dve.tensor_copy(vtok[:, :, :].rearrange("p b c -> p (b c)"), ps[:, 6, :]).then_inc(
                    sem(f"vtok{layer}"), 1)

        def qk_scale(dve, layer, j):
            w = qk_w(layer, j)
            g = vcol((V_KG if j == QK - 1 else V_QG) + layer)
            dve.wait_ge(sem("qk_std"), QK * layer + j + 1)
            dve.reciprocal(rstd[:, j % 2, 0:w], std[:, j % 2, 0:w]).then_inc(sem("qk_rcp"), 1)
            dve.wait_ge(sem("qk_rcp"), QK * layer + j + 1)
            dve.scalar_tensor_tensor(z[:, 12 + j, 0:w], z[:, 12 + j, 0:w], g, rstd[:, j % 2, 0:w], ALU.mult,
                                     ALU.mult).then_inc(sem("qk_hat"), 1)

        def qk_turn(dve, layer, j):
            lat = z[:, 12 + j, 0:SEQ]
            dve.wait_ge(sem("qk_rot"), QK * layer + j + 1)
            dve.tensor_tensor(tn[:, j % 2, :], ps[:, 4 + j % 2, 0:SEQ], sin, ALU.mult).then_inc(
                sem("qk_rs"), 1)
            dve.tensor_tensor(lat, lat, cos, ALU.mult).then_inc(sem("qk_rc"), 1)
            dve.wait_ge(sem("qk_rc"), QK * layer + j + 1)
            dve.tensor_tensor(lat, lat, tn[:, j % 2, :], ALU.add).then_inc(sem("qk_done"), 1)

        def units(layer):
            return [(hd, b) for b in range(NBLK if layer == 0 else 2) for hd in range(HEADS)]

        def unit_keys(b):
            return (0, NBLK) if b < 2 else (2, NBLK)

        def att_pe(pe, layer):
            us = units(layer)
            pe.wait_ge(sem(f"kd{layer}"), 4)
            for u in range(len(us) + 2):
                if u < len(us):
                    hd, b = us[u]
                    k0, k1 = unit_keys(b)
                    if u >= 2:
                        pe.wait_ge(sem(f"p{layer}"), u - 1)
                    s = ps[:, u % 2, 0:(k1 - k0) * P]
                    last = pe.matmul(s, z[:, 12 + hd // 2, b * P:(b + 1) * P],
                                     kd[:, hd // (HEADS // N_KV), hd % 2, k0 * P:k1 * P], start=True, stop=True)
                    if b < 2:
                        m = P * (1 - b)
                        last = pe.matmul(ps[:, u % 2, m:m + P], ident_b[:, :], mask_b[:, b, :], start=False,
                                         stop=True, skip_group_check=True)
                    last.then_inc(sem(f"s{layer}"), 1)
                if 1 <= u <= len(us):
                    v = u - 1
                    k0, k1 = unit_keys(us[v][1])
                    pe.wait_ge(sem(f"p{layer}"), v + 1)
                    if v >= 2:
                        pe.wait_ge(sem(f"pt{layer}"), v - 1)
                    for i in range(k1 - k0):
                        last = pe.transpose(ps[:, 2 + v % 2, i * P:(i + 1) * P], pm[:, v % 2, i * P:(i + 1) * P],
                                            ident)
                    last.then_inc(sem(f"pt_ps{layer}"), 1)
                if u >= 2:
                    v = u - 2
                    hd, b = us[v]
                    g = hd // (HEADS // N_KV)
                    k0, k1 = unit_keys(b)
                    pe.wait_ge(sem(f"pt{layer}"), v + 1)
                    if v == 0:
                        pe.wait_ge(sem(f"vtok{layer}"), 1)
                    if v >= 2:
                        pe.wait_ge(sem(f"o{layer}"), v - 1)
                    for i in range(k1 - k0):
                        last = pe.matmul(ps[:, 4 + v % 2, 0:HD], pt[:, v % 2, i * P:(i + 1) * P],
                                         vtok[:, k0 + i, g * HD:(g + 1) * HD], start=i == 0, stop=i == k1 - k0 - 1)
                    last.then_inc(sem(f"o_ps{layer}"), 1)

        def att_act(act, layer):
            us = units(layer)
            for u in range(len(us) + 2):
                if u < len(us):
                    hd, b = us[u]
                    k0, k1 = unit_keys(b)
                    n = (k1 - k0) * P
                    act.wait_ge(sem(f"negm{layer}"), u + 1)
                    if u >= 2:
                        act.wait_ge(sem(f"pt_ps{layer}"), u - 1)
                    act.activation(pm[:, u % 2, 0:n], ps[:, u % 2, 0:n], ACT.Exp, bias=negm[:, u:u + 1], scale=SCALE,
                                   accum_out=rsum[:, u:u + 1]).then_inc(sem(f"p{layer}"), 1)
                    i = layer * HEADS + hd
                    act.activation(esink[:, u:u + 1], nsink[:, i:i + 1], ACT.Exp, bias=negm[:, u:u + 1],
                                   scale=-1.0).then_inc(sem(f"es{layer}"), 1)
                if u >= 2:
                    v = u - 2
                    hd, b = us[v]
                    act.wait_ge(sem(f"o_ps{layer}"), v + 1)
                    act.wait_ge(sem(f"rden{layer}"), v + 1)
                    act.activation(otok[:, b, hd * HD:(hd + 1) * HD], ps[:, 4 + v % 2, 0:HD], ACT.Copy,
                                   scale=rden[:, v:v + 1]).then_inc(sem(f"o{layer}"), 1)

        def att_dve(dve, layer):
            us = units(layer)
            for u in range(len(us) + 1):
                if u < len(us):
                    hd, b = us[u]
                    k0, k1 = unit_keys(b)
                    dve.wait_ge(sem(f"s{layer}"), u + 1)
                    dve.tensor_reduce(mx[:, u:u + 1], ps[:, u % 2, 0:(k1 - k0) * P], AX.X, ALU.max).then_inc(
                        sem(f"mx{layer}"), 1)
                    dve.wait_ge(sem(f"mx{layer}"), u + 1)
                    i = layer * HEADS + hd
                    dve.tensor_scalar(negm[:, u:u + 1], mx[:, u:u + 1], -SCALE, nsink[:, i:i + 1], ALU.mult,
                                      ALU.min).then_inc(sem(f"negm{layer}"), 1)
                if u >= 1:
                    v = u - 1
                    k0, k1 = unit_keys(us[v][1])
                    n = (k1 - k0) * P
                    dve.wait_ge(sem(f"es{layer}"), v + 1)
                    dve.tensor_tensor(rden[:, v:v + 1], rsum[:, v:v + 1], esink[:, v:v + 1], ALU.add).then_inc(
                        sem(f"den{layer}"), 1)
                    dve.wait_ge(sem(f"pt_ps{layer}"), v + 1)
                    if v >= 2:
                        dve.wait_ge(sem(f"o_ps{layer}"), v - 1)
                    dve.tensor_copy(pt[:, v % 2, 0:n], ps[:, 2 + v % 2, 0:n]).then_inc(sem(f"pt{layer}"), 1)
                    dve.wait_ge(sem(f"den{layer}"), v + 1)
                    dve.reciprocal(rden[:, v:v + 1], rden[:, v:v + 1]).then_inc(sem(f"rden{layer}"), 1)
                if u % 4 == 3 and u < 16:
                    conv_tile(dve, layer, u // 4)

        def conv_tile(dve, layer, t):
            w = width(layer)
            n = w // SEQ
            bg, u, y = z[:, t, 0:w], z[:, CT + t, 0:w], z[:, 2 * CT + t, 0:w]
            u3, y3 = u.rearrange("p (s t) -> p s t", s=n), y.rearrange("p (s t) -> p s t", s=n)
            tap = [vcol(V_CW + (layer * 3 + i) * CT + t) for i in range(3)]
            done = sem(f"cv{layer}")
            dve.tensor_tensor(u, u, y, ALU.mult).then_inc(done, 1)
            dve.wait_ge(done, 5 * t + 1)
            dve.tensor_scalar(y, u, tap[1], None, ALU.mult).then_inc(done, 1)
            dve.wait_ge(done, 5 * t + 2)
            dve.scalar_tensor_tensor(y3[:, :, 1:], u3[:, :, :-1], tap[0], y3[:, :, 1:], ALU.mult,
                                     ALU.add).then_inc(done, 1)
            dve.wait_ge(done, 5 * t + 3)
            dve.scalar_tensor_tensor(y3[:, :, :-1], u3[:, :, 1:], tap[2], y3[:, :, :-1], ALU.mult,
                                     ALU.add).then_inc(done, 1)
            dve.wait_ge(done, 5 * t + 4)
            dve.tensor_tensor(y, y, bg, ALU.mult).then_inc(done, 1)

        def merge_act(act, layer):
            w, nb = width(layer), width(layer) // P
            for b in range(nb):
                act.wait_ge(sem(f"o{layer}"), len(units(layer)))
                if b >= 2:
                    act.wait_ge(sem(f"osq{layer}"), b - 1)
                act.activation(pm[:, b % 2, :], otok[:, b, :], ACT.Square, accum_out=osq[:, 0, b:b + 1]).then_inc(
                    sem(f"osq{layer}"), 1)
            for t in range(CT):
                act.wait_ge(sem(f"cv{layer}"), 5 * (t + 1))
                if t >= 2:
                    act.wait_ge(sem(f"cv_ss{layer}"), t - 1)
                act.activation(tmp[:, t % 2, 0:w], z[:, 2 * CT + t, 0:w], ACT.Square).then_inc(sem(f"cv_sq{layer}"), 1)
            act.wait_ge(sem(f"ovar{layer}"), 1)
            act.activation(osq[:, 2, 0:nb], osq[:, 1, 0:nb], ACT.Sqrt).then_inc(sem(f"ostd{layer}"), 1)
            act.wait_ge(sem(f"cv_var{layer}"), 1)
            act.activation(std[:, 0, 0:w], var[:, 0, 0:w], ACT.Sqrt).then_inc(sem(f"cv_std{layer}"), 1)
            for b in range(nb):
                act.wait_ge(sem(f"ot_ps{layer}"), b + 1)
                for i in range(CT):
                    act.activation(xh[:, CT + i, b * P:(b + 1) * P], ps[:, b, i * P:(i + 1) * P], ACT.Copy,
                                   scale=vcol(V_GA + layer * CT + i)).then_inc(sem(f"yah{layer}"), 1)
            for t in range(CT):
                act.wait_ge(sem(f"cv_n{layer}"), t + 1)
                act.activation(xh[:, t, 0:w], z[:, 2 * CT + t, 0:w], ACT.Copy).then_inc(sem(f"ych{layer}"), 1)

        def merge_pe(pe, layer):
            w, nb = width(layer), width(layer) // P
            for t in range(CT):
                pe.wait_ge(sem(f"cv_sq{layer}"), t + 1)
                pe.matmul(ps[:, NORM_BANK, 0:w], ones, tmp[:, t % 2, 0:w], start=t == 0,
                          stop=t == CT - 1).then_inc(sem(f"cv_ss{layer}"), 1)
            for b in range(nb):
                pe.wait_ge(sem(f"on{layer}"), b + 1)
                for i in range(CT):
                    last = pe.transpose(ps[:, b, i * P:(i + 1) * P], otok[:, b, i * P:(i + 1) * P], ident)
                last.then_inc(sem(f"ot_ps{layer}"), 1)

        def merge_dve(dve, layer):
            w, nb = width(layer), width(layer) // P
            dve.wait_ge(sem(f"osq{layer}"), nb)
            dve.tensor_scalar(osq[:, 1, 0:nb], osq[:, 0, 0:nb], 1.0 / D_CONV, EPS, ALU.mult, ALU.add).then_inc(
                sem(f"ovar{layer}"), 1)
            dve.wait_ge(sem(f"cv_ss{layer}"), CT)
            dve.tensor_scalar(var[:, 0, 0:w], ps[:, NORM_BANK, 0:w], 1.0 / D_CONV, EPS, ALU.mult,
                              ALU.add).then_inc(sem(f"cv_var{layer}"), 1)
            dve.wait_ge(sem(f"ostd{layer}"), 1)
            dve.reciprocal(osq[:, 0, 0:nb], osq[:, 2, 0:nb]).then_inc(sem(f"orcp{layer}"), 1)
            dve.wait_ge(sem(f"orcp{layer}"), 1)
            for b in range(nb):
                dve.tensor_scalar(otok[:, b, :], otok[:, b, :], osq[:, 0, b:b + 1], None, ALU.mult).then_inc(
                    sem(f"on{layer}"), 1)
            dve.wait_ge(sem(f"cv_std{layer}"), 1)
            dve.reciprocal(rstd[:, 0, 0:w], std[:, 0, 0:w]).then_inc(sem(f"cv_rcp{layer}"), 1)
            dve.wait_ge(sem(f"cv_rcp{layer}"), 1)
            for t in range(CT):
                dve.scalar_tensor_tensor(z[:, 2 * CT + t, 0:w], z[:, 2 * CT + t, 0:w], vcol(V_GC + layer * CT + t),
                                         rstd[:, 0, 0:w], ALU.mult, ALU.mult).then_inc(sem(f"cv_n{layer}"), 1)
            for b in range(nb):
                dve.wait_ge(sem(f"yah{layer}"), CT * (b + 1))
                for i in range(CT):
                    dve.scalar_tensor_tensor(xl[:, CT + i, b * P:(b + 1) * P], ps[:, b, i * P:(i + 1) * P],
                                             vcol(V_GA + layer * CT + i), xh[:, CT + i, b * P:(b + 1) * P],
                                             ALU.mult, ALU.subtract).then_inc(sem(f"yl{layer}"), 1)
            for t in range(CT):
                dve.wait_ge(sem(f"ych{layer}"), t + 1)
                dve.tensor_tensor(xl[:, t, 0:w], z[:, 2 * CT + t, 0:w], xh[:, t, 0:w], ALU.subtract).then_inc(
                    sem(f"yl{layer}"), 1)

        def yl_count(layer):
            return width(layer) // P * CT + CT

        R_LG, R_TOP, R_SEL1, R_SEL, R_COMB, R_RANK, R_POS, R_IDX, R_GATE = range(9)

        def rt(i, b):
            return route[:, i, b, :]

        def route_pe(pe):
            pe.wait_ge(sem("xh"), 7 * KT)
            for b in range(2):
                for k in range(KT):
                    last = pe.matmul(ps[:, 6, b * EXPERTS:(b + 1) * EXPERTS], x2[:, k, b * P:(b + 1) * P],
                                     router[:, k, :], start=k == 0, stop=k == KT - 1)
            last.then_inc(sem("logits"), 1)
            for b in range(2):
                for k in range(KT):
                    a = (k % 4) * P
                    last = pe.transpose(ps[:, 2 * b + k // 4, a:a + P], x2[:, k, b * P:(b + 1) * P], ident)
                last.then_inc(sem("x2t_ps"), 1)
            pe.wait_ge(sem("g2_diag"), 1)
            for k in range(KT):
                last = pe.matmul(ps[:, 4 + k // 4, (k % 4) * P:(k % 4 + 1) * P], ones, hg[:, k * P:(k + 1) * P],
                                 start=True, stop=True)
            last.then_inc(sem("g2_ps"), 1)
            pe.wait_ge(sem("selected"), 1)
            tri = const[:, C_TRI:C_TRI + P]
            r0 = 2 * EXPERTS
            pe.matmul(ps[:, 7, r0:r0 + EXPERTS], tri, rt(R_SEL, 0), start=True, stop=True)
            pe.matmul(ps[:, 7, r0 + EXPERTS:r0 + 2 * EXPERTS], tri, rt(R_SEL, 1), start=True, stop=False)
            pe.matmul(ps[:, 7, r0 + EXPERTS:r0 + 2 * EXPERTS], ones, rt(R_SEL, 0), start=False, stop=True)
            pe.matmul(ps[:, 7, 0:EXPERTS], ones, rt(R_SEL, 0), start=True, stop=False)
            pe.matmul(ps[:, 7, 0:EXPERTS], ones, rt(R_SEL, 1), start=False, stop=True).then_inc(sem("rank_ps"), 1)
            pe.wait_ge(sem("g2b"), 1)
            pe.wait_ge(sem("x2t_l"), 2)
            for b in range(2):
                for k in range(KT):
                    a = (k % 4) * P
                    last = pe.transpose(ps[:, 2 * b + k // 4, a:a + P], h[:, k, b * P:(b + 1) * P], ident)
                last.then_inc(sem("h_ps"), 1)

        def route_act(act):
            for b in range(2):
                act.wait_ge(sem("x2t_ps"), b + 1)
                act.activation(x2t_h[:, b, :], ps[:, 2 * b:2 * b + 2, :].rearrange("p a b -> p (a b)"),
                               ACT.Copy).then_inc(sem("x2t_h"), 1)
            act.wait_ge(sem("top"), 1)
            for b in range(2):
                last = act.activation(rt(R_GATE, b)[:, 0:1], rt(R_GATE, b)[:, 2:3], ACT.Exp)
            last.then_inc(sem("gate_exp"), 1)
            act.wait_ge(sem("g2_ps"), 1)
            act.activation(g2b[:, :], ps[:, 4:6, :].rearrange("p a b -> p (a b)"), ACT.Copy).then_inc(sem("g2b"), 1)
            for b in range(2):
                act.wait_ge(sem("h_ps"), b + 1)
                act.activation(htok[:, b, :], ps[:, 2 * b:2 * b + 2, :].rearrange("p a b -> p (a b)"),
                               ACT.Copy).then_inc(sem("htok"), 1)

        def route_dve(dve):
            step = [0]

            def link(ins):
                step[0] += 1
                ins.then_inc(sem("route"), 1)
                dve.wait_ge(sem("route"), step[0])

            dve.wait_ge(sem("xh"), 7 * KT)
            for k in range(KT):
                last = dve.tensor_scalar(hg[:, k * P:(k + 1) * P], ident, modc(1, 0, G2, k), None, ALU.mult)
            last.then_inc(sem("g2_diag"), 1)
            dve.wait_ge(sem("logits"), 1)
            link(dve.tensor_copy(route[:, R_LG, :, :].rearrange("p b e -> p (b e)"), ps[:, 6, 0:2 * EXPERTS]))
            for b in range(2):
                last = dve.max(rt(R_TOP, b), rt(R_LG, b))
            link(last)
            for b in range(2):
                last = dve.tensor_tensor(rt(R_GATE, b)[:, 2:3], rt(R_TOP, b)[:, 1:2], rt(R_TOP, b)[:, 0:1],
                                         ALU.subtract)
            last.then_inc(sem("top"), 1)
            for b in range(2):
                last = dve.max_index(top_i[:, b, :], rt(R_TOP, b), rt(R_LG, b))
            link(last)
            link(dve.tensor_copy(route[:, R_IDX, :, :].rearrange("p b e -> p (b e)"),
                                 top_i[:, :, :].rearrange("p b e -> p (b e)")))
            iota_e = const[:, C_IOTA:C_IOTA + EXPERTS]
            for b in range(2):
                dve.tensor_scalar(rt(R_SEL1, b), iota_e, rt(R_IDX, b)[:, 0:1], None, ALU.is_equal)
                last = dve.tensor_scalar(rt(R_SEL, b), iota_e, rt(R_IDX, b)[:, 1:2], None, ALU.is_equal)
            link(last)
            dve.wait_ge(sem("gate_exp"), 1)
            for b in range(2):
                last = dve.tensor_scalar(rt(R_GATE, b)[:, 1:2], rt(R_GATE, b)[:, 0:1], 1.0, None, ALU.add)
            link(last)
            for b in range(2):
                last = dve.reciprocal(rt(R_GATE, b)[:, 3:4], rt(R_GATE, b)[:, 1:2])
            link(last)
            for b in range(2):
                last = dve.tensor_tensor(rt(R_GATE, b)[:, 4:5], rt(R_GATE, b)[:, 3:4], rt(R_GATE, b)[:, 0:1], ALU.mult)
            link(last)
            for b in range(2):
                last = dve.tensor_scalar(rt(R_COMB, b), rt(R_SEL, b), rt(R_GATE, b)[:, 4:5], None, ALU.mult)
            link(last)
            for b in range(2):
                last = dve.scalar_tensor_tensor(rt(R_COMB, b), rt(R_SEL1, b), rt(R_GATE, b)[:, 3:4], rt(R_COMB, b),
                                                ALU.mult, ALU.add)
            link(last)
            dve.tensor_tensor(route[:, R_SEL, :, :], route[:, R_SEL, :, :], route[:, R_SEL1, :, :],
                              ALU.add).then_inc(sem("selected"), 1)
            dve.wait_ge(sem("selected"), 1)
            link(dve.tensor_scalar(route[:, R_POS, :, :], route[:, R_SEL, :, :], -4.0 * TOK, 4.0 * TOK, ALU.mult,
                                   ALU.add))
            dve.wait_ge(sem("rank_ps"), 1)
            link(dve.tensor_tensor(route[:, R_POS, :, :].rearrange("p b e -> p (b e)"),
                                   route[:, R_POS, :, :].rearrange("p b e -> p (b e)"),
                                   ps[:, 7, 2 * EXPERTS:4 * EXPERTS], ALU.add))
            dve.tensor_reduce(most[:, :], ps[:, 7, 0:EXPERTS], AX.X, ALU.max).then_inc(sem("most"), 1)
            for b in range(2):
                dve.wait_ge(sem("x2t_h"), b + 1)
                dve.tensor_tensor(x2t_l[:, b, :], ps[:, 2 * b:2 * b + 2, :].rearrange("p a b -> p (a b)"),
                                  x2t_h[:, b, :], ALU.subtract).then_inc(sem("x2t_l"), 1)

        def experts(eng, q, body):
            body(0, True, False)
            with eng.Fori(0, EXPERTS - 2) as i:
                body(1 + i, False, False)
            body(EXPERTS - 1, False, True)

        def m_slot(j):
            return (j + MRING // 2) % MRING

        def m_load(sp, q, e, j, first):
            g = e + EXPERTS * q
            s = m_slot(j)
            n = MCH * g + j
            if not first or j >= MRING:
                sp.wait_ge(sem("mgemm"), n - MRING + 1)
            elif q == 0 and j == 0:
                sp.wait_ge(sem("yl1"), yl_count(1))
            elif q == 0 and j == MRING // 2:
                sp.wait_ge(sem("gemm_done"), CHUNKS)
            if j < 8:
                dst = mraw[:, s, :].rearrange("p (k w n) -> p k w n", k=KT, w=2)
                for w, src in enumerate((moe_w1, moe_w3)):
                    sp.dma_start(dst[:, :, w, :], src.rearrange("a e (k p) n -> p (a e k) n", p=P)[
                        :, bass.ts(e, KT), j * MC:(j + 1) * MC]).then_inc(sem(f"mraw{s}"), 16)
            else:
                dst = mraw[:, s, :].rearrange("p (k n) -> p k n", k=FT)
                src = moe_w2.rearrange("a e (k p) n -> p (a e k) n", p=P)
                for k0, k1 in ((0, 6), (6, FT)):
                    sp.dma_start(dst[:, k0:k1, :], src[:, bass.ds(e * FT + k0, k1 - k0),
                                                       (j - 8) * CW:(j - 7) * CW]).then_inc(sem(f"mraw{s}"), 16)

        def m_arrived(eng, q, e, j):
            g = e + EXPERTS * q
            eng.wait_ge(sem(f"mraw{m_slot(j)}"), 32 * (g * (MCH // MRING) + j // MRING + 1))

        def m_hi(act, q, e, j, first):
            g = e + EXPERTS * q
            s = j % 3
            m_arrived(act, q, e, j)
            if not first or j >= 3:
                act.wait_ge(sem("mgemm"), MCH * g + j - 2)
            act.activation(mwh[:, s, :], mraw[:, m_slot(j), :], ACT.Copy).then_inc(sem("mhi"), 1)

        def m_lo(dve, q, e, j, first):
            g = e + EXPERTS * q
            s = j % 3
            m_arrived(dve, q, e, j)
            dve.wait_ge(sem("mhi"), MCH * g + j + 1)
            dve.tensor_tensor(mwl[:, m_slot(j), :], mraw[:, m_slot(j), :], mwh[:, s, :], ALU.subtract).then_inc(sem("mlo"), 1)

        def gather(pe, q, e, half):
            g = e + EXPERTS * q
            if half == 0:
                pe.wait_ge(sem("pick"), g + 1)
            for m in range(4 * half, 4 * half + 4):
                o = ps[:, 4 + m // 4, (m % 4) * P:(m % 4 + 1) * P]
                for b in range(2):
                    for i, part in enumerate((x2t_h, x2t_l)):
                        last = pe.matmul(o, part[:, b, m * P:(m + 1) * P], pick_r[:, b, :], start=b == 0 and i == 0,
                                         stop=b == 1 and i == 1)
            if half == 1:
                last.then_inc(sem("xg_ps"), 1)

        def put_back(pe, q, e):
            g = e + EXPERTS * q
            pe.wait_ge(sem("ye_l"), g + 1)
            pe.wait_ge(sem("place"), g + 1)
            for b in range(2):
                for half in range(2):
                    o = ps[:, 2 + 2 * b + half, :]
                    pe.matmul(o, place[:, b * P:(b + 1) * P], ye_h[:, half * 512:(half + 1) * 512], start=True,
                              stop=False)
                    pe.matmul(o, place[:, b * P:(b + 1) * P], ye_l[:, half * 512:(half + 1) * 512], start=False,
                              stop=True).then_inc(sem("put"), 1)

        def hidden_t(pe, k0, k1):
            for k in range(k0, k1):
                bank = (2, 3, 0)[k // 4]
                last = pe.transpose(ps[:, bank, (k % 4) * P:(k % 4 + 1) * P], hg[:, k * P:(k + 1) * P], ident)
            last.then_inc(sem("ht_ps"), 1)

        def m_pe(pe, q, e, first, last_e):
            g = e + EXPERTS * q
            for j in range(8):
                s = j % 3
                pe.wait_ge(sem("mlo"), MCH * g + j + 1)
                if j == 0:
                    pe.wait_ge(sem("xg_l"), g + 1)
                if j >= 2:
                    pe.wait_ge(sem("hg"), 8 * g + j - 1)
                for k in range(KT):
                    a = k * 2 * MC
                    last = product(pe, (xg_h[:, k, :], xg_l[:, k, :]),
                                   (mwh[:, s, a:a + 2 * MC], mwl[:, m_slot(j), a:a + 2 * MC]), ps[:, j % 2, 0:2 * MC],
                                   k == 0, k == KT - 1)
                last.then_inc(sem("mgemm"), 1)
                if j == 1 and not first:
                    put_back(pe, q, e - 1)
                if j == 3:
                    if first:
                        pe.wait_ge(sem("pick"), 1)
                    else:
                        pe.wait_ge(sem("yacc"), 4 * g + 4)
                    for b in range(2):
                        last = pe.transpose(ps[:, 2, b * P:(b + 1) * P], pick[:, b, :], ident)
                    last.then_inc(sem("place_ps"), 1)
                if j == 6:
                    pe.wait_ge(sem("hg"), 8 * g + 6)
                    pe.wait_ge(sem("place"), g + 1)
                    hidden_t(pe, 0, 8)
            if not last_e:
                gather(pe, q, e + 1, 0)
            pe.wait_ge(sem("hg"), 8 * g + 8)
            hidden_t(pe, 8, FT)
            if not last_e:
                gather(pe, q, e + 1, 1)
            pe.wait_ge(sem("ht_l"), 2 * g + 2)
            for c4 in range(4):
                s = (8 + c4) % 3
                pe.wait_ge(sem("mlo"), MCH * g + 9 + c4)
                for k in range(FT):
                    last = product(pe, (ht_h[:, k * P:(k + 1) * P], ht_l[:, k * P:(k + 1) * P]),
                                   (mwh[:, s, k * CW:(k + 1) * CW],
                                    mwl[:, m_slot(8 + c4), k * CW:(k + 1) * CW]),
                                   ps[:, 6 + c4 // 2, (c4 % 2) * CW:(c4 % 2 + 1) * CW], k == 0, k == FT - 1)
                last.then_inc(sem("mgemm"), 1)
            if last_e:
                put_back(pe, q, e)

        def m_act(act, q, e, first, last_e):
            g = e + EXPERTS * q
            for j in range(8):
                m_hi(act, q, e, j + 2, first)
                if j == 5:
                    act.wait_ge(sem("place_ps"), g + 1)
                    act.activation(place[:, :], ps[:, 2, 0:SEQ], ACT.Copy).then_inc(sem("place"), 1)
                if j == 7:
                    act.wait_ge(sem("ht_ps"), 2 * g + 1)
                    act.activation(ht_h[:, 0:8 * P], ps[:, 2:4, :].rearrange("p a b -> p (a b)"),
                                   ACT.Copy).then_inc(sem("ht_h"), 1)
                act.wait_ge(sem("mgemm"), MCH * g + j + 1)
                if not first or j >= 2:
                    act.wait_ge(sem("hg"), 8 * g + j - 1)
                act.activation(sg[:, j % 2, :], ps[:, j % 2, 0:MC], ACT.Silu).then_inc(sem("sg"), 1)
            act.wait_ge(sem("ht_ps"), 2 * g + 2)
            act.activation(ht_h[:, 8 * P:FT * P], ps[:, 0, 0:(FT - 8) * P], ACT.Copy).then_inc(sem("ht_h"), 1)
            if not last_e:
                xg_act(act, q, e + 1)
            for j in range(10, MCH + 2):
                if j < MCH:
                    m_hi(act, q, e, j, first)
                elif not last_e:
                    m_hi(act, q, e + 1, j - MCH, False)
            act.wait_ge(sem("mgemm"), MCH * g + MCH)
            act.activation(ye_h[:, :], ps[:, 6:8, :].rearrange("p a b -> p (a b)"), ACT.Copy).then_inc(
                sem("ye_h"), 1)

        def xg_act(act, q, e):
            g = e + EXPERTS * q
            act.wait_ge(sem("xg_ps"), g + 1)
            act.activation(xg_h[:, :, :].rearrange("p k s -> p (k s)"),
                           ps[:, 4:6, :].rearrange("p a b -> p (a b)"), ACT.Copy).then_inc(sem("xg_h"), 1)

        def xg_dve(dve, q, e):
            g = e + EXPERTS * q
            dve.wait_ge(sem("xg_h"), g + 1)
            dve.tensor_tensor(xg_l[:, :, :].rearrange("p k s -> p (k s)"),
                              ps[:, 4:6, :].rearrange("p a b -> p (a b)"),
                              xg_h[:, :, :].rearrange("p k s -> p (k s)"), ALU.subtract).then_inc(sem("xg_l"), 1)

        def pick_dve(dve, q, e):
            g = e + EXPERTS * q
            iota = const[:, C_IOTA:C_IOTA + P]
            for b in range(2):
                pos = route[:, R_POS, b, bass.ds(e, 1)]
                dve.tensor_scalar(pick[:, b, :], iota, pos, None, ALU.is_equal)
                last = dve.tensor_scalar(pick_r[:, b, :], iota, pos, None, ALU.is_equal)
            last.then_inc(sem("pick"), 1)

        def sum_dve(dve, q, e):
            g = e + EXPERTS * q
            for b in range(2):
                for half in range(2):
                    i = 2 * b + half
                    dve.wait_ge(sem("put"), 4 * g + i + 1)
                    dve.wait_ge(sem("yacc"), 4 * g + 1 + i)
                    y = ytok[:, b, half * 512:(half + 1) * 512]
                    dve.scalar_tensor_tensor(y, ps[:, 2 + i, :], route[:, R_COMB, b, bass.ds(e, 1)], y, ALU.mult,
                                             ALU.add).then_inc(sem("yacc"), 1)

        def m_dve(dve, q, e, first, last_e):
            g = e + EXPERTS * q
            for j in range(8):
                m_lo(dve, q, e, j + 2, first)
                if j == 7:
                    dve.wait_ge(sem("ht_h"), 2 * g + 1)
                    dve.tensor_tensor(ht_l[:, 0:8 * P], ps[:, 2:4, :].rearrange("p a b -> p (a b)"),
                                      ht_h[:, 0:8 * P], ALU.subtract).then_inc(sem("ht_l"), 1)
                dve.wait_ge(sem("sg"), 8 * g + j + 1)
                dve.tensor_tensor(hg[:, j * MC:(j + 1) * MC], sg[:, j % 2, :], ps[:, j % 2, MC:2 * MC],
                                  ALU.mult).then_inc(sem("hg"), 1)
                if j == 1 and not first:
                    sum_dve(dve, q, e - 1)
                if j == 5 and not last_e:
                    pick_dve(dve, q, e + 1)
            dve.wait_ge(sem("ht_h"), 2 * g + 2)
            dve.tensor_tensor(ht_l[:, 8 * P:FT * P], ps[:, 0, 0:(FT - 8) * P], ht_h[:, 8 * P:FT * P],
                              ALU.subtract).then_inc(sem("ht_l"), 1)
            if not last_e:
                xg_dve(dve, q, e + 1)
            for j in range(10, MCH + 2):
                if j < MCH:
                    m_lo(dve, q, e, j, first)
                elif not last_e:
                    m_lo(dve, q, e + 1, j - MCH, False)
            dve.wait_ge(sem("ye_h"), g + 1)
            dve.tensor_tensor(ye_l[:, :], ps[:, 6:8, :].rearrange("p a b -> p (a b)"), ye_h[:, :],
                              ALU.subtract).then_inc(sem("ye_l"), 1)
            if last_e:
                sum_dve(dve, q, e)

        def pass_sp(sp, q):
            experts(sp, q, lambda e, first, last: [m_load(sp, q, e, j, first) for j in range(MCH)] and None)

        def pass_pe(pe, q):
            gather(pe, q, 0, 0)
            gather(pe, q, 0, 1)
            experts(pe, q, lambda e, first, last: m_pe(pe, q, e, first, last))

        def pass_act(act, q):
            m_hi(act, q, 0, 0, True)
            m_hi(act, q, 0, 1, True)
            xg_act(act, q, 0)
            experts(act, q, lambda e, first, last: m_act(act, q, e, first, last))

        def pass_dve(dve, q):
            pick_dve(dve, q, 0)
            m_lo(dve, q, 0, 0, True)
            m_lo(dve, q, 0, 1, True)
            xg_dve(dve, q, 0)
            experts(dve, q, lambda e, first, last: m_dve(dve, q, e, first, last))

        def overflow(eng):
            eng.wait_ge(sem("most"), 1)
            return eng.value_load(most[0:1, 0:1], min_val=0, max_val=SEQ) > P

        block = stack.enter_context(nc.Block())
        PARTS = [(0, PART), (PART, FF_CH)]

        @block.sync
        def _(sp):
            for dst, src in (
                (const[:, :], table),
                (rows_b[V_C:V_C + KT, :], c.rearrange("b (k p) -> (b k) p", p=P)),
                (rows_b[V_CC:V_CC + KT, :], c_ctx.rearrange("(k p) -> k p", p=P)),
                (rows_b[V_N1:V_N1 + DEPTH * KT, :], norm1_g.rearrange("l (k p) -> (l k) p", p=P)),
                (rows_b[V_N2:V_N2 + DEPTH * KT, :], norm2_g.rearrange("l (k p) -> (l k) p", p=P)),
                (rows_b[V_GC:V_GC + DEPTH * CT, :], out_norm_conv_g.rearrange("l (k p) -> (l k) p", p=P)),
                (rows_b[V_GA:V_GA + DEPTH * CT, :], out_norm_attn_g.rearrange("l (k p) -> (l k) p", p=P)),
                (rows_b[V_CW:V_CW + DEPTH * 3 * CT, :], conv_w.rearrange("l t (k p) -> (l t k) p", p=P)),
                (rows_b[V_QG:V_QG + DEPTH, 0:HD], q_norm_g),
                (rows_b[V_QG:V_QG + DEPTH, HD:P], q_norm_g),
                (rows_b[V_KG:V_KG + DEPTH, 0:HD], k_norm_g),
                (rows_b[V_KG:V_KG + DEPTH, HD:P], k_norm_g),
                (rows_a[0:DEPTH * GROUPS * KT, :], b_ada.rearrange("l (k p) -> (l k) p", p=P)),
                (sink_row[0:1, :], attn_sink.rearrange("(a l) h -> a (l h)", a=1)),
                (router[:, :, :], moe_router[0].rearrange("(k p) e -> p k e", p=P)),
            ):
                sp.dma_start(dst, src).then_inc(sem("params_in"), 16)
            for b in range(2):
                sp.dma_start(xin[:, b, :], x[0].rearrange("(b p) d -> b p d", p=P)[b]).then_inc(sem("x_in"), 16)
                sp.dma_start(xin[:, 2 + b, :], ctx[0].rearrange("(b p) d -> b p d", p=P)[b]).then_inc(
                    sem("x_in"), 16)
            for k in range(KT):
                sp.dma_start(ada0[k // 4][:, k % 4, :], w_ada[0][k * P:(k + 1) * P, 0:2 * D]).then_inc(
                    sem(f"ada0_in{k // 2}"), 16)
            n = first_chunk[0, "in"]
            load(sp, w_in_src(0, in_col(0)), n)
            for j in range(IN_CH):
                if j + 1 < IN_CH:
                    load(sp, w_in_src(0, in_col(j + 1)), n + j + 1)
                else:
                    load(sp, w_out_src(0, 0), first_chunk[0, "out"])
                if j >= 1:
                    ada_load(sp, 1, j - 1)
            for j in range(1, OUT_CH):
                load(sp, w_out_src(0, j), first_chunk[0, "out"] + j)
                for k in (2 * j - 2, 2 * j - 1):
                    ada_load(sp, 2, k)
            for part, (c0, c1) in enumerate(PARTS):
                n = first_chunk[0, f"up{part}"]
                load(sp, up_src(ffn_w1, c0), n)
                if part == 0:
                    for k in (KT - 2, KT - 1):
                        ada_load(sp, 2, k)
                with sp.Fori(0, c1 - c0 - 1) as i:
                    load(sp, up_src(ffn_w3, c0 + i), n + 1, i)
                    load(sp, up_src(ffn_w1, c0 + 1 + i), n + 2, i)
                    if part == 0:
                        ada_load(sp, 3, 0, i)
                load(sp, up_src(ffn_w3, c1 - 1), n + 2 * (c1 - c0) - 1)
                n = first_chunk[0, f"down{part}"]
                load(sp, down_src(c0), n, cols=2)
                if part == 0:
                    ada_load(sp, 3, c1 - c0 - 1)
                for j in range(1, c1 - c0):
                    load(sp, down_src(c0 + j), n + j, cols=2)
                    if part == 0 and j <= 2:
                        ada_load(sp, 3, c1 - c0 - 1 + j)
            n = first_chunk[1, "in"]
            for j in range(IN_CH):
                load(sp, w_in_src(1, in_col(j)), n + j)
            for j in range(OUT_CH):
                load(sp, w_out_src(1, j), first_chunk[1, "out"] + j)

            pass_sp(sp, 0)
            with sp.If(overflow(sp)):
                sp.wait_ge(sem("yacc"), 4 * EXPERTS + 4)
                pass_sp(sp, 1)
            for b in range(2):
                sp.wait_ge(sem("result"), b + 1)
                sp.dma_start(out[0].rearrange("(b p) d -> b p d", p=P)[b], ytok[:, b, :]).then_inc(sem("stored"), 16)
            sp.wait_ge(sem("stored"), 32)

        @block.tensor
        def _(pe):
            pe.wait_ge(sem("params_in"), 15 * 16)
            pe.transpose(ps[:, 0, 0:V_ROWS], rows_b[0:V_ROWS, :], const[0:V_ROWS, C_ID:C_ID + V_ROWS])
            n = DEPTH * GROUPS * KT
            pe.transpose(ps[:, 0, P:P + n], rows_a[0:n, :], const[0:n, C_ID:C_ID + n])
            pe.matmul(ps[:, 0, 2 * P:2 * P + DEPTH * HEADS], const[0:1, C_ONES:C_ONES + P], sink_row[0:1, :],
                      start=True, stop=True).then_inc(sem("params_ps"), 1)
            pe.wait_ge(sem("x_in"), 64)
            pe.wait_ge(sem("params_out"), 3)
            for k in range(KT):
                for b in range(NBLK):
                    last = pe.transpose(ps[:, k, b * P:(b + 1) * P], xin[:, b, k * P:(k + 1) * P], ident)
                last.then_inc(sem("x_ps"), 1)
            pe.wait_ge(sem("h_loaded"), KT)
            for k in range(KT):
                ada0_pe(pe, k)
                if k == KT // 2:
                    norm_pe(pe, (0, 0))
            ada0_cols(pe)
            for layer in range(DEPTH):
                w = width(layer)
                n = first_chunk[layer, "in"]
                for j in range(IN_CH):
                    if j >= 2:
                        pe.wait_ge(sem(f"z{layer}"), j - 1)
                    if j == 0:
                        gemm_first(pe, n, w, normed(layer, 0))
                    else:
                        gemm_chunk(pe, n + j, 0, TOK if j == 2 else w)
                    qk_pe(pe, layer, j)
                if layer == 0:
                    pe.wait_ge(sem("kd0"), 2)
                    mod_rows(pe, 1)
                pe.wait_ge(sem(f"z{layer}"), IN_CH)
                att_pe(pe, layer)
                merge_pe(pe, layer)
                if layer == 0:
                    mod_cols(pe, 1)
                    pe.wait_ge(sem("mod_out"), 2)
                pe.wait_ge(sem(f"yl{layer}"), yl_count(layer))
                n = first_chunk[layer, "out"]
                for j in range(OUT_CH):
                    if j >= 2:
                        pe.wait_ge(sem(f"h_mixed{layer}"), j - 1)
                    gemm_chunk(pe, n + j, 0, w)
                    if j >= 1:
                        norm_pe(pe, (layer, 1), 2 * j - 2, 2 * j)
                norm_pe(pe, (layer, 1), KT - 2, KT)
                if layer == 0:
                    mod_rows(pe, 2)
                    for part, (c0, c1) in enumerate(PARTS):
                        n = first_chunk[0, f"up{part}"]

                        def pair(i, first):
                            n1 = n if first else n + 2
                            if c0 or not first:
                                pe.wait_ge(sem("silu"), c0 + (0 if first else 1) + i)
                            if c0 and first:
                                pe.wait_ge(sem("h_ffn"), 4)
                            if c0 == 0 and first:
                                gemm_first(pe, n1, TOK, normed(0, 1))
                            else:
                                gemm_chunk(pe, n1, i, TOK)
                            if c0 or not first:
                                pe.wait_ge(sem("glu"), c0 + (0 if first else 1) + i)
                            gemm_chunk(pe, n1 + 1, i, TOK)

                        pair(0, True)
                        if part:
                            pe.wait_ge(sem("h_ffn"), KT)
                            mod_rows(pe, 3)
                        mod_cols(pe, 2 + part)
                        with pe.Fori(0, c1 - c0 - 1) as i:
                            pair(i, False)
                        n = first_chunk[0, f"down{part}"]
                        pe.wait_ge(sem("glu"), c1)
                        pe.wait_ge(sem("mod_out"), 3 + part)
                        for j in range(c1 - c0):
                            s = (n + j) % 2
                            pe.wait_ge(sem("lo_done"), n + j + 1)
                            pe.wait_ge(sem("hid"), c0 + j + 1)
                            for r in range(2):
                                for m in range(KT):
                                    a = r * D + m * P
                                    last = product(pe, (wh[:, s, a:a + P], wl[:, s, a:a + P]),
                                                   (hid_h[:, 2 * j + r, :], hid_l[:, 2 * j + r, :]), ps[:, m, :],
                                                   j == 0 and r == 0, j == c1 - c0 - 1 and r == 1)
                            last.then_inc(sem("gemm_done"), 1)
                    norm_pe(pe, (1, 0))
            route_pe(pe)
            pass_pe(pe, 0)
            with pe.If(overflow(pe)):
                pe.wait_ge(sem("yacc"), 4 * EXPERTS + 4)
                pass_pe(pe, 1)

        @block.scalar
        def _(act):
            act.wait_ge(sem("params_ps"), 1)
            act.activation(cs[:, :, :].rearrange("p k s -> p s k"),
                           ps[:, 0, V_C:V_C + 2 * KT].rearrange("p (s k) -> p s k", s=2), ACT.Silu).then_inc(
                sem("cs"), 1)
            for k in range(0, KT, 2):
                act.wait_ge(sem("x_ps"), k + 1)
                act.activation(h[:, k, :], ps[:, k, :], ACT.Copy).then_inc(sem("h_loaded"), 1)
            norm_sq(act, (0, 0))
            split_hi(act, 0)
            mod_row_act(act, 0)
            norm_act(act, (0, 0))
            for layer in range(DEPTH):
                w = width(layer)
                n = first_chunk[layer, "in"]

                def z_out(act, n0, col, w):
                    act.wait_ge(sem("gemm_done"), n0 + 1)
                    b = 2 * (n0 % 2)
                    act.activation(z[:, 2 * col:2 * col + 2, 0:w], ps[:, b:b + 2, 0:w], ACT.Copy).then_inc(
                        sem(f"z{layer}"), 1)

                for j in range(IN_CH):
                    split_hi(act, n + j + 1)
                    z_out(act, n + j, in_col(j), TOK if j == 2 else w)
                    qk_act(act, layer, j)
                if layer == 0:
                    mod_row_act(act, 1)
                att_act(act, layer)
                merge_act(act, layer)
                n = first_chunk[layer, "out"]
                for j in range(OUT_CH):
                    if j < OUT_CH - 1 or layer == 0:
                        split_hi(act, n + j + 1)
                    if j >= 1:
                        norm_sq(act, (layer, 1), 2 * j - 2, 2 * j)
                norm_sq(act, (layer, 1), KT - 2, KT)
                norm_act(act, (layer, 1))
                if layer == 0:
                    for part, (c0, c1) in enumerate(PARTS):
                        n = first_chunk[0, f"up{part}"]

                        def pair(i, n0, p):
                            split_hi(act, n0 + 1, i)
                            act.wait_ge(sem("gemm_done"), n0 + 1 + 2 * i)
                            if p:
                                act.wait_ge(sem("hid"), p + i)
                            b1 = 2 * (n0 % 2)
                            act.activation(tmp[:, :, :], ps[:, b1:b1 + 2, :], ACT.Silu).then_inc(sem("silu"), 1)
                            split_hi(act, n0 + 2, i)
                            act.wait_ge(sem("glu"), p + 1 + i)
                            act.activation(hid_h[:, bass.ts(p - c0 + i, 2), :], tmp[:, :, :], ACT.Copy).then_inc(
                                sem("hid_h"), 1)

                        pair(0, n, c0)
                        mod_row_act(act, 2 + part)
                        with act.Fori(0, c1 - c0 - 1) as i:
                            pair(i, n + 2, c0 + 1)
                        n = first_chunk[0, f"down{part}"]
                        for j in range(c1 - c0):
                            split_hi(act, n + j + 1)
                    norm_sq(act, (1, 0))
                    norm_act(act, (1, 0))
            route_act(act)
            pass_act(act, 0)
            with act.If(overflow(act)):
                act.wait_ge(sem("yacc"), 4 * EXPERTS + 4)
                pass_act(act, 1)

        @block.vector
        def _(dve):
            dve.wait_ge(sem("params_ps"), 1)
            dve.wait_ge(sem("cs"), 1)
            dve.tensor_copy(vec[:, :], ps[:, 0, 0:V_ROWS]).then_inc(sem("params_out"), 1)
            dve.tensor_copy(b_ada_t[:, :], ps[:, 0, P:P + DEPTH * GROUPS * KT]).then_inc(sem("params_out"), 1)
            dve.tensor_scalar(nsink[:, :], ps[:, 0, 2 * P:2 * P + DEPTH * HEADS], -1.0, None, ALU.mult).then_inc(
                sem("params_out"), 1)
            dve.tensor_copy(ident_b[:, :], ident).then_inc(sem("masks"), 1)
            dve.tensor_copy(mask_b[:, :, :].rearrange("p a b -> p (a b)"), const[:, C_MASK:C_MASK + 2 * P]).then_inc(
                sem("masks"), 1)
            for k in range(1, KT, 2):
                dve.wait_ge(sem("x_ps"), k + 1)
                dve.tensor_copy(h[:, k, :], ps[:, k, :]).then_inc(sem("h_loaded"), 1)
            split_lo(dve, 0)
            mod_out(dve, 0)
            norm_dve(dve, (0, 0))
            for layer in range(DEPTH):
                w = width(layer)
                n = first_chunk[layer, "in"]
                for j in range(IN_CH):
                    split_lo(dve, n + j + 1)
                    if layer == 0 and j >= 1:
                        ada_step(dve, 1, j - 1)
                    qk_dve(dve, layer, j)
                dve.wait_ge(sem(f"z{layer}"), IN_CH)
                att_dve(dve, layer)
                merge_dve(dve, layer)
                if layer == 0:
                    mod_out(dve, 1)
                n = first_chunk[layer, "out"]
                for j in range(OUT_CH):
                    if j < OUT_CH - 1 or layer == 0:
                        split_lo(dve, n + j + 1)
                    if layer == 0:
                        ada_step(dve, 2, 2 * j)
                        ada_step(dve, 2, 2 * j + 1)
                    dve.wait_ge(sem("gemm_done"), n + j + 1)
                    for mt in range(2):
                        m = 2 * j + mt
                        for s in range(w // SEQ):
                            last = dve.scalar_tensor_tensor(
                                h[:, m, span(s)], ps[:, 2 * ((n + j) % 2) + mt, span(s)], modc(layer, s, G1, m),
                                h[:, m, span(s)], ALU.mult, ALU.add)
                    last.then_inc(sem(f"h_mixed{layer}"), 1)
                norm_dve(dve, (layer, 1))
                if layer == 0:
                    for part, (c0, c1) in enumerate(PARTS):
                        n = first_chunk[0, f"up{part}"]

                        def pair(i, n0, p):
                            split_lo(dve, n0 + 1, i)
                            split_lo(dve, n0 + 2, i)
                            if part == 0:
                                ada_step(dve, 3, p, i)
                            dve.wait_ge(sem("silu"), p + 1 + i)
                            dve.wait_ge(sem("gemm_done"), n0 + 2 + 2 * i)
                            b3 = 2 * ((n0 + 1) % 2)
                            dve.tensor_tensor(tmp[:, :, :], tmp[:, :, :], ps[:, b3:b3 + 2, :], ALU.mult).then_inc(
                                sem("glu"), 1)
                            dve.wait_ge(sem("hid_h"), p + 1 + i)
                            dve.tensor_tensor(hid_l[:, bass.ts(p - c0 + i, 2), :], tmp[:, :, :],
                                              hid_h[:, bass.ts(p - c0 + i, 2), :], ALU.subtract).then_inc(
                                sem("hid"), 1)

                        pair(0, n, c0)
                        mod_out(dve, 2 + part)
                        with dve.Fori(0, c1 - c0 - 1) as i:
                            pair(i, n + 2, c0 + 1)
                        n = first_chunk[0, f"down{part}"]
                        for j in range(c1 - c0):
                            split_lo(dve, n + j + 1)
                            if part == 0 and j < 2:
                                ada_step(dve, 3, c1 - c0 + j)
                        dve.wait_ge(sem("gemm_done"), n + c1 - c0)
                        for m in range(KT):
                            for s in range(2):
                                last = dve.scalar_tensor_tensor(h[:, m, span(s)], ps[:, m, span(s)],
                                                                modc(0, s, G2, m), h[:, m, span(s)], ALU.mult,
                                                                ALU.add)
                            last.then_inc(sem("h_ffn"), 1)
                    norm_dve(dve, (1, 0))
            route_dve(dve)
            dve.wait_ge(sem("yacc"), 4)
            pass_dve(dve, 0)
            with dve.If(overflow(dve)):
                dve.wait_ge(sem("yacc"), 4 * EXPERTS + 4)
                dve.tensor_scalar(route[:, R_POS, :, :], route[:, R_POS, :, :], -float(P), None,
                                  ALU.add).then_inc(sem("shifted"), 1)
                dve.wait_ge(sem("shifted"), 1)
                pass_dve(dve, 1)
                dve.wait_ge(sem("yacc"), 8 * EXPERTS + 4)
            dve.wait_ge(sem("htok"), 2)
            dve.wait_ge(sem("yacc"), 4 * EXPERTS + 4)
            for b in range(2):
                dve.tensor_tensor(ytok[:, b, :], ytok[:, b, :], g2b[:, :], ALU.mult).then_inc(sem("gated"), 1)
            for b in range(2):
                dve.wait_ge(sem("gated"), b + 1)
                dve.tensor_tensor(ytok[:, b, :], ytok[:, b, :], htok[:, b, :], ALU.add).then_inc(sem("result"), 1)

        @block.gpsimd
        def _(pool):
            pool.wait_ge(sem("h_mixed1"), OUT_CH)
            for i in range(4):
                pool.memset(ytok[:, i // 2, (i % 2) * 512:(i % 2 + 1) * 512], 0.0).then_inc(sem("yacc"), 1)


_INS = ["x", "c", "ctx", "c_ctx", "w_ada", "b_ada", "norm1_g", "norm2_g", "w_in", "conv_w", "q_norm_g", "k_norm_g",
        "attn_sink", "out_norm_conv_g", "out_norm_attn_g", "w_out", "ffn_w1", "ffn_w3", "ffn_w2",
        "moe_router", "moe_w1", "moe_w3", "moe_w2"]
_OUTS = [((1, SEQ, D), "float32")]


def kernel(**inputs):
    import numpy as _np
    import concourse.bacc as _bacc
    from concourse import mybir as _mybir
    from concourse.bass_utils import run_bass_kernel_spmd as _run

    nc = _bacc.Bacc("TRN2", target_bir_lowering=False, num_devices=1)
    arrays, args = {}, []
    for name in _INS:
        a = _np.ascontiguousarray(inputs[name])
        arrays[f"in_{name}_dram"] = a
        args.append(nc.dram_tensor(f"in_{name}_dram", a.shape, _mybir.dt.from_np(a.dtype), kind="ExternalInput").ap())
    table = constant_table(_np)
    arrays["table_dram"] = table
    args.append(nc.dram_tensor("table_dram", table.shape, _mybir.dt.from_np(table.dtype), kind="ExternalInput").ap())
    for i, (shape, dtype) in enumerate(_OUTS):
        dt = _mybir.dt.from_np(_np.dtype(dtype))
        args.append(nc.dram_tensor(f"out_{i}_dram", shape, dt, kind="ExternalOutput").ap())
    hybrid_backbone(nc, *args)
    r = _run(nc, [arrays], core_ids=[0])
    got = tuple(r.results[0][f"out_{i}_dram"] for i in range(len(_OUTS)))
    return got[0]
```

```python
import math
from contextlib import ExitStack

import concourse.bass as bass
from concourse import mybir

F32 = mybir.dt.float32
F32R = mybir.dt.float32r
BF16 = mybir.dt.bfloat16
U32 = mybir.dt.uint32
I32 = mybir.dt.int32
ALU = mybir.AluOpType
ACT = mybir.ActivationFunctionType
AX = mybir.AxisListType

P = 128
D = 1024
KT = D // P
SEQ, CTX = 256, 256
TOK = SEQ + CTX
NBLK = TOK // P
DEPTH = 2
D_CONV = D // 2
CT = D_CONV // P
HEADS, N_KV, HD = 8, 2, 64
D_IN = 3 * D_CONV + 512 + 2 * N_KV * HD
ZT = D_IN // P
D_FF = 2816
EXPERTS, F_EXP = 8, 1408
EPS = 1e-6
SCALE = HD ** -0.5
CW = 256
SLOT = KT * CW
IN_CH, OUT_CH = D_IN // CW, D // CW
FF_CH = D_FF // CW
PART = (FF_CH + 1) // 2
FT = F_EXP // P
MC = F_EXP // 8
MSLOT = 2 * MC * KT
MCH = 8 + D // CW
MRING = 6
assert MSLOT == FT * CW
GROUPS = 6
SH1, SC1, G1, SH2, SC2, G2 = range(GROUPS)

V_N1, V_N2 = 0, DEPTH * KT
V_GC = V_N2 + DEPTH * KT
V_GA = V_GC + DEPTH * CT
V_CW = V_GA + DEPTH * CT
V_C = V_CW + DEPTH * 3 * CT
V_CC = V_C + KT
V_QG = V_CC + KT
V_KG = V_QG + DEPTH
V_ROWS = V_KG + DEPTH

C_COS, C_SIN = 0, SEQ
C_ROT = 2 * SEQ
C_DUP = C_ROT + P
C_BONES = C_DUP + 4 * P
C_ID = C_BONES + P
C_ONES = C_ID + P
C_TRI = C_ONES + P
C_MASK = C_TRI + P
C_IOTA = C_MASK + 2 * P
C_SLIDE = C_IOTA + P
C_EPS = C_SLIDE + 31
C_ALL = C_EPS + 1


def constant_table(np):
    n_freq = HD // 4
    inv = (np.float32(10000.0) ** (-np.arange(n_freq, dtype=np.float32) / np.float32(n_freq))).astype(np.float32)
    tok = np.arange(SEQ)
    row, col = (tok // 64).astype(np.float32), (tok % 64).astype(np.float32)
    ar, ac = row[:, None] * inv, col[:, None] * inv
    ang = np.concatenate([ar, ar, ac, ac], axis=-1).astype(np.float32).T
    t = np.zeros((P, C_ALL), np.float32)
    t[:, C_COS:C_COS + SEQ] = np.tile(np.cos(ang), (2, 1))
    t[:, C_SIN:C_SIN + SEQ] = np.tile(np.sin(ang), (2, 1))
    for p in range(P):
        if p % 32 < 16:
            t[p + 16, C_ROT + p] = -1.0
        else:
            t[p - 16, C_ROT + p] = 1.0
        for g in range(2):
            t[HD * g + p % HD, C_DUP + (2 * g + p // HD) * P + p] = 1.0
        t[HD * (p // HD):HD * (p // HD + 1), C_BONES + p] = 1.0
        t[p, C_ID + p] = 1.0
        t[p, C_TRI + p + 1:C_TRI + P] = 1.0
    t[:, C_ONES:C_ONES + P] = 1.0
    q, k = np.arange(P)[:, None], np.arange(P)[None, :]
    t[:, C_MASK:C_MASK + P] = np.where(k <= q, 0.0, -1e30)
    t[:, C_MASK + P:C_MASK + 2 * P] = np.where(k >= q, 0.0, -1e30)
    t[:, C_IOTA:C_IOTA + P] = np.arange(P, dtype=np.float32)
    t[:, C_SLIDE + 15] = 1.0
    t[:, C_EPS] = EPS
    return t


def stages():
    out, n = [], 0
    for layer in range(DEPTH):
        plan = [("in", IN_CH), ("out", OUT_CH)]
        if layer == 0:
            plan += [("up0", 2 * PART), ("down0", PART), ("up1", 2 * (FF_CH - PART)), ("down1", FF_CH - PART)]
        for name, count in plan:
            out.append((layer, name, n, count))
            n += count
    return out, n


def hybrid_backbone(nc, x, c, ctx, c_ctx, w_ada, b_ada, norm1_g, norm2_g, w_in, conv_w, q_norm_g, k_norm_g,
                    attn_sink, out_norm_conv_g, out_norm_attn_g, w_out, ffn_w1, ffn_w3, ffn_w2,
                    moe_router, moe_w1, moe_w3, moe_w2, table, out):
    STAGES, CHUNKS = stages()
    first_chunk = {(layer, name): n for layer, name, n, _ in STAGES}

    with ExitStack() as stack:
        sems = {}

        def sem(name):
            if name not in sems:
                sems[name] = stack.enter_context(nc.semaphore(name))
            return sems[name]

        base = -(-nc.sbuf_base // 64) * 64

        def at(name, offset, shape, dt=F32):
            size = -(-math.prod(shape[1:]) * (2 if dt == BF16 else 4) // 64) * 64
            assert base + offset + size <= nc.sbuf_usable_end, (name, offset + size)
            return nc.alloc_sbuf_tensor_at(name, shape, dt, offset=base + offset), offset + size

        const, o = at("const", 0, [P, C_ALL])
        ident_b, o = at("ident_b", o, [P, P], BF16)
        mask_b, o = at("mask_b", o, [P, 2, P], BF16)
        vec, o = at("vec", o, [P, V_ROWS])
        b_ada_t, o = at("b_ada_t", o, [P, DEPTH * GROUPS * KT])
        cs, o = at("cs", o, [P, KT, 2])
        mod, o = at("mod", o, [P, DEPTH, 2, GROUPS * KT])
        gain, o = at("gain", o, [P, DEPTH, 2, 2, KT])
        nsink, o = at("nsink", o, [P, DEPTH * HEADS])
        router, o = at("router", o, [P, KT, EXPERTS])
        route, o = at("route", o, [P, 12, 2, EXPERTS])
        top_i, o = at("top_i", o, [P, 2, EXPERTS], U32)
        most, o = at("most", o, [P, 1], I32)
        h, o = at("h", o, [P, KT, TOK])
        ZONE = o
        xh, o = at("xh", o, [P, KT, TOK], F32R)
        xl, o = at("xl", o, [P, KT, TOK], F32R)
        Z = o
        z, o = at("z", Z, [P, ZT, TOK])
        VAR = o
        std, o = at("std", o, [P, 2, TOK])
        rstd, o = at("rstd", o, [P, 2, TOK])
        xin, o2 = at("xin", Z, [P, NBLK, D])
        rows0, o2 = at("rows0", o2, [2, 2 * D])
        sq0, o2 = at("sq0", o2, [P, 4, TOK])
        sq0_sum, o2 = at("sq0_sum", o2, [P, TOK])
        assert o2 <= VAR
        hid_h, o2 = at("hid_h", Z, [P, 2 * PART, TOK], F32R)
        hid_l, o2 = at("hid_l", o2, [P, 2 * PART, TOK], F32R)
        RAW = max(o + 4 * TOK, o2, VAR + 4096 + 4096 + 4096)
        raw, o = at("raw", RAW, [P, 2, SLOT])
        rows_a, o2 = at("rows_a", o, [P, P])
        rows_b, o2 = at("rows_b", o2, [P, P])
        sink_row, o2 = at("sink_row", o2, [P, DEPTH * HEADS])
        wh, o = at("wh", o, [P, 2, SLOT], F32R)
        wl, o = at("wl", o, [P, 2, SLOT], F32R)
        ada, o = at("ada", o, [P, 2, D])
        TMP = o
        tmp, o = at("tmp", o, [P, 2, TOK])
        tn, o = at("tn", o, [P, 2, SEQ])
        tmp4 = tmp[:, :, :].rearrange("p a (b t) -> p (a b) t", b=2)
        A = o
        acc, _ = at("acc", A, [P, 8, D])
        ada0 = [at("ada0_a", ZONE, [P, 4, 2 * D])[0], at("ada0_b", A, [P, 4, 2 * D])[0]]
        kd, o = at("kd", A, [P, 2, 2, TOK])
        vtok, o = at("vtok", o, [P, NBLK, P])
        acc_mix, rows_at = at("acc_mix", o, [P, 6, D])
        mod_row, _ = at("mod_row", rows_at, [16, TOK])
        pm, o = at("pm", o, [P, 2, TOK])
        pt, o = at("pt", o, [P, 2, TOK])
        otok, o = at("otok", o, [P, NBLK, D_CONV])
        NU = NBLK * HEADS
        mx, o = at("mx", o, [P, NU])
        negm, o = at("negm", o, [P, NU])
        rsum, o = at("rsum", o, [P, NU])
        esink, o = at("esink", o, [P, NU])
        rden, o = at("rden", o, [P, NU])
        osq, o = at("osq", o, [P, 3, NBLK])
        mwh, o = at("mwh", A, [P, 3, MSLOT], F32R)
        g2b, o = at("g2b", o, [P, D])
        mraw, o = at("mraw", ZONE, [P, MRING, MSLOT])
        mwl, _ = at("mwl", ZONE, [P, MRING, MSLOT], F32R)
        assert o <= VAR and Z <= ZONE + MRING // 2 * MSLOT * 4
        ye_h, o = at("ye_h", VAR, [P, D], F32R)
        ye_l, o = at("ye_l", o, [P, D], F32R)
        pick, o = at("pick", o, [P, 2, P])
        pick_r, o = at("pick_r", o, [P, 2, P], F32R)
        place, o = at("place", o, [P, SEQ], F32R)
        assert o <= RAW
        x2t_h, o = at("x2t_h", RAW, [P, 2, D], F32R)
        x2t_l, o = at("x2t_l", o, [P, 2, D], F32R)
        xg_h, o = at("xg_h", o, [P, KT, P], F32R)
        xg_l, o = at("xg_l", o, [P, KT, P], F32R)
        x2, _ = at("x2", o, [P, KT, SEQ])
        ht_h, _ = at("ht_h", o, [P, FT * P], F32R)
        htok, o = at("htok", o + KT * SEQ * 4, [P, 2, D])
        ytok, o = at("ytok", o, [P, 2, D])
        ht_l, o = at("ht_l", o, [P, FT * P], F32R)
        sg, o = at("sg", o, [P, 2, MC])
        assert o <= TMP
        hg, o = at("hg", TMP, [P, F_EXP])
        assert o <= A

        ps = stack.enter_context(nc.psum_tensor("ps", [P, 8, 512], F32))

        cos, sin = const[:, C_COS:C_COS + SEQ], const[:, C_SIN:C_SIN + SEQ]
        eps = const[:, C_EPS:C_EPS + 1]
        ident, ones = const[:, C_ID:C_ID + P], const[:, C_ONES:C_ONES + P]
        rot, bones = const[:, C_ROT:C_ROT + P], const[:, C_BONES:C_BONES + P]

        def width(layer):
            return TOK if layer == 0 else SEQ

        def modc(layer, stream, group, k):
            return mod[:, layer, stream, group * KT + k:group * KT + k + 1]

        def vcol(v):
            return vec[:, v:v + 1]

        def span(stream):
            return slice(stream * SEQ, (stream + 1) * SEQ)

        def arrived(eng, n0, i=0):
            eng.wait_ge(sem(f"raw_in{n0 % 2}"), 16 * (n0 // 2 + 1) + 16 * i)

        def split_hi(act, n0, i=0):
            s = n0 % 2
            arrived(act, n0, i)
            if n0 >= 2:
                act.wait_ge(sem("gemm_done"), n0 - 1 + 2 * i)
            act.activation(wh[:, s, :], raw[:, s, :], ACT.Copy).then_inc(sem("hi_done"), 1)

        def split_lo(dve, n0, i=0):
            s = n0 % 2
            arrived(dve, n0, i)
            dve.wait_ge(sem("hi_done"), n0 + 1 + 2 * i)
            dve.tensor_tensor(wl[:, s, :], raw[:, s, :], wh[:, s, :], ALU.subtract).then_inc(sem("lo_done"), 1)

        def load(sp, src, n0, i=0, cols=None):
            s = n0 % 2
            if n0 >= 2:
                sp.wait_ge(sem("lo_done"), n0 - 1 + 2 * i)
            sp.dma_start(raw[:, s, :].rearrange("p (k n) -> p k n", k=cols or KT), src).then_inc(
                sem(f"raw_in{s}"), 16)

        def w_in_src(layer, col):
            return w_in[layer].rearrange("(k p) n -> p k n", p=P)[:, :, bass.ts(col, CW)]

        def w_out_src(layer, col):
            return w_out[layer].rearrange("(k p) n -> p k n", p=P)[:, :, bass.ts(col, CW)]

        def up_src(w, col):
            return w[0].rearrange("(k p) n -> p k n", p=P)[:, :, bass.ts(col, CW)]

        def down_src(chunk):
            return ffn_w2[0].rearrange("(c p) n -> p c n", p=P)[:, bass.ts(chunk, 2), :]

        def in_col(j):
            return (2 * 3 + j) % IN_CH

        def product(pe, lo_hi, rhs, out_ap, first, last):
            (lh, ll), (rh, rl) = lo_hi, rhs
            pe.matmul(out_ap, lh, rh, start=first, stop=False)
            pe.matmul(out_ap, lh, rl, start=False, stop=False)
            return pe.matmul(out_ap, ll, rh, start=False, stop=last)

        def gemm_chunk(pe, n0, i, w):
            s = n0 % 2
            pe.wait_ge(sem("lo_done"), n0 + 1 + 2 * i)
            for mt in range(2):
                for k in range(KT):
                    a = k * CW + mt * P
                    last = product(pe, (wh[:, s, a:a + P], wl[:, s, a:a + P]), (xh[:, k, 0:w], xl[:, k, 0:w]),
                                   ps[:, 2 * s + mt, 0:w], k == 0, k == KT - 1)
            last.then_inc(sem("gemm_done"), 1)

        def gemm_first(pe, n0, w, ready, between=None):
            s = n0 % 2
            pe.wait_ge(sem("lo_done"), n0 + 1)
            for k in range(KT):
                if between and k == CT - 1:
                    between()
                pe.wait_ge(*ready(k))
                for mt in range(2):
                    a = k * CW + mt * P
                    last = product(pe, (wh[:, s, a:a + P], wl[:, s, a:a + P]), (xh[:, k, 0:w], xl[:, k, 0:w]),
                                   ps[:, 2 * s + mt, 0:w], k == 0, k == KT - 1)
            last.then_inc(sem("gemm_done"), 1)

        def normed(layer, norm):
            return lambda k: (sem("xl"), 2 * KT * (2 * layer + norm) + 2 * k + 2)

        ADA = [
            dict(layer=0, groups=[SH1, SC1], both=2),
            dict(layer=0, groups=[G1, SH2, SC2], both=3),
            dict(layer=0, groups=[G2], both=1),
            dict(layer=1, groups=[SH1, SC1, G1, SH2], both=2),
            dict(layer=1, groups=[SC2, G2], both=0),
        ]
        ada_base = [0, 0]
        for ph in ADA[1:]:
            ada_base.append(ada_base[-1] + KT * len(ph["groups"]))

        def sums(phase):
            ph = ADA[phase]
            return [(s, gi) for s in range(2) for gi in range(len(ph["groups"])) if s == 0 or gi < ph["both"]]

        def acc_at(phase, stream, gi):
            v = sums(phase).index((stream, gi))
            return acc_mix[:, v, :] if phase < 3 else acc[:, v + (6 if phase == 4 else 0), :]

        def ada_load(sp, phase, k0, i=0):
            ph = ADA[phase]
            n = len(ph["groups"])
            for gi, g in enumerate(ph["groups"]):
                t = ada_base[phase] + k0 * n + gi
                if t >= 2:
                    sp.wait_ge(sem("ada_used"), t - 1 + n * i)
                src = w_ada[ph["layer"]][:, g * D:(g + 1) * D]
                src = src[bass.ts(k0 + i, P), :]
                sp.dma_start(ada[:, t % 2, :], src).then_inc(sem(f"ada_in{t % 2}"), 16)

        def ada_step(dve, phase, k0, i=0, gis=None):
            ph = ADA[phase]
            n = len(ph["groups"])
            for gi in gis or range(n):
                if k0 == 0 and gi == 0 and phase < 4:
                    dve.wait_ge(sem("mod_sum"), phase)
                t = ada_base[phase] + k0 * n + gi
                dve.wait_ge(sem(f"ada_in{t % 2}"), 16 * (t // 2 + 1) + 16 * (n // 2) * i)
                if k0 > 0:
                    dve.wait_ge(sem("ada_used"), t - n + 1 + n * i)
                for s in range(2 if gi < ph["both"] else 1):
                    a = acc_at(phase, s, gi)
                    scalar = cs[:, bass.ds(k0 + i, 1), s]
                    if k0 == 0:
                        last = dve.tensor_scalar(a, ada[:, t % 2, :], scalar, None, ALU.mult)
                    else:
                        last = dve.scalar_tensor_tensor(a, ada[:, t % 2, :], scalar, a, ALU.mult, ALU.add)
                last.then_inc(sem("ada_used"), 1)

        SUM_BANK, COL_BANK = 5, 6

        def ada0_pe(pe, k):
            if k % 2 == 0:
                pe.wait_ge(sem(f"ada0_in{k // 2}"), 32)
            for b in range(4):
                last = pe.matmul(ps[0:2, b, :], cs[:, k, :], ada0[k // 4][:, k % 4, b * 512:(b + 1) * 512],
                                 start=k == 0, stop=k == KT - 1)
            if k == KT - 1:
                last.then_inc(sem("mod_sum"), 1)

        def ada0_cols(pe):
            pe.wait_ge(sem("mod_row"), 1)
            for i in range(2 * KT):
                last = pe.transpose(ps[:, COL_BANK, 2 * i:2 * i + 2], rows0[0:2, i * P:(i + 1) * P], ident[0:2, 0:2])
            last.then_inc(sem("mod_col"), 1)

        def mod_rows(pe, phase):
            pe.wait_ge(sem("ada_used"), ada_base[phase + 1])
            n = 2 * len(sums(phase))
            for v, (s, gi) in enumerate(sums(phase)):
                for half in range(2):
                    a = C_SLIDE + 15 - (2 * v + half)
                    last = pe.matmul(ps[0:n, SUM_BANK, :], const[:, a:a + n],
                                     acc_at(phase, s, gi)[:, half * 512:(half + 1) * 512],
                                     start=v == 0 and half == 0, stop=2 * v + half == n - 1)
            last.then_inc(sem("mod_sum"), 1)

        def mod_row_act(act, phase):
            act.wait_ge(sem("mod_sum"), phase + 1)
            if phase == 0:
                act.activation(rows0[:, :], ps[0:2, 0:4, :].rearrange("p a b -> p (a b)"), ACT.Copy).then_inc(
                    sem("mod_row"), 1)
                return
            n = 2 * len(sums(phase))
            act.activation(mod_row[0:n, :], ps[0:n, SUM_BANK, :], ACT.Copy).then_inc(sem("mod_row"), 1)

        def mod_cols(pe, phase):
            pe.wait_ge(sem("mod_row"), phase + 1)
            n = 2 * len(sums(phase))
            for q in range(4):
                last = pe.transpose(ps[:, COL_BANK, 16 * q:16 * q + n], mod_row[0:n, q * P:(q + 1) * P],
                                    ident[0:n, 0:n])
            last.then_inc(sem("mod_col"), 1)

        def mod_out(dve, phase):
            ph = ADA[phase]
            layer = ph["layer"]
            dve.wait_ge(sem("mod_col"), phase + 1)
            g0, g1 = ph["groups"][0], ph["groups"][-1] + 1
            for s in range(2):
                e = g1 if s == 0 else ph["groups"][0] + ph["both"]
                if e == g0:
                    continue
                dst = mod[:, layer, s, g0 * KT:e * KT]
                bias = b_ada_t[:, (layer * GROUPS + g0) * KT:(layer * GROUPS + e) * KT]
                if phase == 0:
                    src = ps[:, COL_BANK, 0:4 * KT].rearrange("p (i s) -> p s i", s=2)[:, s, :]
                else:
                    v = 2 * (g1 - g0) * s
                    src = ps[:, COL_BANK, 0:64].rearrange("p (q v) -> p v q", q=4)[:, v:v + 2 * (e - g0), :]
                    dst = dst.rearrange("p (v q) -> p v q", q=4)
                    bias = bias.rearrange("p (v q) -> p v q", q=4)
                last = dve.tensor_tensor(dst, src, bias, ALU.add)
            last.then_inc(sem("mod_out"), 1)
            dve.wait_ge(sem("mod_out"), phase + 1)
            for norm, scale, v in ((0, SC1, V_N1), (1, SC2, V_N2)):
                if scale not in ph["groups"]:
                    continue
                for s in range(1 if norm == 1 and layer == 1 else 2):
                    last = dve.scalar_tensor_tensor(
                        gain[:, layer, norm, s, :], mod[:, layer, s, scale * KT:(scale + 1) * KT], 1.0,
                        vec[:, v + layer * KT:v + (layer + 1) * KT], ALU.add, ALU.mult)
            if SC1 in ph["groups"] or SC2 in ph["groups"]:
                last.then_inc(sem("gain_out"), 1)

        NORM_BANK = 7
        norm_w = {(0, 0): TOK, (0, 1): TOK, (1, 0): TOK, (1, 1): SEQ}

        def h_ready(key, k):
            if key == (0, 0):
                return sem("h_loaded"), KT
            if key == (1, 0):
                return sem("h_ffn"), KT + k + 1
            return sem(f"h_mixed{key[0]}"), k // 2 + 1

        mods_at = {(0, 0): 1, (0, 1): 2, (1, 0): 3, (1, 1): 4}

        def norm_bank(key):
            return 0 if key == (1, 0) else NORM_BANK

        def norm_sq(act, key, k0=0, k1=KT):
            q, w = 2 * key[0] + key[1], norm_w[key]
            for k in range(k0, k1):
                act.wait_ge(*h_ready(key, k))
                if key == (0, 0):
                    if k >= 4:
                        act.wait_ge(sem("sq_used"), max(k - 4, 1))
                    act.activation(sq0[:, k % 4, :], h[:, k, 0:w], ACT.Square).then_inc(sem("sq"), 1)
                    continue
                if k >= 2:
                    act.wait_ge(sem("sq_used"), KT * q + k - 1)
                act.activation(tmp[:, k % 2, 0:w], h[:, k, 0:w], ACT.Square).then_inc(sem("sq"), 1)

        def first_sum(dve):
            for k in range(1, KT):
                dve.wait_ge(sem("sq"), k + 1)
                if k >= 2:
                    dve.wait_ge(sem("sq_used"), k - 1)
                dve.tensor_tensor(sq0_sum[:, :], sq0[:, 0, :] if k == 1 else sq0_sum[:, :], sq0[:, k % 4, :],
                                  ALU.add).then_inc(sem("sq_used"), 1)

        def first_sum_pe(pe):
            pe.wait_ge(sem("sq_used"), KT - 1)
            pe.matmul(ps[:, NORM_BANK, :], ones, sq0_sum[:, :], start=True, stop=True).then_inc(sem("sq_used"), 1)

        def norm_unit(key, u):
            return (u // 2, u % 2) if norm_w[key] == TOK else (u, 0)

        def root_act(act, key):
            q, w = 2 * key[0] + key[1], norm_w[key]
            act.wait_ge(sem("sq_used"), KT * (q + 1))
            act.activation(std[:, 0, 0:w], ps[:, norm_bank(key), 0:w], ACT.Sqrt, bias=eps, scale=1.0 / D).then_inc(
                sem("std"), 1)

        def norm_act(act, key, meanwhile=None):
            q, w = 2 * key[0] + key[1], norm_w[key]
            if key != (0, 0):
                root_act(act, key)
            if meanwhile:
                meanwhile(act)
            for u in range(KT * w // SEQ):
                k, s = norm_unit(key, u)
                act.wait_ge(sem("tn"), 2 * KT * q + u + 1)
                act.activation(x2[:, k, :] if key == (1, 1) else xh[:, k, span(s)], tmp4[:, u % 4, :], ACT.Identity,
                               bias=modc(key[0], s, 3 * key[1] + SH1, k)).then_inc(sem("xh"), 1)

        def norm_pe(pe, key, k0=0, k1=KT):
            q, w = 2 * key[0] + key[1], norm_w[key]
            for k in range(k0, k1):
                pe.wait_ge(sem("sq"), KT * q + k + 1)
                pe.matmul(ps[:, norm_bank(key), 0:w], ones, tmp[:, k % 2, 0:w], start=k == 0,
                          stop=k == KT - 1).then_inc(sem("sq_used"), 1)

        def root_dve(dve, key):
            q, w = 2 * key[0] + key[1], norm_w[key]
            dve.wait_ge(sem("std"), q + 1)
            dve.reciprocal(rstd[:, 0, 0:w], std[:, 0, 0:w]).then_inc(sem("rstd"), 1)

        def norm_dve(dve, key):
            q, w = 2 * key[0] + key[1], norm_w[key]
            layer, norm = key
            if key != (0, 0):
                root_dve(dve, key)
            dve.wait_ge(sem("rstd"), q + 1)
            dve.wait_ge(sem("gain_out"), mods_at[key])
            units = KT * w // SEQ
            for u in range(units + 2):
                if u < units:
                    k, s = norm_unit(key, u)
                    if u >= 4:
                        dve.wait_ge(sem("xh" if key == (1, 1) else "xl"), 2 * KT * q + u - 3)
                    dve.scalar_tensor_tensor(tmp4[:, u % 4, :], h[:, k, span(s)], gain[:, layer, norm, s, k:k + 1],
                                             rstd[:, 0, span(s)], ALU.mult, ALU.mult).then_inc(sem("tn"), 1)
                if u >= 2 and key != (1, 1):
                    k, s = norm_unit(key, u - 2)
                    dve.wait_ge(sem("xh"), 2 * KT * q + u - 1)
                    dve.scalar_tensor_tensor(xl[:, k, span(s)], tmp4[:, (u - 2) % 4, :],
                                             modc(layer, s, 3 * norm + SH1, k), xh[:, k, span(s)],
                                             ALU.add, ALU.subtract).then_inc(sem("xl"), 1)

        QK = CT + 1

        def qk_w(layer, j):
            return TOK if j == QK - 1 else width(layer)

        QK_SS = {2: (0, 1), 3: (2, 3), 4: (4,)}
        QK_ROT = {4: (0, 1), 5: (2, 3), 6: (4,)}
        QK_SQ = {1: (0, 1), 2: (2, 3), 3: (4,)}
        ADA_AT = {0: (0,), 1: (1,), 2: (2,), 3: (3,), 5: (4,), 6: (5,), 7: (6,), 8: (7,)}
        KD_AT, VT_AT = 7, 8

        def qk_act(act, layer, c):
            for j in QK_SS.get(c, ()):
                w = qk_w(layer, j)
                act.wait_ge(sem("qk_ss"), QK * layer + j + 1)
                if j >= 2:
                    act.wait_ge(sem("qk_rcp"), QK * layer + j - 1)
                act.activation(std[:, j % 2, 0:w], ps[:, 6 + j % 2, 0:w], ACT.Sqrt, bias=eps,
                               scale=1.0 / HD).then_inc(sem("qk_std"), 1)
            for j in QK_SQ.get(c, ()):
                w = qk_w(layer, j)
                act.wait_ge(sem(f"z{layer}"), j // 2 + 1)
                if j >= 2:
                    act.wait_ge(sem("qk_ss"), QK * layer + j - 1)
                act.activation(tmp[:, j % 2, 0:w], z[:, 12 + j, 0:w], ACT.Square).then_inc(sem("qk_sq"), 1)
            if c == KD_AT:
                for i in range(4):
                    act.wait_ge(sem("kd_ps"), 4 * layer + i + 1)
                    act.activation(kd[:, i // 2, i % 2, :], ps[:, 4 + i, :], ACT.Copy).then_inc(sem("kd"), 1)

        def qk_pe(pe, layer, c):
            for i in QK_ROT.get(c, ()):
                pe.wait_ge(sem("qk_hat"), QK * layer + i + 1)
                if i >= 2:
                    pe.wait_ge(sem("qk_rs"), QK * layer + i - 1)
                pe.matmul(ps[:, 4 + i % 2, 0:SEQ], rot, z[:, 12 + i, 0:SEQ], start=True, stop=True).then_inc(
                    sem("qk_rot"), 1)
            for j in QK_SS.get(c, ()):
                w = qk_w(layer, j)
                pe.wait_ge(sem("qk_sq"), QK * layer + j + 1)
                if j >= 2:
                    pe.wait_ge(sem("qk_std"), QK * layer + j - 1)
                pe.matmul(ps[:, 6 + j % 2, 0:w], bones, tmp[:, j % 2, 0:w], start=True, stop=True).then_inc(
                    sem("qk_ss"), 1)
            if c == KD_AT:
                pe.wait_ge(sem("qk_done"), QK * layer + QK)
                for i in range(4):
                    pe.matmul(ps[:, 4 + i, :], const[:, C_DUP + i * P:C_DUP + (i + 1) * P], z[:, 16, :],
                              start=True, stop=True).then_inc(sem("kd_ps"), 1)
            if c == VT_AT:
                pe.wait_ge(sem("kd"), 4 * layer + 3)
                for b in range(NBLK):
                    last = pe.transpose(ps[:, 6, b * P:(b + 1) * P], z[:, 17, b * P:(b + 1) * P], ident)
                last.then_inc(sem("vt_ps"), 1)

        def qk_dve(dve, layer, c):
            for j in QK_ROT.get(c, ()):
                qk_turn(dve, layer, j)
            for j in QK_SS.get(c, ()):
                qk_scale(dve, layer, j)
            if c == VT_AT:
                dve.wait_ge(sem("vt_ps"), layer + 1)
                dve.tensor_copy(vtok[:, :, :].rearrange("p b c -> p (b c)"), ps[:, 6, :]).then_inc(
                    sem("vtok"), 1)

        def qk_scale(dve, layer, j):
            w = qk_w(layer, j)
            g = vcol((V_KG if j == QK - 1 else V_QG) + layer)
            dve.wait_ge(sem("qk_std"), QK * layer + j + 1)
            dve.reciprocal(rstd[:, j % 2, 0:w], std[:, j % 2, 0:w]).then_inc(sem("qk_rcp"), 1)
            dve.wait_ge(sem("qk_rcp"), QK * layer + j + 1)
            dve.scalar_tensor_tensor(z[:, 12 + j, 0:w], z[:, 12 + j, 0:w], g, rstd[:, j % 2, 0:w], ALU.mult,
                                     ALU.mult).then_inc(sem("qk_hat"), 1)

        def qk_turn(dve, layer, j):
            lat = z[:, 12 + j, 0:SEQ]
            dve.wait_ge(sem("qk_rot"), QK * layer + j + 1)
            dve.tensor_tensor(tn[:, j % 2, :], ps[:, 4 + j % 2, 0:SEQ], sin, ALU.mult).then_inc(
                sem("qk_rs"), 1)
            dve.tensor_tensor(lat, lat, cos, ALU.mult).then_inc(sem("qk_rc"), 1)
            dve.wait_ge(sem("qk_rc"), QK * layer + j + 1)
            dve.tensor_tensor(lat, lat, tn[:, j % 2, :], ALU.add).then_inc(sem("qk_done"), 1)

        def units(layer):
            return [(hd, b) for b in range(NBLK if layer == 0 else 2) for hd in range(HEADS)]

        def unit_keys(b):
            return (0, NBLK) if b < 2 else (2, NBLK)

        def pt_sem(layer, v):
            return sem(f"pt{'ad'[v % 2]}{layer}")

        def pt_copy(eng, layer, v, out_of):
            k0, k1 = unit_keys(units(layer)[v][1])
            n = (k1 - k0) * P
            eng.wait_ge(sem(f"pt_ps{layer}"), v + 1)
            if v >= 2:
                eng.wait_ge(sem(f"o_ps{layer}"), v - 1)
            out_of(pt[:, v % 2, 0:n], ps[:, 2 + v % 2, 0:n]).then_inc(pt_sem(layer, v), 1)

        def att_pe(pe, layer):
            us = units(layer)
            pe.wait_ge(sem("kd"), 4 * layer + 4)
            for u in range(len(us) + AFTER):
                if u < len(us):
                    hd, b = us[u]
                    k0, k1 = unit_keys(b)
                    if u >= 2:
                        pe.wait_ge(sem(f"p{layer}"), u - 1)
                    s = ps[:, u % 2, 0:(k1 - k0) * P]
                    last = pe.matmul(s, z[:, 12 + hd // 2, b * P:(b + 1) * P],
                                     kd[:, hd // (HEADS // N_KV), hd % 2, k0 * P:k1 * P], start=True, stop=True)
                    if b < 2:
                        m = P * (1 - b)
                        last = pe.matmul(ps[:, u % 2, m:m + P], ident_b[:, :], mask_b[:, b, :], start=False,
                                         stop=True, skip_group_check=True)
                    last.then_inc(sem(f"s{layer}"), 1)
                if 1 <= u <= len(us):
                    v = u - 1
                    k0, k1 = unit_keys(us[v][1])
                    pe.wait_ge(sem(f"p{layer}"), v + 1)
                    if v >= 2:
                        pe.wait_ge(pt_sem(layer, v), v // 2)
                    for i in range(k1 - k0):
                        last = pe.transpose(ps[:, 2 + v % 2, i * P:(i + 1) * P], pm[:, v % 2, i * P:(i + 1) * P],
                                            ident)
                    last.then_inc(sem(f"pt_ps{layer}"), 1)
                if 2 <= u < len(us) + 2:
                    v = u - 2
                    hd, b = us[v]
                    g = hd // (HEADS // N_KV)
                    k0, k1 = unit_keys(b)
                    pe.wait_ge(pt_sem(layer, v), v // 2 + 1)
                    if v == 0:
                        pe.wait_ge(sem("vtok"), layer + 1)
                    if v >= 2:
                        pe.wait_ge(sem(f"o{layer}"), v - 1)
                    for i in range(k1 - k0):
                        last = pe.matmul(ps[:, 4 + v % 2, 0:HD], pt[:, v % 2, i * P:(i + 1) * P],
                                         vtok[:, k0 + i, g * HD:(g + 1) * HD], start=i == 0, stop=i == k1 - k0 - 1)
                    last.then_inc(sem(f"o_ps{layer}"), 1)
                if u == 2:
                    mod_cols(pe, 4 if layer else 1)
                own_norms_pe(pe, layer, u)

        def att_act(act, layer):
            us = units(layer)
            for u in range(len(us) + AFTER):
                if u < len(us):
                    hd, b = us[u]
                    k0, k1 = unit_keys(b)
                    n = (k1 - k0) * P
                    act.wait_ge(sem(f"negm{layer}"), u + 1)
                    if u >= 2:
                        act.wait_ge(sem(f"pt_ps{layer}"), u - 1)
                    act.activation(pm[:, u % 2, 0:n], ps[:, u % 2, 0:n], ACT.Exp, bias=negm[:, u:u + 1], scale=SCALE,
                                   accum_out=rsum[:, u:u + 1]).then_inc(sem(f"p{layer}"), 1)
                    i = layer * HEADS + hd
                    act.activation(esink[:, u:u + 1], nsink[:, i:i + 1], ACT.Exp, bias=negm[:, u:u + 1],
                                   scale=-1.0).then_inc(sem(f"es{layer}"), 1)
                if 1 <= u < len(us) + 1 and u % 2:
                    pt_copy(act, layer, u - 1, lambda o, i: act.activation(o, i, ACT.Copy))
                if 2 <= u < len(us) + 2:
                    v = u - 2
                    hd, b = us[v]
                    act.wait_ge(sem(f"o_ps{layer}"), v + 1)
                    act.wait_ge(sem(f"rden{layer}"), v + 1)
                    act.activation(otok[:, b, hd * HD:(hd + 1) * HD], ps[:, 4 + v % 2, 0:HD], ACT.Copy,
                                   scale=rden[:, v:v + 1]).then_inc(sem(f"o{layer}"), 1)
                own_norms_act(act, layer, u)

        def att_dve(dve, layer):
            us = units(layer)
            for u in range(len(us) + AFTER):
                if u < len(us):
                    hd, b = us[u]
                    k0, k1 = unit_keys(b)
                    dve.wait_ge(sem(f"s{layer}"), u + 1)
                    dve.tensor_reduce(mx[:, u:u + 1], ps[:, u % 2, 0:(k1 - k0) * P], AX.X, ALU.max).then_inc(
                        sem(f"mx{layer}"), 1)
                    dve.wait_ge(sem(f"mx{layer}"), u + 1)
                    i = layer * HEADS + hd
                    dve.tensor_scalar(negm[:, u:u + 1], mx[:, u:u + 1], -SCALE, nsink[:, i:i + 1], ALU.mult,
                                      ALU.min).then_inc(sem(f"negm{layer}"), 1)
                if 1 <= u < len(us) + 1:
                    v = u - 1
                    dve.wait_ge(sem(f"es{layer}"), v + 1)
                    dve.tensor_tensor(rden[:, v:v + 1], rsum[:, v:v + 1], esink[:, v:v + 1], ALU.add).then_inc(
                        sem(f"den{layer}"), 1)
                    if v % 2:
                        pt_copy(dve, layer, v, dve.tensor_copy)
                    dve.wait_ge(sem(f"den{layer}"), v + 1)
                    dve.reciprocal(rden[:, v:v + 1], rden[:, v:v + 1]).then_inc(sem(f"rden{layer}"), 1)
                if u == 2:
                    mod_out(dve, 4 if layer else 1)
                for step in range(conv_rate(layer) * u, min(conv_rate(layer) * (u + 1), 5 * CT)):
                    conv_step(dve, layer, step // 5, step % 5)
                own_norms_dve(dve, layer, u)

        def conv_rate(layer):
            return 1 if layer == 0 else 3

        def conv_step(dve, layer, t, step):
            w = width(layer)
            n = w // SEQ
            bg, u, y = z[:, t, 0:w], z[:, CT + t, 0:w], z[:, 2 * CT + t, 0:w]
            u3, y3 = u.rearrange("p (s t) -> p s t", s=n), y.rearrange("p (s t) -> p s t", s=n)
            tap = [vcol(V_CW + (layer * 3 + i) * CT + t) for i in range(3)]
            if step:
                dve.wait_ge(sem(f"cv{layer}"), 5 * t + step)
            if step == 0:
                ins = dve.tensor_tensor(u, u, y, ALU.mult)
            elif step == 1:
                ins = dve.tensor_scalar(y, u, tap[1], None, ALU.mult)
            elif step == 2:
                ins = dve.scalar_tensor_tensor(y3[:, :, 1:], u3[:, :, :-1], tap[0], y3[:, :, 1:], ALU.mult, ALU.add)
            elif step == 3:
                ins = dve.scalar_tensor_tensor(y3[:, :, :-1], u3[:, :, 1:], tap[2], y3[:, :, :-1], ALU.mult, ALU.add)
            else:
                ins = dve.tensor_tensor(y, y, bg, ALU.mult)
            ins.then_inc(sem(f"cv{layer}"), 1)

        AFTER = 7

        def conv_at(layer, u):
            return u + -5 * CT // conv_rate(layer)

        ROOT_AT = CT + 2

        def ends_block(layer, u, v):
            b, at_unit = divmod(u - v - 1, HEADS)
            return b - 1 if at_unit == 0 and 1 <= b <= width(layer) // P else None

        def block_at(layer, u, step):
            v, n = conv_at(layer, u) - ROOT_AT - 2 - step, width(layer) // P
            if ends_block(layer, u, 3 + step) == n - 1:
                return n - 1
            return {0: 0, 1: 1, 3: 2}.get(v) if {0: 0, 1: 1, 3: 2}.get(v, n) < n - 1 else None

        def turn_bank(b):
            return 6 + b % 2

        def own_norms_act(act, layer, u):
            w, v = width(layer), conv_at(layer, u)
            if 0 <= v < CT:
                act.wait_ge(sem(f"cv{layer}"), 5 * (v + 1))
                if v >= 2:
                    act.wait_ge(sem(f"cv_ss{layer}"), v - 1)
                act.activation(tmp[:, v % 2, 0:w], z[:, 2 * CT + v, 0:w], ACT.Square).then_inc(sem(f"cv_sq{layer}"), 1)
            nb = w // P
            if v == ROOT_AT:
                act.wait_ge(sem(f"cv_ss{layer}"), CT)
                act.activation(std[:, 0, 0:w], ps[:, NORM_BANK, 0:w], ACT.Sqrt, bias=eps,
                               scale=1.0 / D_CONV).then_inc(sem("cv_std"), 1)
                act.wait_ge(sem(f"osq{layer}"), nb - 1)
                act.activation(osq[:, 2, 0:nb - 1], osq[:, 0, 0:nb - 1], ACT.Sqrt, bias=eps,
                               scale=1.0 / D_CONV).then_inc(sem(f"ostd{layer}"), 1)
            if v in (CT + 6, CT + 7):
                for t in (0, 1) if v == CT + 6 else (2, 3):
                    act.wait_ge(sem(f"cv_n{layer}"), t + 1)
                    act.activation(xh[:, t, 0:w], z[:, 2 * CT + t, 0:w], ACT.Copy).then_inc(sem(f"ych{layer}"), 1)
            b = ends_block(layer, u, 0)
            if b is not None:
                act.wait_ge(sem(f"o{layer}"), HEADS * (b + 1))
                act.activation(std[:, 1, :], otok[:, b, :], ACT.Square, accum_out=osq[:, 0, b:b + 1]).then_inc(
                    sem(f"osq{layer}"), 1)
            if b == nb - 1:
                act.wait_ge(sem(f"osq{layer}"), nb)
                act.activation(osq[:, 2, b:b + 1], osq[:, 0, b:b + 1], ACT.Sqrt, bias=eps,
                               scale=1.0 / D_CONV).then_inc(sem(f"ostd{layer}"), 1)
            b = block_at(layer, u, 1)
            if b is not None:
                act.wait_ge(sem(f"ot_ps{layer}"), b + 1)
                for i in range(CT):
                    act.activation(xh[:, CT + i, b * P:(b + 1) * P], ps[:, turn_bank(b), i * P:(i + 1) * P], ACT.Copy,
                                   scale=vcol(V_GA + layer * CT + i)).then_inc(sem(f"yah{layer}"), 1)

        def own_norms_pe(pe, layer, u):
            w, v = width(layer), conv_at(layer, u)
            if 2 <= v <= CT + 1:
                t = v - 2
                pe.wait_ge(sem(f"cv_sq{layer}"), t + 1)
                pe.matmul(ps[:, NORM_BANK, 0:w], ones, tmp[:, t % 2, 0:w], start=t == 0,
                          stop=t == CT - 1).then_inc(sem(f"cv_ss{layer}"), 1)
            b = block_at(layer, u, 0)
            if b is not None and b < w // P - 1:
                block_pe(pe, layer, b)

        def block_pe(pe, layer, b):
            pe.wait_ge(sem(f"on{layer}"), b + 1)
            if b >= 2:
                pe.wait_ge(sem(f"yal{layer}"), CT * (b - 1))
            elif b == 1:
                pe.wait_ge(sem("cv_std"), layer + 1)
            else:
                pe.wait_ge(sem("mod_out"), 5 if layer else 2)
            for i in range(CT):
                last = pe.transpose(ps[:, turn_bank(b), i * P:(i + 1) * P], otok[:, b, i * P:(i + 1) * P], ident)
            last.then_inc(sem(f"ot_ps{layer}"), 1)

        def own_norms_dve(dve, layer, u):
            w, v = width(layer), conv_at(layer, u)
            if v in (CT + 3, CT + 4) and (v - CT - 3) * SEQ < w:
                s = span(v - CT - 3)
                dve.wait_ge(sem("cv_std"), layer + 1)
                dve.reciprocal(rstd[:, 0, s], std[:, 0, s]).then_inc(sem("cv_rcp"), 1)
            if v in (CT + 5, CT + 6):
                dve.wait_ge(sem("cv_rcp"), layer + 2)
                for t in (0, 1) if v == CT + 5 else (2, 3):
                    dve.scalar_tensor_tensor(z[:, 2 * CT + t, 0:w], z[:, 2 * CT + t, 0:w],
                                             vcol(V_GC + layer * CT + t), rstd[:, 0, 0:w], ALU.mult,
                                             ALU.mult).then_inc(sem(f"cv_n{layer}"), 1)
            if v in (CT + 7, CT + 8):
                for t in (0, 1) if v == CT + 7 else (2, 3):
                    dve.wait_ge(sem(f"ych{layer}"), t + 1)
                    dve.tensor_tensor(xl[:, t, 0:w], z[:, 2 * CT + t, 0:w], xh[:, t, 0:w], ALU.subtract).then_inc(
                        sem(f"ycl{layer}"), 1)
            nb = w // P
            last_block = ends_block(layer, u, 2) == nb - 1
            if v == ROOT_AT + 1 or last_block:
                b0, b1 = (nb - 1, nb) if last_block else (0, nb - 1)
                dve.wait_ge(sem(f"ostd{layer}"), 2 if last_block else 1)
                dve.reciprocal(osq[:, 1, b0:b1], osq[:, 2, b0:b1]).then_inc(sem(f"orcp{layer}"), 1)
            b = nb - 1 if last_block else v - ROOT_AT - 1
            if last_block or 0 <= b < nb - 1:
                dve.wait_ge(sem(f"orcp{layer}"), 2 if last_block else 1)
                dve.tensor_scalar(otok[:, b, :], otok[:, b, :], osq[:, 1, b:b + 1], None, ALU.mult).then_inc(
                    sem(f"on{layer}"), 1)
            b = block_at(layer, u, 2)
            if b is not None:
                dve.wait_ge(sem(f"yah{layer}"), CT * (b + 1))
                for i in range(CT):
                    dve.scalar_tensor_tensor(xl[:, CT + i, b * P:(b + 1) * P], ps[:, turn_bank(b), i * P:(i + 1) * P],
                                             vcol(V_GA + layer * CT + i), xh[:, CT + i, b * P:(b + 1) * P],
                                             ALU.mult, ALU.subtract).then_inc(sem(f"yal{layer}"), 1)

        def merged(layer):
            before = CT * (width(layer) // P - 1) - CT
            return lambda k: (sem(f"ycl{layer}"), k + 1) if k < CT else (sem(f"yal{layer}"), before + k + 1)

        R_LG, R_TOP, R_SEL1, R_SEL, R_COMB, R_RANK, R_POS, R_IDX, R_GATE, R_BOTH = range(10)

        def rt(i, b):
            return route[:, i, b, :]

        def route_pe(pe):
            pe.wait_ge(sem("xh"), 7 * KT)
            for b in range(2):
                for k in range(KT):
                    last = pe.matmul(ps[:, 6, b * EXPERTS:(b + 1) * EXPERTS], x2[:, k, b * P:(b + 1) * P],
                                     router[:, k, :], start=k == 0, stop=k == KT - 1)
            last.then_inc(sem("logits"), 1)
            pe.wait_ge(sem("htok"), 2)
            for b in range(2):
                for k in range(KT):
                    a = (k % 4) * P
                    last = pe.transpose(ps[:, 2 * b + k // 4, a:a + P], x2[:, k, b * P:(b + 1) * P], ident)
                last.then_inc(sem("x2t_ps"), 1)
            pe.wait_ge(sem("selected"), 1)
            tri = const[:, C_TRI:C_TRI + P]
            r0 = 2 * EXPERTS
            pe.matmul(ps[:, 7, r0:r0 + EXPERTS], tri, rt(R_BOTH, 0), start=True, stop=True)
            pe.matmul(ps[:, 7, r0 + EXPERTS:r0 + 2 * EXPERTS], tri, rt(R_BOTH, 1), start=True, stop=False)
            pe.matmul(ps[:, 7, r0 + EXPERTS:r0 + 2 * EXPERTS], ones, rt(R_BOTH, 0), start=False, stop=True)
            pe.matmul(ps[:, 7, 0:EXPERTS], ones, rt(R_BOTH, 0), start=True, stop=False)
            pe.matmul(ps[:, 7, 0:EXPERTS], ones, rt(R_BOTH, 1), start=False, stop=True).then_inc(sem("rank_ps"), 1)
            pe.wait_ge(sem("g2b"), 1)
            pe.wait_ge(sem("x2t_l"), 2)

        def residual_pe(pe):
            pe.wait_ge(sem("h_mixed1"), OUT_CH)
            for b in range(2):
                for k in range(KT):
                    a = (k % 4) * P
                    last = pe.transpose(ps[:, 2 * b + k // 4, a:a + P], h[:, k, b * P:(b + 1) * P], ident)
                last.then_inc(sem("h_ps"), 1)
            pe.wait_ge(sem("g2_diag"), 1)
            for k in range(KT):
                last = pe.matmul(ps[:, 4 + k // 4, (k % 4) * P:(k % 4 + 1) * P], ones, ada[:, 0, k * P:(k + 1) * P],
                                 start=True, stop=True)
            last.then_inc(sem("g2_ps"), 1)

        def residual_act(act):
            for b in range(2):
                act.wait_ge(sem("h_ps"), b + 1)
                act.activation(htok[:, b, :], ps[:, 2 * b:2 * b + 2, :].rearrange("p a b -> p (a b)"),
                               ACT.Copy).then_inc(sem("htok"), 1)

        def route_act(act):
            for b in range(2):
                act.wait_ge(sem("x2t_ps"), b + 1)
                act.activation(x2t_h[:, b, :], ps[:, 2 * b:2 * b + 2, :].rearrange("p a b -> p (a b)"),
                               ACT.Copy).then_inc(sem("x2t_h"), 1)
            act.wait_ge(sem("top"), 1)
            for b in range(2):
                last = act.activation(rt(R_GATE, b)[:, 0:1], rt(R_GATE, b)[:, 2:3], ACT.Exp)
            last.then_inc(sem("gate_exp"), 1)
            act.wait_ge(sem("g2_ps"), 1)
            act.activation(g2b[:, :], ps[:, 4:6, :].rearrange("p a b -> p (a b)"), ACT.Copy).then_inc(sem("g2b"), 1)

        route_step = [0]

        def route_dve(dve):
            def link(ins):
                route_step[0] += 1
                ins.then_inc(sem("route"), 1)
                dve.wait_ge(sem("route"), route_step[0])

            m_lo(dve, 0, 0, 0, True)
            dve.wait_ge(sem("logits"), 1)
            link(dve.tensor_copy(route[:, R_LG, :, :].rearrange("p b e -> p (b e)"), ps[:, 6, 0:2 * EXPERTS]))
            for b in range(2):
                last = dve.max(rt(R_TOP, b), rt(R_LG, b))
            link(last)
            for b in range(2):
                last = dve.tensor_tensor(rt(R_GATE, b)[:, 2:3], rt(R_TOP, b)[:, 1:2], rt(R_TOP, b)[:, 0:1],
                                         ALU.subtract)
            last.then_inc(sem("top"), 1)
            for b in range(2):
                last = dve.max_index(top_i[:, b, :], rt(R_TOP, b), rt(R_LG, b))
            link(last)
            link(dve.tensor_copy(route[:, R_IDX, :, :].rearrange("p b e -> p (b e)"),
                                 top_i[:, :, :].rearrange("p b e -> p (b e)")))
            iota_e = const[:, C_IOTA:C_IOTA + EXPERTS]
            for b in range(2):
                dve.tensor_scalar(rt(R_SEL1, b), iota_e, rt(R_IDX, b)[:, 0:1], None, ALU.is_equal)
                last = dve.tensor_scalar(rt(R_SEL, b), iota_e, rt(R_IDX, b)[:, 1:2], None, ALU.is_equal)
            link(last)
            dve.tensor_tensor(route[:, R_BOTH, :, :], route[:, R_SEL, :, :], route[:, R_SEL1, :, :],
                              ALU.add).then_inc(sem("selected"), 1)
            dve.wait_ge(sem("selected"), 1)
            link(dve.tensor_scalar(route[:, R_POS, :, :], route[:, R_BOTH, :, :], -4.0 * TOK, 4.0 * TOK, ALU.mult,
                                   ALU.add))
            for b in range(2):
                dve.wait_ge(sem("x2t_h"), b + 1)
                dve.tensor_tensor(x2t_l[:, b, :], ps[:, 2 * b:2 * b + 2, :].rearrange("p a b -> p (a b)"),
                                  x2t_h[:, b, :], ALU.subtract).then_inc(sem("x2t_l"), 1)
            dve.wait_ge(sem("rank_ps"), 1)
            link(dve.tensor_tensor(route[:, R_POS, :, :].rearrange("p b e -> p (b e)"),
                                   route[:, R_POS, :, :].rearrange("p b e -> p (b e)"),
                                   ps[:, 7, 2 * EXPERTS:4 * EXPERTS], ALU.add))
            dve.tensor_reduce(most[:, :], ps[:, 7, 0:EXPERTS], AX.X, ALU.max).then_inc(sem("most"), 1)

        def gates_dve(dve):
            def link(ins):
                route_step[0] += 1
                ins.then_inc(sem("route"), 1)
                dve.wait_ge(sem("route"), route_step[0])

            dve.wait_ge(sem("gate_exp"), 1)
            for b in range(2):
                last = dve.tensor_scalar(rt(R_GATE, b)[:, 1:2], rt(R_GATE, b)[:, 0:1], 1.0, None, ALU.add)
            link(last)
            for b in range(2):
                last = dve.reciprocal(rt(R_GATE, b)[:, 3:4], rt(R_GATE, b)[:, 1:2])
            link(last)
            for b in range(2):
                last = dve.tensor_tensor(rt(R_GATE, b)[:, 4:5], rt(R_GATE, b)[:, 3:4], rt(R_GATE, b)[:, 0:1], ALU.mult)
            link(last)
            for b in range(2):
                last = dve.tensor_scalar(rt(R_COMB, b), rt(R_SEL, b), rt(R_GATE, b)[:, 4:5], None, ALU.mult)
            link(last)
            for b in range(2):
                last = dve.scalar_tensor_tensor(rt(R_COMB, b), rt(R_SEL1, b), rt(R_GATE, b)[:, 3:4], rt(R_COMB, b),
                                                ALU.mult, ALU.add)
            link(last)

        def experts(eng, q, body):
            body(0, True, False)
            with eng.Fori(0, EXPERTS - 2) as i:
                body(1 + i, False, False)
            body(EXPERTS - 1, False, True)

        def m_slot(j):
            return (j + MRING // 2) % MRING

        def m_load(sp, q, e, j, first):
            g = e + EXPERTS * q
            s = m_slot(j)
            n = MCH * g + j
            if not first or j >= MRING:
                sp.wait_ge(sem("mgemm"), n - MRING + 1)
            elif q == 0 and j == 0:
                sp.wait_ge(sem("ycl1"), CT)
                sp.wait_ge(sem("yal1"), 2 * CT)
            elif q == 0 and j == MRING // 2:
                sp.wait_ge(sem("gemm_done"), CHUNKS)
            if j < 8:
                dst = mraw[:, s, :].rearrange("p (k w n) -> p k w n", k=KT, w=2)
                for w, src in enumerate((moe_w1, moe_w3)):
                    sp.dma_start(dst[:, :, w, :], src.rearrange("a e (k p) n -> p (a e k) n", p=P)[
                        :, bass.ts(e, KT), j * MC:(j + 1) * MC]).then_inc(sem(f"mraw{s}"), 16)
            else:
                dst = mraw[:, s, :].rearrange("p (k n) -> p k n", k=FT)
                src = moe_w2.rearrange("a e (k p) n -> p (a e k) n", p=P)
                for k0, k1 in ((0, 6), (6, FT)):
                    sp.dma_start(dst[:, k0:k1, :], src[:, bass.ds(e * FT + k0, k1 - k0),
                                                       (j - 8) * CW:(j - 7) * CW]).then_inc(sem(f"mraw{s}"), 16)

        def m_arrived(eng, q, e, j):
            g = e + EXPERTS * q
            eng.wait_ge(sem(f"mraw{m_slot(j)}"), 32 * (g * (MCH // MRING) + j // MRING + 1))

        def m_hi(act, q, e, j, first):
            g = e + EXPERTS * q
            s = j % 3
            m_arrived(act, q, e, j)
            if not first or j >= 3:
                act.wait_ge(sem("mgemm"), MCH * g + j - 2)
            act.activation(mwh[:, s, :], mraw[:, m_slot(j), :], ACT.Copy).then_inc(sem("mhi"), 1)

        def m_lo(dve, q, e, j, first):
            g = e + EXPERTS * q
            s = j % 3
            m_arrived(dve, q, e, j)
            dve.wait_ge(sem("mhi"), MCH * g + j + 1)
            dve.tensor_tensor(mwl[:, m_slot(j), :], mraw[:, m_slot(j), :], mwh[:, s, :], ALU.subtract).then_inc(sem("mlo"), 1)

        def gather(pe, q, e):
            g = e + EXPERTS * q
            pe.wait_ge(sem("pick"), g + 1)
            for m in range(KT):
                o = ps[:, 4 + m // 4, (m % 4) * P:(m % 4 + 1) * P]
                for b in range(2):
                    for i, part in enumerate((x2t_h, x2t_l)):
                        last = pe.matmul(o, part[:, b, m * P:(m + 1) * P], pick_r[:, b, :], start=b == 0 and i == 0,
                                         stop=b == 1 and i == 1)
            last.then_inc(sem("xg_ps"), 1)

        def put_back(pe, q, e):
            g = e + EXPERTS * q
            pe.wait_ge(sem("ye_l"), g + 1)
            pe.wait_ge(sem("place"), g + 1)
            for b in range(2):
                for half in range(2):
                    o = ps[:, 2 + 2 * b + half, :]
                    pe.matmul(o, place[:, b * P:(b + 1) * P], ye_h[:, half * 512:(half + 1) * 512], start=True,
                              stop=False)
                    pe.matmul(o, place[:, b * P:(b + 1) * P], ye_l[:, half * 512:(half + 1) * 512], start=False,
                              stop=True).then_inc(sem("put"), 1)

        def hidden_t(pe, k0, k1):
            for k in range(k0, k1):
                bank = (2, 3, 0)[k // 4]
                last = pe.transpose(ps[:, bank, (k % 4) * P:(k % 4 + 1) * P], hg[:, k * P:(k + 1) * P], ident)
            last.then_inc(sem("ht_ps"), 1)

        def m_pe(pe, q, e, first, last_e):
            g = e + EXPERTS * q
            for j in range(8):
                s = j % 3
                pe.wait_ge(sem("mlo"), MCH * g + j + 1)
                if j == 0:
                    pe.wait_ge(sem("xg_l"), g + 1)
                if j >= 2:
                    pe.wait_ge(sem("hg"), 8 * g + j - 1)
                for k in range(KT):
                    a = k * 2 * MC
                    last = product(pe, (xg_h[:, k, :], xg_l[:, k, :]),
                                   (mwh[:, s, a:a + 2 * MC], mwl[:, m_slot(j), a:a + 2 * MC]), ps[:, j % 2, 0:2 * MC],
                                   k == 0, k == KT - 1)
                last.then_inc(sem("mgemm"), 1)
                if j == 1 and not first:
                    put_back(pe, q, e - 1)
                if j == 3:
                    if first:
                        pe.wait_ge(sem("pick"), 1)
                    else:
                        pe.wait_ge(sem("yacc"), 4 * g + 4)
                    for b in range(2):
                        last = pe.transpose(ps[:, 2, b * P:(b + 1) * P], pick[:, b, :], ident)
                    last.then_inc(sem("place_ps"), 1)
                if j == 6:
                    pe.wait_ge(sem("hg"), 8 * g + 6)
                    pe.wait_ge(sem("place"), g + 1)
                    hidden_t(pe, 0, 8)
            if not last_e:
                gather(pe, q, e + 1)
            pe.wait_ge(sem("ht_l"), 2 * g + 1)
            for c4 in range(4):
                s = (8 + c4) % 3
                pe.wait_ge(sem("mlo"), MCH * g + 9 + c4)
                for k in range(FT):
                    if c4 == 0 and k == 8:
                        pe.wait_ge(sem("ht_l"), 2 * g + 2)
                    elif c4 == 0 and k == 4:
                        pe.wait_ge(sem("hg"), 8 * g + 8)
                        hidden_t(pe, 8, FT)
                    last = product(pe, (ht_h[:, k * P:(k + 1) * P], ht_l[:, k * P:(k + 1) * P]),
                                   (mwh[:, s, k * CW:(k + 1) * CW],
                                    mwl[:, m_slot(8 + c4), k * CW:(k + 1) * CW]),
                                   ps[:, 6 + c4 // 2, (c4 % 2) * CW:(c4 % 2 + 1) * CW], k == 0, k == FT - 1)
                last.then_inc(sem("mgemm"), 1)
            if last_e:
                put_back(pe, q, e)

        def m_act(act, q, e, first, last_e):
            g = e + EXPERTS * q
            for j in range(8):
                m_hi(act, q, e, j + 2, first)
                if j == 5:
                    act.wait_ge(sem("place_ps"), g + 1)
                    act.activation(place[:, :], ps[:, 2, 0:SEQ], ACT.Copy).then_inc(sem("place"), 1)
                if j == 7:
                    act.wait_ge(sem("ht_ps"), 2 * g + 1)
                    act.activation(ht_h[:, 0:8 * P], ps[:, 2:4, :].rearrange("p a b -> p (a b)"),
                                   ACT.Copy).then_inc(sem("ht_h"), 1)
                act.wait_ge(sem("mgemm"), MCH * g + j + 1)
                if not first or j >= 2:
                    act.wait_ge(sem("hg"), 8 * g + j - 1)
                act.activation(sg[:, j % 2, :], ps[:, j % 2, 0:MC], ACT.Silu).then_inc(sem("sg"), 1)
            act.wait_ge(sem("ht_ps"), 2 * g + 2)
            act.activation(ht_h[:, 8 * P:FT * P], ps[:, 0, 0:(FT - 8) * P], ACT.Copy).then_inc(sem("ht_h"), 1)
            if not last_e:
                xg_act(act, q, e + 1)
            for j in range(10, MCH + 2):
                if j < MCH:
                    m_hi(act, q, e, j, first)
                elif not last_e:
                    m_hi(act, q, e + 1, j - MCH, False)
            act.wait_ge(sem("mgemm"), MCH * g + MCH)
            act.activation(ye_h[:, :], ps[:, 6:8, :].rearrange("p a b -> p (a b)"), ACT.Copy).then_inc(
                sem("ye_h"), 1)

        def xg_act(act, q, e):
            g = e + EXPERTS * q
            act.wait_ge(sem("xg_ps"), g + 1)
            act.activation(xg_h[:, :, :].rearrange("p k s -> p (k s)"),
                           ps[:, 4:6, :].rearrange("p a b -> p (a b)"), ACT.Copy).then_inc(sem("xg_h"), 1)

        def xg_dve(dve, q, e):
            g = e + EXPERTS * q
            dve.wait_ge(sem("xg_h"), g + 1)
            dve.tensor_tensor(xg_l[:, :, :].rearrange("p k s -> p (k s)"),
                              ps[:, 4:6, :].rearrange("p a b -> p (a b)"),
                              xg_h[:, :, :].rearrange("p k s -> p (k s)"), ALU.subtract).then_inc(sem("xg_l"), 1)

        def pick_dve(dve, q, e):
            g = e + EXPERTS * q
            iota = const[:, C_IOTA:C_IOTA + P]
            for b in range(2):
                pos = route[:, R_POS, b, bass.ds(e, 1)]
                dve.tensor_scalar(pick[:, b, :], iota, pos, None, ALU.is_equal)
                last = dve.tensor_scalar(pick_r[:, b, :], iota, pos, None, ALU.is_equal)
            last.then_inc(sem("pick"), 1)

        def sum_dve(dve, q, e):
            g = e + EXPERTS * q
            for b in range(2):
                for half in range(2):
                    i = 2 * b + half
                    dve.wait_ge(sem("put"), 4 * g + i + 1)
                    dve.wait_ge(sem("yacc"), 4 * g + 1 + i)
                    y = ytok[:, b, half * 512:(half + 1) * 512]
                    dve.scalar_tensor_tensor(y, ps[:, 2 + i, :], route[:, R_COMB, b, bass.ds(e, 1)], y, ALU.mult,
                                             ALU.add).then_inc(sem("yacc"), 1)

        def m_dve(dve, q, e, first, last_e):
            g = e + EXPERTS * q
            for j in range(8):
                m_lo(dve, q, e, j + 2, first)
                dve.wait_ge(sem("sg"), 8 * g + j + 1)
                dve.tensor_tensor(hg[:, j * MC:(j + 1) * MC], sg[:, j % 2, :], ps[:, j % 2, MC:2 * MC],
                                  ALU.mult).then_inc(sem("hg"), 1)
                if j == 1 and not first:
                    sum_dve(dve, q, e - 1)
                if j == 5 and not last_e:
                    pick_dve(dve, q, e + 1)
            dve.wait_ge(sem("ht_h"), 2 * g + 1)
            dve.tensor_tensor(ht_l[:, 0:8 * P], ps[:, 2:4, :].rearrange("p a b -> p (a b)"),
                              ht_h[:, 0:8 * P], ALU.subtract).then_inc(sem("ht_l"), 1)
            dve.wait_ge(sem("ht_h"), 2 * g + 2)
            dve.tensor_tensor(ht_l[:, 8 * P:FT * P], ps[:, 0, 0:(FT - 8) * P], ht_h[:, 8 * P:FT * P],
                              ALU.subtract).then_inc(sem("ht_l"), 1)
            if not last_e:
                xg_dve(dve, q, e + 1)
            for j in range(10, MCH + 2):
                if j < MCH:
                    m_lo(dve, q, e, j, first)
                elif not last_e:
                    m_lo(dve, q, e + 1, j - MCH, False)
            dve.wait_ge(sem("ye_h"), g + 1)
            dve.tensor_tensor(ye_l[:, :], ps[:, 6:8, :].rearrange("p a b -> p (a b)"), ye_h[:, :],
                              ALU.subtract).then_inc(sem("ye_l"), 1)
            if last_e:
                sum_dve(dve, q, e)

        def pass_sp(sp, q):
            experts(sp, q, lambda e, first, last: [m_load(sp, q, e, j, first) for j in range(MCH)] and None)

        def pass_pe(pe, q):
            gather(pe, q, 0)
            experts(pe, q, lambda e, first, last: m_pe(pe, q, e, first, last))

        def pass_act(act, q):
            if q:
                m_hi(act, q, 0, 0, True)
            m_hi(act, q, 0, 1, True)
            xg_act(act, q, 0)
            experts(act, q, lambda e, first, last: m_act(act, q, e, first, last))

        def pass_dve(dve, q):
            pick_dve(dve, q, 0)
            if q:
                m_lo(dve, q, 0, 0, True)
            else:
                gates_dve(dve)
            m_lo(dve, q, 0, 1, True)
            xg_dve(dve, q, 0)
            experts(dve, q, lambda e, first, last: m_dve(dve, q, e, first, last))

        def overflow(eng):
            eng.wait_ge(sem("most"), 1)
            return eng.value_load(most[0:1, 0:1], min_val=0, max_val=SEQ) > P

        block = stack.enter_context(nc.Block())
        PARTS = [(0, PART), (PART, FF_CH)]

        @block.sync
        def _(sp):
            sp.dma_start(const[:, :], table).then_inc(sem("table_in"), 16)
            for b in range(2):
                sp.dma_start(xin[:, b, :], x[0].rearrange("(b p) d -> b p d", p=P)[b]).then_inc(sem("x_in"), 16)
                sp.dma_start(xin[:, 2 + b, :], ctx[0].rearrange("(b p) d -> b p d", p=P)[b]).then_inc(
                    sem("x_in"), 16)
            sp.wait_ge(sem("params_in"), 14 * 16)
            for k in range(KT):
                sp.dma_start(ada0[k // 4][:, k % 4, :], w_ada[0][k * P:(k + 1) * P, 0:2 * D]).then_inc(
                    sem(f"ada0_in{k // 2}"), 16)
            n = first_chunk[0, "in"]
            load(sp, w_in_src(0, in_col(0)), n)
            for j in range(1, IN_CH):
                load(sp, w_in_src(0, in_col(j)), n + j)
            for j in range(OUT_CH):
                load(sp, w_out_src(0, j), first_chunk[0, "out"] + j)
            for part, (c0, c1) in enumerate(PARTS):
                n = first_chunk[0, f"up{part}"]
                load(sp, up_src(ffn_w1, c0), n)
                with sp.Fori(0, c1 - c0 - 1) as i:
                    load(sp, up_src(ffn_w3, c0 + i), n + 1, i)
                    load(sp, up_src(ffn_w1, c0 + 1 + i), n + 2, i)
                load(sp, up_src(ffn_w3, c1 - 1), n + 2 * (c1 - c0) - 1)
                n = first_chunk[0, f"down{part}"]
                for j in range(c1 - c0):
                    load(sp, down_src(c0 + j), n + j, cols=2)
            n = first_chunk[1, "in"]
            for j in range(IN_CH):
                load(sp, w_in_src(1, in_col(j)), n + j)
            for j in range(OUT_CH):
                load(sp, w_out_src(1, j), first_chunk[1, "out"] + j)

            pass_sp(sp, 0)
            with sp.If(overflow(sp)):
                sp.wait_ge(sem("yacc"), 4 * EXPERTS + 4)
                pass_sp(sp, 1)
            for b in range(2):
                sp.wait_ge(sem("result"), b + 1)
                sp.dma_start(out[0].rearrange("(b p) d -> b p d", p=P)[b], ytok[:, b, :]).then_inc(sem("stored"), 16)
            sp.wait_ge(sem("stored"), 32)

        @block.tensor
        def _(pe):
            pe.wait_ge(sem("table_in"), 16)
            pe.wait_ge(sem("params_in"), 14 * 16)
            pe.transpose(ps[:, 0, 0:V_ROWS], rows_b[0:V_ROWS, :], const[0:V_ROWS, C_ID:C_ID + V_ROWS])
            n = DEPTH * GROUPS * KT
            pe.transpose(ps[:, 0, P:P + n], rows_a[0:n, :], const[0:n, C_ID:C_ID + n])
            pe.matmul(ps[:, 0, 2 * P:2 * P + DEPTH * HEADS], const[0:1, C_ONES:C_ONES + P], sink_row[0:1, :],
                      start=True, stop=True).then_inc(sem("params_ps"), 1)
            pe.wait_ge(sem("x_in"), 64)
            pe.wait_ge(sem("params_out"), 3)
            for k in range(KT):
                for b in range(NBLK):
                    last = pe.transpose(ps[:, k, b * P:(b + 1) * P], xin[:, b, k * P:(k + 1) * P], ident)
                last.then_inc(sem("x_ps"), 1)
            pe.wait_ge(sem("h_loaded"), KT)
            for k in range(KT):
                ada0_pe(pe, k)
                if k == KT // 2 - 1:
                    first_sum_pe(pe)
            ada0_cols(pe)
            for layer in range(DEPTH):
                w = width(layer)
                n = first_chunk[layer, "in"]
                for j in range(IN_CH):
                    if j >= 2:
                        pe.wait_ge(sem(f"z{layer}"), j - 1)
                    if j == 0:
                        gemm_first(pe, n, w, normed(layer, 0))
                    else:
                        gemm_chunk(pe, n + j, 0, TOK if j == 2 else w)
                    qk_pe(pe, layer, j)
                if layer == 0:
                    pe.wait_ge(sem("kd"), 2)
                    mod_rows(pe, 1)
                pe.wait_ge(sem(f"z{layer}"), IN_CH)
                att_pe(pe, layer)
                n = first_chunk[layer, "out"]
                for j in range(OUT_CH):
                    if j >= 2:
                        pe.wait_ge(sem(f"h_mixed{layer}"), j - 1)
                    if j == 0:
                        gemm_first(pe, n, w, merged(layer), lambda: block_pe(pe, layer, w // P - 1))
                    else:
                        gemm_chunk(pe, n + j, 0, w)
                    if j >= 1:
                        norm_pe(pe, (layer, 1), 2 * j - 2, 2 * j)
                norm_pe(pe, (layer, 1), KT - 2, KT)
                if layer == 0:
                    mod_rows(pe, 2)
                    for part, (c0, c1) in enumerate(PARTS):
                        n = first_chunk[0, f"up{part}"]

                        def pair(i, first):
                            n1 = n if first else n + 2
                            if c0 or not first:
                                pe.wait_ge(sem("silu"), c0 + (0 if first else 1) + i)
                            if c0 and first:
                                pe.wait_ge(sem("h_ffn"), 4)
                            if c0 == 0 and first:
                                gemm_first(pe, n1, TOK, normed(0, 1))
                            else:
                                gemm_chunk(pe, n1, i, TOK)
                            if c0 or not first:
                                pe.wait_ge(sem("glu"), c0 + (0 if first else 1) + i)
                            gemm_chunk(pe, n1 + 1, i, TOK)

                        if part:
                            pe.wait_ge(sem("h_ffn"), KT)
                            mod_rows(pe, 3)
                        pair(0, True)
                        mod_cols(pe, 2 + part)
                        with pe.Fori(0, c1 - c0 - 1) as i:
                            pair(i, False)
                        n = first_chunk[0, f"down{part}"]
                        pe.wait_ge(sem("mod_out"), 3 + part)
                        for j in range(c1 - c0):
                            s = (n + j) % 2
                            pe.wait_ge(sem("lo_done"), n + j + 1)
                            pe.wait_ge(sem("hid"), c0 + j + 1)
                            for m0 in ((4, 0) if j == 0 else (0,)):
                                m1 = KT if m0 or j else 4
                                if j == 0 and m0 == 0:
                                    pe.wait_ge(sem("glu"), c1)
                                for r in range(2):
                                    for m in range(m0, m1):
                                        a = r * D + m * P
                                        end = j == c1 - c0 - 1 and r == 1
                                        last = product(pe, (wh[:, s, a:a + P], wl[:, s, a:a + P]),
                                                       (hid_h[:, 2 * j + r, :], hid_l[:, 2 * j + r, :]), ps[:, m, :],
                                                       j == 0 and r == 0, end)
                                        if end and m < KT - 1:
                                            last.then_inc(sem("down"), 1)
                            last.then_inc(sem("gemm_done"), 1)
                    norm_pe(pe, (1, 0))
                    pe.wait_ge(sem("h_ffn"), 2 * KT)
                    mod_rows(pe, 4)
            residual_pe(pe)
            route_pe(pe)
            pass_pe(pe, 0)
            with pe.If(overflow(pe)):
                pe.wait_ge(sem("yacc"), 4 * EXPERTS + 4)
                pass_pe(pe, 1)

        @block.scalar
        def _(act):
            for dst, src in (
                (rows_b[V_C:V_C + KT, :], c.rearrange("b (k p) -> (b k) p", p=P)),
                (rows_b[V_CC:V_CC + KT, :], c_ctx.rearrange("(k p) -> k p", p=P)),
                (rows_b[V_N1:V_N1 + DEPTH * KT, :], norm1_g.rearrange("l (k p) -> (l k) p", p=P)),
                (rows_b[V_N2:V_N2 + DEPTH * KT, :], norm2_g.rearrange("l (k p) -> (l k) p", p=P)),
                (rows_b[V_GC:V_GC + DEPTH * CT, :], out_norm_conv_g.rearrange("l (k p) -> (l k) p", p=P)),
                (rows_b[V_GA:V_GA + DEPTH * CT, :], out_norm_attn_g.rearrange("l (k p) -> (l k) p", p=P)),
                (rows_b[V_CW:V_CW + DEPTH * 3 * CT, :], conv_w.rearrange("l t (k p) -> (l t k) p", p=P)),
                (rows_b[V_QG:V_QG + DEPTH, 0:HD], q_norm_g),
                (rows_b[V_QG:V_QG + DEPTH, HD:P], q_norm_g),
                (rows_b[V_KG:V_KG + DEPTH, 0:HD], k_norm_g),
                (rows_b[V_KG:V_KG + DEPTH, HD:P], k_norm_g),
                (rows_a[0:DEPTH * GROUPS * KT, :], b_ada.rearrange("l (k p) -> (l k) p", p=P)),
                (sink_row[0:1, :], attn_sink.rearrange("(a l) h -> a (l h)", a=1)),
                (router[:, :, :], moe_router[0].rearrange("(k p) e -> p k e", p=P)),
            ):
                act.dma_start(dst, src).then_inc(sem("params_in"), 16)
            act.wait_ge(sem("params_ps"), 1)
            act.activation(cs[:, :, :].rearrange("p k s -> p s k"),
                           ps[:, 0, V_C:V_C + 2 * KT].rearrange("p (s k) -> p s k", s=2), ACT.Silu).then_inc(
                sem("cs"), 1)
            for k in range(0, KT, 2):
                act.wait_ge(sem("x_ps"), k + 1)
                act.activation(h[:, k, :], ps[:, k, :], ACT.Copy).then_inc(sem("h_loaded"), 1)
            norm_sq(act, (0, 0))
            root_act(act, (0, 0))
            split_hi(act, 0)
            mod_row_act(act, 0)
            norm_act(act, (0, 0))
            for layer in range(DEPTH):
                w = width(layer)
                n = first_chunk[layer, "in"]

                def z_out(act, n0, col, w):
                    act.wait_ge(sem("gemm_done"), n0 + 1)
                    b = 2 * (n0 % 2)
                    act.activation(z[:, 2 * col:2 * col + 2, 0:w], ps[:, b:b + 2, 0:w], ACT.Copy).then_inc(
                        sem(f"z{layer}"), 1)

                for j in range(IN_CH):
                    split_hi(act, n + j + 1)
                    z_out(act, n + j, in_col(j), TOK if j == 2 else w)
                    qk_act(act, layer, j)
                if layer == 0:
                    mod_row_act(act, 1)
                att_act(act, layer)
                n = first_chunk[layer, "out"]
                for j in range(OUT_CH):
                    if j < OUT_CH - 1 or layer == 0:
                        split_hi(act, n + j + 1)
                    if j >= 1:
                        norm_sq(act, (layer, 1), 2 * j - 2, 2 * j)
                norm_sq(act, (layer, 1), KT - 2, KT)
                norm_act(act, (layer, 1), residual_act if layer else None)
                if layer:
                    m_hi(act, 0, 0, 0, True)
                if layer == 0:
                    for part, (c0, c1) in enumerate(PARTS):
                        n = first_chunk[0, f"up{part}"]

                        def pair(i, n0, p):
                            split_hi(act, n0 + 1, i)
                            act.wait_ge(sem("gemm_done"), n0 + 1 + 2 * i)
                            if p:
                                act.wait_ge(sem("hid"), p + i)
                            b1 = 2 * (n0 % 2)
                            act.activation(tmp[:, :, :], ps[:, b1:b1 + 2, :], ACT.Silu).then_inc(sem("silu"), 1)
                            split_hi(act, n0 + 2, i)
                            act.wait_ge(sem("glu"), p + 1 + i)
                            act.activation(hid_h[:, bass.ts(p - c0 + i, 2), :], tmp[:, :, :], ACT.Copy).then_inc(
                                sem("hid_h"), 1)

                        mod_row_act(act, 2 + part)
                        pair(0, n, c0)
                        with act.Fori(0, c1 - c0 - 1) as i:
                            pair(i, n + 2, c0 + 1)
                        n = first_chunk[0, f"down{part}"]
                        for j in range(c1 - c0):
                            split_hi(act, n + j + 1)
                    norm_sq(act, (1, 0))
                    norm_act(act, (1, 0))
                    mod_row_act(act, 4)
            route_act(act)
            pass_act(act, 0)
            with act.If(overflow(act)):
                act.wait_ge(sem("yacc"), 4 * EXPERTS + 4)
                pass_act(act, 1)

        @block.vector
        def _(dve):
            dve.wait_ge(sem("params_ps"), 1)
            dve.wait_ge(sem("cs"), 1)
            dve.tensor_copy(vec[:, :], ps[:, 0, 0:V_ROWS]).then_inc(sem("params_out"), 1)
            dve.tensor_copy(b_ada_t[:, :], ps[:, 0, P:P + DEPTH * GROUPS * KT]).then_inc(sem("params_out"), 1)
            dve.tensor_scalar(nsink[:, :], ps[:, 0, 2 * P:2 * P + DEPTH * HEADS], -1.0, None, ALU.mult).then_inc(
                sem("params_out"), 1)
            dve.tensor_copy(ident_b[:, :], ident).then_inc(sem("masks"), 1)
            dve.tensor_copy(mask_b[:, :, :].rearrange("p a b -> p (a b)"), const[:, C_MASK:C_MASK + 2 * P]).then_inc(
                sem("masks"), 1)
            for k in range(1, KT, 2):
                dve.wait_ge(sem("x_ps"), k + 1)
                dve.tensor_copy(h[:, k, :], ps[:, k, :]).then_inc(sem("h_loaded"), 1)
            first_sum(dve)
            root_dve(dve, (0, 0))
            split_lo(dve, 0)
            mod_out(dve, 0)
            norm_dve(dve, (0, 0))
            for layer in range(DEPTH):
                w = width(layer)
                n = first_chunk[layer, "in"]
                for j in range(IN_CH):
                    split_lo(dve, n + j + 1)
                    for k in ADA_AT.get(j, ()) if layer == 0 else ():
                        ada_step(dve, 1, k)
                    qk_dve(dve, layer, j)
                dve.wait_ge(sem(f"z{layer}"), IN_CH)
                att_dve(dve, layer)
                n = first_chunk[layer, "out"]
                for j in range(OUT_CH):
                    if j < OUT_CH - 1 or layer == 0:
                        split_lo(dve, n + j + 1)
                    if layer == 0:
                        ada_step(dve, 2, 2 * j)
                        ada_step(dve, 2, 2 * j + 1)
                    dve.wait_ge(sem("gemm_done"), n + j + 1)
                    for mt in range(2):
                        m = 2 * j + mt
                        for s in range(w // SEQ):
                            last = dve.scalar_tensor_tensor(
                                h[:, m, span(s)], ps[:, 2 * ((n + j) % 2) + mt, span(s)], modc(layer, s, G1, m),
                                h[:, m, span(s)], ALU.mult, ALU.add)
                    last.then_inc(sem(f"h_mixed{layer}"), 1)
                if layer:
                    for k in range(KT):
                        last = dve.tensor_scalar(ada[:, 0, k * P:(k + 1) * P], ident, modc(1, 0, G2, k), None,
                                                 ALU.mult)
                    last.then_inc(sem("g2_diag"), 1)
                norm_dve(dve, (layer, 1))
                if layer == 0:
                    for part, (c0, c1) in enumerate(PARTS):
                        n = first_chunk[0, f"up{part}"]

                        def pair(i, n0, p):
                            split_lo(dve, n0 + 1, i)
                            k = p - c0
                            if part == 0:
                                ada_step(dve, 3, k, i, (0, 1))
                            else:
                                ada_step(dve, 4, k, i, (0,))
                            split_lo(dve, n0 + 2, i)
                            if part == 0:
                                ada_step(dve, 3, k, i, (2, 3))
                            else:
                                ada_step(dve, 4, k, i, (1,))
                            dve.wait_ge(sem("silu"), p + 1 + i)
                            dve.wait_ge(sem("gemm_done"), n0 + 2 + 2 * i)
                            b3 = 2 * ((n0 + 1) % 2)
                            dve.tensor_tensor(tmp[:, :, :], tmp[:, :, :], ps[:, b3:b3 + 2, :], ALU.mult).then_inc(
                                sem("glu"), 1)
                            dve.wait_ge(sem("hid_h"), p + 1 + i)
                            dve.tensor_tensor(hid_l[:, bass.ts(p - c0 + i, 2), :], tmp[:, :, :],
                                              hid_h[:, bass.ts(p - c0 + i, 2), :], ALU.subtract).then_inc(
                                sem("hid"), 1)

                        pair(0, n, c0)
                        mod_out(dve, 2 + part)
                        with dve.Fori(0, c1 - c0 - 1) as i:
                            pair(i, n + 2, c0 + 1)
                        n = first_chunk[0, f"down{part}"]
                        for j in range(c1 - c0):
                            split_lo(dve, n + j + 1)
                            if part == 0 and j < 2 * (KT - c1 + c0):
                                ada_step(dve, 3, c1 - c0 + j // 2, 0, ((0, 1), (2, 3))[j % 2])
                            if part == 1 and c1 - c0 + j < KT:
                                ada_step(dve, 4, c1 - c0 + j)
                        for m in range(KT):
                            if m < KT - 1:
                                dve.wait_ge(sem("down"), part * (KT - 1) + m + 1)
                            else:
                                dve.wait_ge(sem("gemm_done"), n + c1 - c0)
                            for s in range(2):
                                last = dve.scalar_tensor_tensor(h[:, m, span(s)], ps[:, m, span(s)],
                                                                modc(0, s, G2, m), h[:, m, span(s)], ALU.mult,
                                                                ALU.add)
                            last.then_inc(sem("h_ffn"), 1)
                    norm_dve(dve, (1, 0))
            route_dve(dve)
            dve.wait_ge(sem("yacc"), 4)
            pass_dve(dve, 0)
            with dve.If(overflow(dve)):
                dve.wait_ge(sem("yacc"), 4 * EXPERTS + 4)
                dve.tensor_scalar(route[:, R_POS, :, :], route[:, R_POS, :, :], -float(P), None,
                                  ALU.add).then_inc(sem("shifted"), 1)
                dve.wait_ge(sem("shifted"), 1)
                pass_dve(dve, 1)
                dve.wait_ge(sem("yacc"), 8 * EXPERTS + 4)
            dve.wait_ge(sem("htok"), 2)
            dve.wait_ge(sem("yacc"), 4 * EXPERTS + 4)
            for b in range(2):
                dve.tensor_tensor(ytok[:, b, :], ytok[:, b, :], g2b[:, :], ALU.mult).then_inc(sem("gated"), 1)
            for b in range(2):
                dve.wait_ge(sem("gated"), b + 1)
                dve.tensor_tensor(ytok[:, b, :], ytok[:, b, :], htok[:, b, :], ALU.add).then_inc(sem("result"), 1)

        @block.gpsimd
        def _(pool):
            pool.wait_ge(sem("ada0_in3"), 32)
            for phase in (1, 2):
                for k in range(KT):
                    ada_load(pool, phase, k)
            for phase in (3, 4):
                with pool.Fori(0, KT) as i:
                    ada_load(pool, phase, 0, i)
            pool.wait_ge(sem("h_mixed1"), OUT_CH)
            for i in range(4):
                pool.memset(ytok[:, i // 2, (i % 2) * 512:(i % 2 + 1) * 512], 0.0).then_inc(sem("yacc"), 1)


_INS = ["x", "c", "ctx", "c_ctx", "w_ada", "b_ada", "norm1_g", "norm2_g", "w_in", "conv_w", "q_norm_g", "k_norm_g",
        "attn_sink", "out_norm_conv_g", "out_norm_attn_g", "w_out", "ffn_w1", "ffn_w3", "ffn_w2",
        "moe_router", "moe_w1", "moe_w3", "moe_w2"]
_OUTS = [((1, SEQ, D), "float32")]


def kernel(**inputs):
    import numpy as _np
    import concourse.bacc as _bacc
    from concourse import mybir as _mybir
    from concourse.bass_utils import run_bass_kernel_spmd as _run

    nc = _bacc.Bacc("TRN2", target_bir_lowering=False, num_devices=1)
    arrays, args = {}, []
    for name in _INS:
        a = _np.ascontiguousarray(inputs[name])
        arrays[f"in_{name}_dram"] = a
        args.append(nc.dram_tensor(f"in_{name}_dram", a.shape, _mybir.dt.from_np(a.dtype), kind="ExternalInput").ap())
    table = constant_table(_np)
    arrays["table_dram"] = table
    args.append(nc.dram_tensor("table_dram", table.shape, _mybir.dt.from_np(table.dtype), kind="ExternalInput").ap())
    for i, (shape, dtype) in enumerate(_OUTS):
        dt = _mybir.dt.from_np(_np.dtype(dtype))
        args.append(nc.dram_tensor(f"out_{i}_dram", shape, dt, kind="ExternalOutput").ap())
    hybrid_backbone(nc, *args)
    r = _run(nc, [arrays], core_ids=[0])
    got = tuple(r.results[0][f"out_{i}_dram"] for i in range(len(_OUTS)))
    return got[0]
```
